# Optimizing a Trainium2 kernel written in Bass

```python
import math
import jax, jax.numpy as jnp
from jax import lax
import numpy as np

D_MODEL = 1024
BATCH = 1
SEQ = 512
DEPTH = 1
DEC_BATCH = 8
DEC_SEQ = 4
PAST_LEN = 256
PAGE_SIZE = 128

N_HEADS = 8
HEAD_DIM = 64
D_ATTN = N_HEADS * HEAD_DIM
D_RNN = 512
N_RG_BLOCKS = 8
RG_BLOCK = D_RNN // N_RG_BLOCKS
CONV_W = 4
RG_C = 8.0
MOBA_BLOCK = 256
MOBA_TOP_K = 3
NUM_BUCKETS = 32
MAX_DISTANCE = 128
D_FF = -(-8 * D_MODEL // (3 * 256)) * 256
D_IN = 3 * D_ATTN + 2 * D_RNN + 2 * D_MODEL
Q_CHUNK = 64
RMS_EPS = 1e-6
NEG_INF = -1e30

kernel_name = "hybrid_moba_rglru_decode_step"

def rmsnorm(x, g):
    x32 = x.astype(jnp.float32)
    y = x32 * lax.rsqrt(jnp.mean(x32 * x32, axis=-1, keepdims=True) + RMS_EPS)
    return (y * g.astype(jnp.float32)).astype(x.dtype)

def t5_bucket(rel):
    n = jnp.maximum(-rel, 0)
    max_exact = NUM_BUCKETS // 2
    nf = jnp.maximum(n, 1).astype(jnp.float32)
    large = max_exact + (jnp.log(nf / max_exact) / math.log(MAX_DISTANCE / max_exact)
                         * (NUM_BUCKETS - max_exact)).astype(jnp.int32)
    large = jnp.minimum(large, NUM_BUCKETS - 1)
    return jnp.where(n < max_exact, n, large)

def moba_attend(q, q_pos, kb, vb, means, rel_bias):
    B, H, Q, dh = q.shape
    NB = kb.shape[2]
    k_sel = max(1, min(MOBA_TOP_K, NB - 1))
    own = q_pos // MOBA_BLOCK
    blk_scores = jnp.einsum('bhqd,bhnd->bhqn', q.astype(jnp.float32), means)
    past = jnp.arange(NB)[None, :] < own[:, None]
    blk_scores = jnp.where(past, blk_scores, NEG_INF)
    _, sel = lax.top_k(blk_scores, k_sel)
    sel_valid = sel < own[:, None]
    own_b = jnp.broadcast_to(own[:, None], (B, H, Q, 1)).astype(sel.dtype)
    idx = jnp.concatenate([sel, own_b], axis=-1)
    blk_valid = jnp.concatenate([sel_valid, jnp.ones((B, H, Q, 1), bool)], axis=-1)
    J = k_sel + 1
    gather = jax.vmap(jax.vmap(lambda t, i: t[i]))
    kg = gather(kb, idx)
    vg = gather(vb, idx)
    k_pos = idx[..., None] * MOBA_BLOCK + jnp.arange(MOBA_BLOCK)
    rel = k_pos - q_pos[:, None, None]
    is_own = jnp.arange(J) == J - 1
    mask = jnp.where(is_own[:, None], rel <= 0, blk_valid[..., None])
    bias = rel_bias.T[jnp.arange(H)[:, None, None, None], t5_bucket(rel)].astype(jnp.float32)
    logits = jnp.einsum('bhqd,bhqjkd->bhqjk', q, kg).astype(jnp.float32) * (HEAD_DIM ** -0.5) + bias
    logits = jnp.where(mask, logits, NEG_INF)
    p = jax.nn.softmax(logits.reshape(B, H, Q, J * MOBA_BLOCK), axis=-1)
    p = p.reshape(B, H, Q, J, MOBA_BLOCK).astype(vg.dtype)
    return jnp.einsum('bhqjk,bhqjkd->bhqd', p, vg)

def moba_chunked(q, q_pos, kb, vb, means, rel_bias, chunk):
    B, H, Q, dh = q.shape
    n = Q // chunk
    qc = q.reshape(B, H, n, chunk, dh).transpose(2, 0, 1, 3, 4)
    pc = q_pos.reshape(n, chunk)
    out = lax.map(lambda a: moba_attend(a[0], a[1], kb, vb, means, rel_bias), (qc, pc))
    return out.transpose(1, 2, 0, 3, 4).reshape(B, H, Q, dh)

def rglru(xc, h0, w_r, b_r, w_i, b_i, lam):
    B, T, _ = xc.shape
    x32 = xc.astype(jnp.float32)
    xb = x32.reshape(B, T, N_RG_BLOCKS, RG_BLOCK)
    r = jax.nn.sigmoid(jnp.einsum('btnc,ncd->btnd', xb, w_r.astype(jnp.float32)).reshape(B, T, D_RNN)
                       + b_r.astype(jnp.float32))
    i = jax.nn.sigmoid(jnp.einsum('btnc,ncd->btnd', xb, w_i.astype(jnp.float32)).reshape(B, T, D_RNN)
                       + b_i.astype(jnp.float32))
    log_a = -RG_C * r * jax.nn.softplus(-lam.astype(jnp.float32))
    a = jnp.exp(log_a)
    b = jnp.sqrt(-jnp.expm1(2.0 * log_a)) * (i * x32)

    def combine(c1, c2):
        a1, b1 = c1
        a2, b2 = c2
        return a1 * a2, a2 * b1 + b2

    a_c, b_c = lax.associative_scan(combine, (a, b), axis=1)
    h = a_c * h0.astype(jnp.float32)[:, None, :] + b_c
    return h, h[:, -1]

def layer(x, q_pos, k_past, v_past, conv_past, h_past, chunk, w):
    (g_mix_pre, g_mix_post, w_in, rel_bias, conv_w, conv_b, w_r, b_r, w_i, b_i, lam,
     w_pa, w_pr, w_out, g_ffn_pre, g_ffn_post, w_gate_up, w_down) = w
    B, T, _ = x.shape
    h = rmsnorm(x, g_mix_pre)
    proj = h @ w_in
    q, k, v, xr, gb, gates = jnp.split(
        proj, [D_ATTN, 2 * D_ATTN, 3 * D_ATTN, 3 * D_ATTN + D_RNN, 3 * D_ATTN + 2 * D_RNN], axis=-1)
    q = q.reshape(B, T, N_HEADS, HEAD_DIM)
    k = k.reshape(B, T, N_HEADS, HEAD_DIM)
    v = v.reshape(B, T, N_HEADS, HEAD_DIM)
    k_all = jnp.concatenate([k_past.astype(k.dtype), k], axis=1)
    v_all = jnp.concatenate([v_past.astype(v.dtype), v], axis=1)
    T_all = k_all.shape[1]
    NB = -(-T_all // MOBA_BLOCK)
    pad = ((0, 0), (0, NB * MOBA_BLOCK - T_all), (0, 0), (0, 0))
    kb = jnp.pad(k_all, pad).reshape(B, NB, MOBA_BLOCK, N_HEADS, HEAD_DIM).transpose(0, 3, 1, 2, 4)
    vb = jnp.pad(v_all, pad).reshape(B, NB, MOBA_BLOCK, N_HEADS, HEAD_DIM).transpose(0, 3, 1, 2, 4)
    means = jnp.mean(kb.astype(jnp.float32), axis=3)
    o_attn = moba_chunked(q.transpose(0, 2, 1, 3), q_pos, kb, vb, means, rel_bias, chunk)
    o_attn = o_attn.transpose(0, 2, 1, 3).reshape(B, T, D_ATTN)
    xpad = jnp.concatenate([conv_past.astype(xr.dtype), xr], axis=1)
    xc = sum(xpad[:, j:j + T] * conv_w[j] for j in range(CONV_W)) + conv_b
    new_conv = xpad[:, -(CONV_W - 1):]
    hseq, h_last = rglru(xc, h_past, w_r, b_r, w_i, b_i, lam)
    o_rnn = hseq.astype(x.dtype) * jax.nn.gelu(gb)
    gate_a, gate_r = jnp.split(gates, 2, axis=-1)
    merged = jax.nn.sigmoid(gate_a) * (o_attn @ w_pa) + jax.nn.sigmoid(gate_r) * (o_rnn @ w_pr)
    x = x + rmsnorm(merged @ w_out, g_mix_post)
    f = rmsnorm(x, g_ffn_pre)
    g_, u_ = jnp.split(f @ w_gate_up, 2, axis=-1)
    x = x + rmsnorm((jax.nn.silu(g_) * u_) @ w_down, g_ffn_post)
    return x, k, v, new_conv, h_last.astype(h_past.dtype)

def setup_inputs(seed: int = 0) -> dict:
    key = jax.random.key(seed)
    ks = jax.random.split(key, 32)
    nrm = lambda k, shape, s: jax.random.normal(k, shape, jnp.float32) * s
    n_pages = PAST_LEN // PAGE_SIZE
    used = DEC_BATCH * n_pages
    n_phys = used + max(1, used // 4)
    page_table = jax.random.permutation(ks[4], n_phys)[:used].reshape(DEC_BATCH, n_pages).astype(jnp.int32)
    a0 = jax.random.uniform(ks[17], (DEPTH, D_RNN), jnp.float32, 0.9, 0.999)
    s = a0 ** (1.0 / RG_C)
    rg_lambda = jnp.log(s) - jnp.log1p(-s)
    return {
        "x_prompt": nrm(ks[0], (BATCH, SEQ, D_MODEL), 1.0),
        "x_sample": nrm(ks[1], (DEC_BATCH, DEC_SEQ, D_MODEL), 1.0),
        "cache_k": nrm(ks[2], (DEPTH, n_phys, PAGE_SIZE, N_HEADS, HEAD_DIM), 1.0),
        "cache_v": nrm(ks[3], (DEPTH, n_phys, PAGE_SIZE, N_HEADS, HEAD_DIM), 1.0),
        "page_table": page_table,
        "state_conv": nrm(ks[5], (DEPTH, DEC_BATCH, CONV_W - 1, D_RNN), 1.0),
        "state_h": nrm(ks[6], (DEPTH, DEC_BATCH, D_RNN), 0.5),
        "norm_mix_pre": 1.0 + nrm(ks[7], (DEPTH, D_MODEL), 0.01),
        "norm_mix_post": 1.0 + nrm(ks[8], (DEPTH, D_MODEL), 0.01),
        "w_in": nrm(ks[9], (DEPTH, D_MODEL, D_IN), D_MODEL ** -0.5),
        "rel_bias": nrm(ks[10], (NUM_BUCKETS, N_HEADS), 0.5),
        "conv_w": nrm(ks[11], (DEPTH, CONV_W, D_RNN), 0.5),
        "conv_b": nrm(ks[12], (DEPTH, D_RNN), 0.01),
        "rg_w_r": nrm(ks[13], (DEPTH, N_RG_BLOCKS, RG_BLOCK, RG_BLOCK), RG_BLOCK ** -0.5),
        "rg_b_r": nrm(ks[14], (DEPTH, D_RNN), 0.01),
        "rg_w_i": nrm(ks[15], (DEPTH, N_RG_BLOCKS, RG_BLOCK, RG_BLOCK), RG_BLOCK ** -0.5),
        "rg_b_i": nrm(ks[16], (DEPTH, D_RNN), 0.01),
        "rg_lambda": rg_lambda,
        "w_proj_attn": nrm(ks[18], (DEPTH, D_ATTN, D_MODEL), D_ATTN ** -0.5),
        "w_proj_rnn": nrm(ks[19], (DEPTH, D_RNN, D_MODEL), D_RNN ** -0.5),
        "w_out": nrm(ks[20], (DEPTH, D_MODEL, D_MODEL), D_MODEL ** -0.5),
        "norm_ffn_pre": 1.0 + nrm(ks[21], (DEPTH, D_MODEL), 0.01),
        "norm_ffn_post": 1.0 + nrm(ks[22], (DEPTH, D_MODEL), 0.01),
        "w_gate_up": nrm(ks[23], (DEPTH, D_MODEL, 2 * D_FF), D_MODEL ** -0.5),
        "w_down": nrm(ks[24], (DEPTH, D_FF, D_MODEL), D_FF ** -0.5),
    }

def reference(x_prompt, x_sample, cache_k, cache_v, page_table, state_conv, state_h,
              norm_mix_pre, norm_mix_post, w_in, rel_bias, conv_w, conv_b,
              rg_w_r, rg_b_r, rg_w_i, rg_b_i, rg_lambda, w_proj_attn, w_proj_rnn, w_out,
              norm_ffn_pre, norm_ffn_post, w_gate_up, w_down):
    Bp, Tp, _ = x_prompt.shape
    Bs, Ts, _ = x_sample.shape
    past_len = page_table.shape[1] * cache_k.shape[2]
    pos_prompt = jnp.arange(Tp, dtype=jnp.int32)
    pos_sample = past_len + jnp.arange(Ts, dtype=jnp.int32)
    chunk_prompt = math.gcd(Tp, Q_CHUNK)
    xp, xs = x_prompt, x_sample
    nkp, nvp, nks, nvs, ncp, nhp, ncs, nhs = [], [], [], [], [], [], [], []
    for l in range(DEPTH):
        wl = (norm_mix_pre[l], norm_mix_post[l], w_in[l], rel_bias, conv_w[l], conv_b[l],
              rg_w_r[l], rg_b_r[l], rg_w_i[l], rg_b_i[l], rg_lambda[l], w_proj_attn[l],
              w_proj_rnn[l], w_out[l], norm_ffn_pre[l], norm_ffn_post[l], w_gate_up[l], w_down[l])
        xp, kp, vp, cp, hp = layer(
            xp, pos_prompt,
            jnp.zeros((Bp, 0, N_HEADS, HEAD_DIM), xp.dtype), jnp.zeros((Bp, 0, N_HEADS, HEAD_DIM), xp.dtype),
            jnp.zeros((Bp, CONV_W - 1, D_RNN), xp.dtype), jnp.zeros((Bp, D_RNN), state_h.dtype),
            chunk_prompt, wl)
        k_past = cache_k[l][page_table].reshape(Bs, past_len, N_HEADS, HEAD_DIM)
        v_past = cache_v[l][page_table].reshape(Bs, past_len, N_HEADS, HEAD_DIM)
        xs, ks_, vs_, cs, hs = layer(xs, pos_sample, k_past, v_past, state_conv[l], state_h[l], 1, wl)
        nkp.append(kp); nvp.append(vp); nks.append(ks_); nvs.append(vs_)
        ncp.append(cp); nhp.append(hp); ncs.append(cs); nhs.append(hs)
    return (xp, xs, jnp.stack(nkp), jnp.stack(nvp), jnp.stack(nks), jnp.stack(nvs),
            jnp.stack(ncp), jnp.stack(nhp), jnp.stack(ncs), jnp.stack(nhs))


_drawn_inputs = setup_inputs


def setup_inputs(seed=0):
    import zlib

    import numpy as np

    out = dict(_drawn_inputs(seed))
    spreads = {}
    factors = {'norm_mix_pre': 4.652,
     'norm_mix_post': 34.615,
     'rg_b_r': 43.017,
     'rg_b_i': 28.473,
     'norm_ffn_pre': 34.159,
     'norm_ffn_post': 61.061,
     'conv_b': 4.633}
    for name, (base, spread) in spreads.items():
        noise = np.random.default_rng([zlib.crc32(name.encode()), seed]).standard_normal(out[name].shape)
        drawn = base * np.exp(spread * noise) if base else spread * noise
        out[name] = __import__('jax').numpy.asarray(drawn.astype(out[name].dtype))
    for name, factor in factors.items():
        out[name] = (out[name] * factor).astype(out[name].dtype)
    return out
```

```python
import math
from contextlib import ExitStack

import numpy as np

import concourse.bass as bass
from concourse import mybir

F32 = mybir.dt.float32
F32R = mybir.dt.float32r
I32 = mybir.dt.int32
ALU = mybir.AluOpType
ACT = mybir.ActivationFunctionType
AP = bass.AP

P = 128
D = 1024
KD = D // P
SEQ = 512
DEC_B, DEC_T = 8, 4
TS = DEC_B * DEC_T
T = SEQ + TS
HT = T // 2
HEADS, DH = 8, 64
DA = HEADS * DH
PAIRS = DA // P
DR = 512
RGB = 64
CW = 4
PAST = 256
PAGE = 128
NPG = PAST // PAGE
DFF = -(-8 * D // (3 * 256)) * 256
KF = DFF // P
TT = SEQ // P
NB, MAXD = 32, 128
EPS = 1e-6
NEG = -1.0e30
BIG = 3.0e38
EXT = SEQ + DEC_B * (DEC_T + 1)
EH = EXT // 2
RELW = 640
KS = PAST + TS
ROWS_S = DEC_B * 2 * DEC_T

TILES_IT = 8
GT_IT = 3
C_TAIL = PAIRS * TILES_IT
GT_TAIL = 2 * KD - PAIRS * GT_IT
C_MIX = C_TAIL + GT_TAIL
C_OUT = C_MIX + KD
C_FFN = C_OUT + KD
C_DOWN = C_FFN + 2 * KF
DOWN_K = [8, 8, KF - 16]

SERIES = 9
GELU_C1 = math.sqrt(2.0 / math.pi)
GELU_C2 = GELU_C1 * 0.044715


def bucket_table():
    n = np.arange(RELW) - 127
    pos = np.maximum(n, 1).astype(np.float32)
    half = NB // 2
    large = half + (np.log(pos / half) / math.log(MAXD / half) * (NB - half)).astype(np.int32)
    bucket = np.where(n < half, np.maximum(n, 0), np.minimum(large, NB - 1))
    table = np.zeros((NB + 1, RELW), np.float32)
    table[np.where(n < 0, NB, bucket), np.arange(RELW)] = 1.0
    return table


def program(nc, x_prompt, x_sample, cache_k, cache_v, page_table, state_conv, state_h,
            norm_mix_pre, norm_mix_post, w_in, rel_bias, conv_w, conv_b, rg_w_r, rg_b_r,
            rg_w_i, rg_b_i, rg_lambda, w_proj_attn, w_proj_rnn, w_out, norm_ffn_pre,
            norm_ffn_post, w_gate_up, w_down, bucket_of,
            y_prompt, y_sample, new_k_prompt, new_v_prompt, new_k_sample, new_v_sample,
            new_conv_prompt, new_h_prompt, new_conv_sample, new_h_sample):
    n_phys = cache_k.shape[1]
    dist_bias = nc.dram_tensor("dist_bias", (HEADS, RELW), F32, kind="Internal").ap()

    at = [-(-nc.sbuf_base // 64) * 64]

    def put(name, shape, dt=F32, where=None):
        size = 4 * int(np.prod(shape[1:]))
        size = -(-size // 32) * 32
        if where is None:
            offset, at[0] = at[0], at[0] + size
        else:
            offset, where[0] = where[0], where[0] + size
        assert offset + size <= nc.sbuf_usable_end, (name, offset + size)
        return nc.alloc_sbuf_tensor_at(name, shape, dt, offset=offset)

    ring = [[put(f"w_{part}{s}", [P, KD, P], dt) for s in range(2)]
            for part, dt in (("raw", F32), ("hi", F32R), ("lo", F32R))]
    w_raw, w_hi, w_lo = ring
    xin_at = at[0]
    xin_hi = put("xin_hi", [P, KD, T], F32R)
    xin_lo = put("xin_lo", [P, KD, T], F32R)
    ident = put("ident", [P, P])
    ones = put("ones", [P, P])
    prm = put("prm", [P, 56])
    eps_col = put("eps_col", [P, 1])
    tiny_col = put("tiny_col", [P, 1])
    big_at = at[0]

    ocat_hi = put("ocat_hi", [P, 2 * PAIRS, T], F32R)
    ocat_lo = put("ocat_lo", [P, 2 * PAIRS, T], F32R)
    gates = put("gates", [P, 2 * KD, T])
    stage_at = at[0]
    qT, kT, vT = (put(n, [P, T]) for n in ("qT", "kT", "vT"))
    tok = put("tok", [P, 2, TT + 1, P])
    q_bd = put("q_bd", [P, 72 * DEC_B])
    q_all = put("q_all", [P, ROWS_S])
    kcT = put("kcT", [P, DEC_B, PAST])
    kc = put("kc", [P, DEC_B * NPG, P])
    vc = put("vc", [P, DEC_B * NPG, P])
    biasT = put("biasT", [P, 2, SEQ])
    lgt_at = at[0]
    lgt = put("lgt", [P, 2, SEQ])
    prT = put("prT", [P, 2, SEQ])
    lgt_s = put("lgt_s", [P, KS])
    prT_s = put("prT_s", [P, 3, ROWS_S])
    mask_s = put("mask_s", [P, KS])
    bias8 = put("bias8", [P, PAIRS, KS])
    rep8 = put("rep8", [P, P])
    nmax = put("nmax", [P, 9])
    den = put("den", [P, 9])
    rden = put("rden", [P, 9])
    stT = put("stT", [P, PAIRS, 32])
    stcol = put("stcol", [P, PAIRS, 36])
    prm_it = put("prm_it", [P, 8])
    bd = put("bd", [P, 2, P])
    xp = put("xp", [P, SEQ + CW - 1])
    xps = put("xps", [P, DEC_B, DEC_T + CW - 1])
    xc = put("xc", [P, EXT])
    th = put("th", [P, EXT])
    ti = put("ti", [P, EXT])
    dd = put("dd", [P, EXT])
    aa = put("aa", [P, EXT])
    sq = put("sq", [P, EXT])
    gb = put("gb", [P, T])
    gp = put("gp", [P, T])
    st_out = put("st_out", [36, DR], where=[lgt_at])
    w = [big_at]
    x_tok = put("x_tok", [P, TT + 1, D], where=w)
    x_sq = put("x_sq", [P, D], where=w)
    g_row = put("g_row", [P, D], where=w)
    ssum = put("ssum", [P, 8], where=w)
    rstd_x = put("rstd_x", [P, 8], where=w)
    prow = put("prow", [56, P], where=w)
    strow = put("strow", [32, DR], where=w)
    rel33 = put("rel33", [NB + 1, HEADS], where=w)
    bktab = put("bktab", [NB + 1, RELW], where=w)
    drow = put("drow", [HEADS, RELW], where=w)
    pages = put("pages", [1, DEC_B * NPG], I32, where=w)
    sp = [put(f"sp{i}", [P, 4], where=w) for i in range(6)]
    bias8_rev = put("bias8_rev", [8, PAIRS, KS], where=w)
    assert w[0] <= stage_at
    w = [stage_at]
    ma = [put(f"ma{i}", [P, T], where=w) for i in range(2)]
    mr = [put(f"mr{i}", [P, T], where=w) for i in range(2)]
    xk = [put(f"xk{i}", [P, TT + 1, P], where=w) for i in range(2)]
    hid_end = big_at + 2 * 4 * KF * T
    assert w[0] <= hid_end
    w = [hid_end]
    x1 = put("x1", [P, KD, T], where=w)
    ytok = put("ytok", [P, TT + 1, D], where=w)
    rb = [put(f"rb{i}", [P, T], where=w) for i in range(2)]
    std = put("std", [P, T], where=w)
    fg, fu, ft = (put(n, [P, T], where=w) for n in ("fg", "fu", "ft"))
    w = [big_at]
    og = put("og", [P, KD, T], where=w)
    osq = [put(f"osq{i}", [P, T], where=w) for i in range(2)]
    oacc = [put(f"oacc{i}", [P, T], where=w) for i in range(2)]
    assert w[0] <= stage_at
    w = [big_at]
    hid_hi = put("hid_hi", [P, KF, T], F32R, where=w)
    hid_lo = put("hid_lo", [P, KF, T], F32R, where=w)
    w = [xin_at]
    x1tok = put("x1tok", [P, TT + 1, D], where=w)
    yg = [put(f"yg{i}", [P, T], where=w) for i in range(2)]
    x1s = [put(f"x1s{i}", [P, T], where=w) for i in range(2)]
    ysq = put("ysq", [P, T], where=w)
    yacc = put("yacc", [P, T], where=w)
    ycol = put("ycol", [P, 16], where=w)
    assert w[0] <= xin_at + 2 * 4 * KD * T

    with ExitStack() as ctx:
        def sem(name):
            return ctx.enter_context(nc.semaphore(name))

        ps = ctx.enter_context(nc.psum_tensor("ps", [P, 8, 512], F32))
        S_BANK, T_BANK, O_BANK, M_BANK = 4, 5, 6, 7

        w_in_slot = [sem("w_slot0"), sem("w_slot1")]
        hi_done = sem("hi_done")
        lo_done = sem("lo_done")
        tile_done = sem("tile_done")
        tile_free = [sem("tile_free0"), sem("tile_free1")]
        x_in = [sem(f"x_in{i}") for i in range(TT + 1)]
        par_in = sem("par_in")
        rel_in = sem("rel_in")
        g_in = sem("g_in")
        page_in = sem("page_in")
        bias8_in = sem("bias8_in")
        dist_out = sem("dist_out")
        consts = sem("consts")
        consts_v = sem("consts_v")
        sq_sum = sem("sq_sum")
        std_x = sem("std_x")
        rx_done = sem("rx_done")
        xs_done = sem("xs_done")
        xt_ready = sem("xt_ready")
        xt_hi = sem("xt_hi")
        xt_lo = sem("xt_lo")
        small_T = sem("small_T")
        small_c = sem("small_c")
        sp_act = sem("sp_act")
        sp_dve = sem("sp_dve")
        kc_in = sem("kc_in")
        vc_in = sem("vc_in")
        bias_in = sem("bias_in")
        bd_in = sem("bd_in")
        kv_out = sem("kv_out")
        it_ready = sem("it_ready")
        q_spread = sem("q_spread")
        s_ready = sem("s_ready")
        logits_done = sem("logits_done")
        exp_done = sem("exp_done")
        rden_done = sem("rden_done")
        probs_done = sem("probs_done")
        tp_ready = sem("tp_ready")
        tp_free = sem("tp_free")
        mi_ready = sem("mi_ready")
        mi_free = sem("mi_free")
        so_hi = sem("so_hi")
        pv_done = sem("pv_done")
        o_hi = sem("o_hi")
        o_free = sem("o_free")
        conv_step = sem("conv_step")
        th_done = sem("th_done")
        sq_done = sem("sq_done")
        gelu_step = sem("gelu_step")
        tg_done = sem("tg_done")
        rg_step = sem("rg_step")
        orn_hi = sem("orn_hi")
        rg_done = sem("rg_done")
        st_saved = sem("st_saved")
        st_ready = sem("st_ready")
        st_copied = sem("st_copied")
        st_out_s = sem("st_out_s")
        xk_in = [sem("xk_in0"), sem("xk_in1")]
        mix_free = sem("mix_free")
        mix_sum = sem("mix_sum")
        mix_hi = sem("mix_hi")
        mix_lo = sem("mix_lo")
        out_free = sem("out_free")
        osq_used = sem("osq_used")
        xT_ready = sem("xT_ready")
        xT_free = sem("xT_free")
        n_ready = sem("n_ready")
        n_std = sem("n_std")
        n_rstd = sem("n_rstd")
        t_done = sem("t_done")
        x1_done = sem("x1_done")
        f_hi = sem("f_hi")
        f_sq = sem("f_sq")
        f_lo = sem("f_lo")
        f_acc = sem("f_acc")
        gu_scaled = sem("gu_scaled")
        gu_free = sem("gu_free")
        fsil = sem("fsil")
        fprod = sem("fprod")
        hid_h = sem("hid_h")
        hid_l = sem("hid_l")
        y_free = sem("y_free")
        ysq_used = sem("ysq_used")
        acc_zero = sem("acc_zero")
        x1s_done = sem("x1s_done")
        x1t_ready = sem("x1t_ready")
        x1t_free = sem("x1t_free")
        yt_ready = sem("yt_ready")
        yt_free = sem("yt_free")
        ycol_step = sem("ycol_step")
        yn_ready = sem("yn_ready")
        z_done = sem("z_done")
        y_out = sem("y_out")

        def two(pair):
            return ps[:, 2 * pair:2 * pair + 2, 0:HT]

        def halves(buf):
            return buf.rearrange("p (h t) -> p h t", h=2)

        def bt(ap):
            return ap.rearrange("p (b t) -> p b t", b=DEC_B)

        def x_fill(dst, tt, hf, f):
            if tt < TT:
                return (dst[:, 4 * hf:4 * hf + 4, tt * P:(tt + 1) * P],
                        ps[:, 4 + f % 4, :].rearrange("p (k c) -> p k c", c=P))
            return dst[:, :, SEQ:T], ps[:, 4 + f % 4, 0:KD * TS].rearrange("p (k c) -> p k c", c=TS)

        def tile_of(buf, k, k0=0):
            flat = buf[:, :, :].rearrange("p k t -> p (k t)")
            return halves(flat[:, bass.ds(k * T + k0 * T, T)])

        SP_ABS = 3
        block = ctx.enter_context(nc.Block())

        @block.sync
        def _(sp_):
            e = sp_
            wi = w_in[0].rearrange("(kt p) n -> p kt n", p=P)
            wpa = w_proj_attn[0].rearrange("(kt p) n -> p kt n", p=P)
            wpr = w_proj_rnn[0].rearrange("(kt p) n -> p kt n", p=P)
            wo = w_out[0].rearrange("(kt p) n -> p kt n", p=P)
            wgu = w_gate_up[0].rearrange("(kt p) n -> p kt n", p=P)
            wd = w_down[0].rearrange("(kt p) n -> p kt n", p=P)

            def load(i, s, src, k=KD):
                e.wait_ge(lo_done, i + 1)
                for k0, k1 in ((0, 4), (4, k)):
                    e.dma_start(w_raw[s][:, k0:k1, :], src[:, k0:k1, :]).then_inc(w_in_slot[s], 16)

            for tt in range(TT):
                e.dma_start(x_tok[:, tt, :], x_prompt[0, tt * P:(tt + 1) * P, :]).then_inc(x_in[tt], 16)
            e.dma_start(x_tok[0:TS, TT, :], x_sample.rearrange("b t d -> (b t) d")).then_inc(x_in[TT], 16)
            e.dma_start(pages[:, :], page_table.rearrange("b n -> (b n)").rearrange("(a n) -> a n", a=1)
                        ).then_inc(page_in, 16)
            e.wait_ge(page_in, 16)
            page = [e.value_load(pages[0:1, j:j + 1], min_val=0, max_val=n_phys - 1)
                    for j in range(DEC_B * NPG)]

            def load_pages(cache, dst, done, it, part):
                for j in range(8 * part, 8 * part + 8):
                    src = cache[0].rearrange("n t h d -> n t (h d)")[bass.ds(page[j], 1), :, bass.ds(it * P, P)]
                    e.dma_start(dst[:, j, :], src.rearrange("o t c -> t (o c)")).then_inc(done, 16)

            def iteration(it, last):
                for j in range(TILES_IT):
                    if j < 5:
                        col = it * P + 512 * j
                    else:
                        col = it * (GT_IT * P) + 2560 + (j - 5) * P
                    load(it * TILES_IT + j, j % 2, wi[:, :, bass.ds(col, P)])
                    if j == 1:
                        e.wait_ge(consts, 12)
                        e.wait_ge(logits_done, it * 9 + 1)
                        src = AP(dist_bias.tensor, it * (2 * RELW), [[1, P], [RELW, 2], [1, SEQ]])
                        e.wait_ge(dist_out, 16)
                        e.dma_start(biasT[:, :, :], src).then_inc(bias_in, 16)
                        e.wait_ge(mi_free, it * 8 + 1)
                        for g, wrg in enumerate((rg_w_r, rg_w_i)):
                            for blk in range(2):
                                rows = slice(RGB * blk, RGB * blk + RGB)
                                e.dma_start(bd[rows, g, rows],
                                            wrg[0][bass.ds(it * 2 + blk, 1)].rearrange("o c d -> c (o d)")
                                            ).then_inc(bd_in, 16)
                    if j in (5, 6) and not last:
                        e.wait_ge(s_ready, it * 9 + 1)
                        load_pages(cache_k, kc, kc_in, it + 1, j - 5)
                e.wait_ge(mi_free, it * 8 + 4)
                for g, (op, os) in enumerate(((new_k_prompt, new_k_sample), (new_v_prompt, new_v_sample))):
                    dst = op[0, 0].rearrange("(tt p) h d -> p tt (h d)", p=P)[:, :, bass.ds(it * P, P)]
                    e.dma_start(dst, tok[:, g, 0:TT, :]).then_inc(kv_out, 16)
                    dst = os[0].rearrange("b t h d -> (b t) (h d)")[:, bass.ds(it * P, P)]
                    e.dma_start(dst, tok[0:TS, g, TT, :]).then_inc(kv_out, 16)
                if not last:
                    e.wait_ge(mi_ready, it * 8 + 4)
                    load_pages(cache_v, vc, vc_in, it + 1, 0)
                    load_pages(cache_v, vc, vc_in, it + 1, 1)

            for part in range(2):
                load_pages(cache_k, kc, kc_in, 0, part)
            for part in range(2):
                load_pages(cache_v, vc, vc_in, 0, part)
            with e.Fori(0, PAIRS - 1) as it:
                iteration(it, False)
            iteration(PAIRS - 1, True)
            with e.Fori(0, GT_TAIL // 2) as n:
                for s in range(2):
                    load(n * 2 + (C_TAIL + s), s, wi[:, :, bass.ds(n * (2 * P) + 2560 + (PAIRS * GT_IT + s) * P, P)])
            with e.Fori(0, KD // 2) as n:
                for s in range(2):
                    e.wait_ge(lo_done, n * 2 + (C_MIX + s + 1))
                    for k0, wp in ((0, wpa), (PAIRS, wpr)):
                        e.dma_start(w_raw[s][:, k0:k0 + PAIRS, :], wp[:, :, bass.ds(n * (2 * P) + s * P, P)]
                                    ).then_inc(w_in_slot[s], 16)
            e.wait_ge(st_copied, 1)
            e.wait_ge(rg_done, PAIRS + 1)
            e.wait_ge(o_free, PAIRS + 1)
            e.wait_ge(kv_out, 64 * (PAIRS + 1))
            e.dma_start(new_conv_prompt[0, 0], st_out[0:3, :]).then_inc(st_out_s, 16)
            e.dma_start(new_conv_sample[0].rearrange("b j d -> (b j) d"), st_out[3:27, :]).then_inc(st_out_s, 16)
            e.dma_start(new_h_prompt[0], st_out[27:28, :]).then_inc(st_out_s, 16)
            e.dma_start(new_h_sample[0], st_out[28:36, :]).then_inc(st_out_s, 16)
            xpt = x_prompt[0].rearrange("(tt p) d -> p tt d", p=P)
            xst = x_sample.rearrange("b t d -> (b t) d")
            with e.Fori(0, KD // 2) as n:
                for s in range(2):
                    load(n * 2 + (C_OUT + s), s, wo[:, :, bass.ds(n * (2 * P) + s * P, P)])
                    e.wait_ge(xT_free, n * 2 + (s + 1))
                    cols = bass.ds(n * (2 * P) + s * P, P)
                    e.dma_start(xk[s][:, 0:TT, :], xpt[:, :, cols]).then_inc(xk_in[s], 16)
                    e.dma_start(xk[s][0:TS, TT, :], xst[:, cols]).then_inc(xk_in[s], 16)
            with e.Fori(0, KF) as m:
                for s in range(2):
                    load(m * 2 + (C_FFN + s), s, wgu[:, :, bass.ds(m * P + s * DFF, P)])

            def load_down(m, c, s):
                k0 = sum(DOWN_K[:c])
                load(m * 3 + (C_DOWN + c), s, wd[:, k0:k0 + DOWN_K[c], bass.ds(m * P, P)], DOWN_K[c])

            with e.Fori(0, KD // 2) as n:
                for m2 in range(2):
                    for c in range(3):
                        load_down(n * 2 + m2, c, (m2 * 3 + c) % 2)
            for tt in range(TT + 1):
                e.wait_ge(z_done, tt + 1)
                if tt < TT:
                    e.dma_start(y_prompt[0, tt * P:(tt + 1) * P, :], ytok[:, tt, :]).then_inc(y_out, 16)
                else:
                    e.dma_start(y_sample.rearrange("b t d -> (b t) d"), ytok[0:TS, TT, :]).then_inc(y_out, 16)
            e.wait_ge(kv_out, 64 * (PAIRS + 1))
            e.wait_ge(st_out_s, 64)
            e.wait_ge(y_out, 16 * (TT + 1))

        @block.gpsimd
        def _(e):
            e.memset(ident[:, :], 0.0).then_inc(consts, 1)
            e.wait_ge(consts, 1)
            e.affine_select(out=ident[:, :], in_=ident[:, :], compare_op=ALU.not_equal, fill=1.0,
                            base=0, pattern=[[-1, P]], channel_multiplier=1).then_inc(consts, 1)
            e.memset(rep8[:, :], 0.0).then_inc(consts, 1)
            e.wait_ge(consts, 3)
            rep = rep8[:, :].rearrange("p (b k) -> p b k", k=8)
            e.affine_select(out=rep, in_=rep, compare_op=ALU.not_equal, fill=1.0,
                            base=0, pattern=[[0, P // 8], [-1, 8]], channel_multiplier=1).then_inc(consts, 1)
            e.memset(mask_s[:, :], 0.0).then_inc(consts, 1)
            e.wait_ge(consts, 5)
            own = mask_s[:, PAST:KS].rearrange("p (b t) -> p b t", b=DEC_B)
            e.affine_select(out=own, in_=own, compare_op=ALU.is_ge, fill=NEG,
                            base=0, pattern=[[-8, DEC_B], [0, DEC_T]], channel_multiplier=1).then_inc(consts, 1)
            e.wait_ge(consts, 6)
            e.affine_select(out=own, in_=own, compare_op=ALU.is_ge, fill=NEG,
                            base=7, pattern=[[8, DEC_B], [0, DEC_T]], channel_multiplier=-1).then_inc(consts, 1)
            e.memset(q_bd[:, :], 0.0).then_inc(consts, 1)
            e.memset(q_all[:, :], 0.0).then_inc(consts, 1)
            e.memset(bd[:, :, :], 0.0).then_inc(consts, 1)
            e.memset(xp[:, 0:CW - 1], 0.0).then_inc(consts, 1)
            e.memset(xc[:, :], 0.0).then_inc(consts, 1)
            e.wait_ge(bias8_in, 160)
            for b0 in range(PAIRS):
                e.tensor_copy(bias8[0:8, b0, :], bias8_rev[0:8, b0, ::-1]).then_inc(consts, 1)

            with e.Fori(0, PAIRS) as it:
                count = e.to_reg(it + 1)
                e.wait_ge(small_c, 6)
                e.wait_ge(rg_done, count)
                e.tensor_copy(prm_it[:, :], prm[:, 0:32].rearrange("p (c f) -> p c f", f=PAIRS)[:, :, bass.ds(it, 1)])
                e.tensor_copy(xps[:, :, 0:CW - 1],
                              stT[:, bass.ds(it, 1), 0:24].rearrange("p o (b j) -> p (o b) j", b=DEC_B)
                              ).then_inc(it_ready, 1)
                count = e.to_reg(it * 4 + 2)
                e.wait_ge(consts, 12)
                e.wait_ge(tile_free[0], count)
                e.wait_ge(it_ready, it + 1)
                for h in range(2):
                    rows = slice(DH * h, DH * h + DH)
                    src = bt(qT[rows, SEQ:T])
                    e.tensor_copy(q_all[rows, :].rearrange("p (b k) -> p b k", b=DEC_B)[:, :, 4 * h:4 * h + 4], src)
                    last = e.tensor_copy(q_bd[rows, :].rearrange("p (b k) -> p b k", b=DEC_B)[:, :, 4 * h:4 * h + 4],
                                         src)
                last.then_inc(q_spread, 1)
                count = e.to_reg(it * 4 + 3)
                e.wait_ge(consts, 12)
                e.wait_ge(tile_free[1], count)
                e.wait_ge(q_spread, it + 1)
                e.tensor_copy(stcol[:, bass.ds(it, 1), 0:3], xp[:, SEQ:SEQ + 3])
                e.tensor_copy(stcol[:, bass.ds(it, 1), 3:27].rearrange("p o (b j) -> p (o b) j", b=DEC_B),
                              xps[:, :, DEC_T:DEC_T + 3])
                e.wait_ge(tile_free[0], it * 4 + 4)
                e.tensor_tensor(gp[:, :], gb[:, :], gb[:, :], ALU.mult).then_inc(gelu_step, 1)
                count = e.to_reg(it * 3 + 1)
                e.wait_ge(consts, 12)
                e.wait_ge(gelu_step, count)
                e.tensor_scalar(gp[:, :], gp[:, :], GELU_C2, GELU_C1, ALU.mult, ALU.add).then_inc(gelu_step, 1)
                e.wait_ge(gelu_step, it * 3 + 2)
                e.tensor_tensor(gp[:, :], gp[:, :], gb[:, :], ALU.mult).then_inc(gelu_step, 1)
                count = e.to_reg(it * 12 + 9)
                e.wait_ge(small_c, 6)
                e.wait_ge(rg_step, count)
                e.tensor_copy(stcol[:, bass.ds(it, 1), 27:28], sq[:, SEQ - 1:SEQ])
                e.tensor_copy(stcol[:, bass.ds(it, 1), 28:36],
                              sq[:, SEQ:EXT].rearrange("p (b k) -> p b k", b=DEC_B)[:, :, DEC_T]
                              ).then_inc(st_saved, 1)
            e.wait_ge(n_ready, 1)
            for k in range(KD):
                e.wait_ge(f_sq, k + 1)
                if k >= 1:
                    e.wait_ge(f_acc, k)
                    e.tensor_tensor(oacc[1][:, :], oacc[1][:, :], osq[k % 2][:, :], ALU.add).then_inc(f_acc, 1)
                else:
                    e.tensor_copy(oacc[1][:, :], osq[0][:, :]).then_inc(f_acc, 1)
            with e.Fori(0, KD // 2) as n:
                for s in range(2):
                    count = e.to_reg(n * 2 + (s + 1))
                    e.wait_ge(tile_done, C_DOWN + 2)
                    e.wait_ge(x1t_free, count)
                    e.tensor_copy(x1s[s][:, :], x1[:, bass.ds(n * 2 + s, 1), :]).then_inc(x1s_done, 1)

        @block.tensor
        def _(e):
            def steps(s, bank, xh, xl, ks, first, last, ready=None):
                for kw, kx in ks:
                    if ready is not None:
                        e.wait_ge(ready, kx + 1)
                    for wt, xt in ((w_hi, xh), (w_hi, xl), (w_lo, xh)):
                        for h in range(2):
                            mm = e.matmul(ps[:, bank + h, 0:HT], wt[s][:, kw, :], xt[:, kx, h * HT:h * HT + HT],
                                          start=first and wt is w_hi and xt is xh,
                                          stop=last and (kw, kx) == ks[-1] and wt is w_lo)
                    first = False
                return mm

            def split_ready(i):
                e.wait_ge(lo_done, i + 3)

            e.wait_ge(consts, 2)
            e.wait_ge(par_in, 160)
            e.transpose(ps[:, 0, 0:56], prow[:, :], ident[0:56, 0:56]).then_inc(small_T, 1)
            for f in range(PAIRS):
                mm = e.transpose(ps[:, 1, 32 * f:32 * f + 32], strow[:, f * P:f * P + P], ident[0:32, 0:32])
            mm.then_inc(small_T, 1)
            e.wait_ge(rel_in, 32)
            e.matmul(ps[0:HEADS, 2, 0:512], rel33[:, :], bktab[:, 0:512], start=True, stop=True)
            e.matmul(ps[0:HEADS, 3, 0:RELW - 512], rel33[:, :], bktab[:, 512:RELW], start=True,
                     stop=True).then_inc(small_T, 1)
            for tt in range(TT + 1):
                e.wait_ge(xs_done, tt + 1)
                rows = P if tt < TT else TS
                for hf in range(2 if tt < TT else 1):
                    f = 2 * tt + hf
                    if f >= 4:
                        e.wait_ge(xt_lo, f - 3)
                    kts = range(4 * hf, 4 * hf + 4) if tt < TT else range(KD)
                    for n, kt in enumerate(kts):
                        mm = e.transpose(ps[:, 4 + f % 4, n * rows:(n + 1) * rows],
                                         x_tok[0:rows, tt, kt * P:kt * P + P], ident[0:rows, 0:rows])
                    mm.then_inc(xt_ready, 1)
            e.wait_ge(small_c, 4)
            e.wait_ge(xt_lo, 9)

            with e.Fori(0, PAIRS) as it:
                i0 = it * TILES_IT

                def begin(j):
                    split_ready(i0 + j)
                    e.wait_ge(tile_free[j % 2], it * 4 + (j // 2 + 1))

                def part(j, k0, k1):
                    mm = steps(j % 2, 2 * (j % 2), xin_hi, xin_lo, [(k, k) for k in range(k0, k1)], k0 == 0, k1 == KD)
                    if k1 == KD:
                        mm.then_inc(tile_done, 1)

                def tp_wait(use):
                    e.wait_ge(tp_free, it * 13 + (use + 1))

                def mi_wait(use):
                    e.wait_ge(mi_free, it * 8 + (use + 1))

                def cache_T(f):
                    if f == 0:
                        e.wait_ge(kc_in, it * 256 + 256)
                    tp_wait(f)
                    for n in range(4):
                        mm = e.transpose(ps[:, T_BANK, n * P:n * P + P], kc[:, 4 * f + n, :], ident[:, :])
                    mm.then_inc(tp_ready, 1)

                def scores_s():
                    e.wait_ge(q_spread, it + 1)
                    e.wait_ge(consts, 16)
                    e.wait_ge(tile_free[1], it * 4 + 2)
                    tp_wait(4)
                    e.wait_ge(logits_done, it * 9 + 1)
                    e.matmul(ps[:, S_BANK, 0:KS], rep8[0:8, :], bias8[0:8, :, :].rearrange("p f k -> p (f k)")[:, bass.ds(it * KS, KS)], start=True, stop=False,
                             skip_group_check=True)
                    for b in range(DEC_B):
                        e.matmul(ps[0:ROWS_S, S_BANK, 0:PAST], q_bd[:, ROWS_S * b:ROWS_S * b + ROWS_S], kcT[:, b, :],
                                 start=False, stop=False, skip_group_check=True)
                    e.matmul(ps[0:ROWS_S, S_BANK, PAST:KS], q_all[:, :], kT[:, SEQ:T], start=False, stop=True,
                             skip_group_check=True).then_inc(s_ready, 1)

                def scores(u):
                    h, qt = u // TT, u % TT
                    rows = slice(DH * h, DH * h + DH)
                    e.wait_ge(logits_done, it * 9 + (u + 2))
                    e.matmul(ps[:, S_BANK, 0:(qt + 1) * P], qT[rows, qt * P:(qt + 1) * P], kT[rows, 0:(qt + 1) * P],
                             start=True, stop=True).then_inc(s_ready, 1)

                def probs_T(u):
                    e.wait_ge(probs_done, it * 9 + (u + 2))
                    tp_wait(5 + u)
                    for kt in range(u % TT + 1):
                        mm = e.transpose(ps[:, T_BANK, kt * P:kt * P + P], lgt[:, u % 2, kt * P:kt * P + P], ident[:, :])
                    mm.then_inc(tp_ready, 1)

                def probs_T_s():
                    e.wait_ge(consts, 2)
                    e.wait_ge(probs_done, it * 9 + 1)
                    tp_wait(4)
                    for n in range(NPG):
                        e.transpose(ps[:, T_BANK, n * ROWS_S:(n + 1) * ROWS_S], lgt_s[0:ROWS_S, n * P:n * P + P],
                                    ident[0:ROWS_S, 0:ROWS_S])
                    e.transpose(ps[0:TS, T_BANK, NPG * ROWS_S:(NPG + 1) * ROWS_S], lgt_s[0:ROWS_S, PAST:KS],
                                ident[0:ROWS_S, 0:ROWS_S]).then_inc(tp_ready, 1)

                def values(u):
                    h, qt = u // TT, u % TT
                    if u == 0:
                        e.wait_ge(o_free, it + 1)
                    e.wait_ge(tp_free, it * 13 + (5 + u + 2))
                    for kt in range(qt + 1):
                        mm = e.matmul(ps[DH * h:DH * h + DH, O_BANK, qt * P:(qt + 1) * P],
                                      tok[:, 1, kt, DH * h:DH * h + DH], prT[:, u % 2, kt * P:kt * P + P],
                                      start=kt == 0, stop=kt == qt)
                    if u == 2 * TT - 1:
                        mm.then_inc(pv_done, 1)

                def values_s():
                    e.wait_ge(vc_in, it * 256 + 256)
                    mi_wait(3)
                    e.matmul(ps[:, M_BANK, 0:ROWS_S], tok[0:TS, 1, TT, :], prT_s[0:TS, 2, :], start=True, stop=False,
                             skip_group_check=True)
                    for b in range(DEC_B):
                        for n in range(NPG):
                            mm = e.matmul(ps[:, M_BANK, 8 * b:8 * b + 8], vc[:, NPG * b + n, :],
                                          prT_s[:, n, 8 * b:8 * b + 8], start=False, stop=b == DEC_B - 1 and n == NPG - 1,
                                          skip_group_check=True)
                    mm.then_inc(mi_ready, 1)

                def tok_prompt(use, src, free, n_free):
                    e.wait_ge(tile_free[free], it * 4 + n_free)
                    mi_wait(use)
                    for tt in range(TT):
                        mm = e.transpose(ps[:, M_BANK, tt * P:tt * P + P], src[:, tt * P:tt * P + P], ident[:, :])
                    mm.then_inc(mi_ready, 1)

                def tok_sample():
                    mi_wait(1)
                    e.transpose(ps[0:TS, M_BANK, 0:P], kT[:, SEQ:T], ident[:, :])
                    e.transpose(ps[0:TS, M_BANK, P:2 * P], vT[:, SEQ:T], ident[:, :]).then_inc(mi_ready, 1)

                def rg(g, h):
                    if g == 0 and h == 0:
                        e.wait_ge(conv_step, it * 8 + 8)
                        e.wait_ge(bd_in, it * 64 + 64)
                    mi_wait(4 + 2 * g + h)
                    e.matmul(ps[:, M_BANK, 0:EH], bd[:, g, :], xc[:, EH * h:EH * h + EH], start=True,
                             stop=True).then_inc(mi_ready, 1)

                begin(0); part(0, 0, 4); cache_T(0); part(0, 4, 8)
                begin(1); cache_T(1); part(1, 0, 4); cache_T(2); part(1, 4, 8)
                begin(2); cache_T(3); part(2, 0, 5); scores_s(); part(2, 5, 8)
                begin(3); scores(0); part(3, 0, 2); probs_T_s(); part(3, 2, 4)
                tok_prompt(0, vT, 0, 3); probs_T(0); scores(1); part(3, 4, 6); tok_sample(); part(3, 6, 8)
                begin(4); tok_prompt(2, kT, 1, 2); values(0); probs_T(1); scores(2); part(4, 0, 4)
                values_s(); values(1); probs_T(2); scores(3); part(4, 4, 8)
                begin(5); values(2); probs_T(3); scores(4); part(5, 0, 2); rg(0, 0); part(5, 2, 4)
                values(3); probs_T(4); scores(5); rg(0, 1); part(5, 4, 6); rg(1, 0); part(5, 6, 8)
                begin(6); values(4); probs_T(5); scores(6); rg(1, 1); part(6, 0, 4)
                values(5); probs_T(6); scores(7); part(6, 4, 8)
                begin(7); values(6); probs_T(7); part(7, 0, 4); values(7); part(7, 4, 8)

            with e.Fori(0, GT_TAIL // 2) as n:
                for s in range(2):
                    split_ready(n * 2 + (C_TAIL + s))
                    e.wait_ge(tile_free[s], n + (4 * PAIRS + 1))
                    steps(s, 2 * s, xin_hi, xin_lo, [(k, k) for k in range(KD)], True, True).then_inc(tile_done, 1)
            e.wait_ge(st_saved, PAIRS)
            e.wait_ge(mi_free, 8 * PAIRS + 1)
            for f in range(PAIRS):
                mm = e.transpose(ps[0:36, M_BANK, f * P:f * P + P], stcol[:, f, :], ident[:, :])
            mm.then_inc(st_ready, 1)

            e.wait_ge(o_free, PAIRS + 1)
            e.wait_ge(rg_done, PAIRS + 1)
            e.wait_ge(logits_done, 9 * PAIRS + 1)
            e.wait_ge(tp_free, 13 * PAIRS + 1)
            e.wait_ge(st_copied, 1)
            for s in range(2):
                e.wait_ge(tile_free[s], 4 * PAIRS + GT_TAIL // 2 + 1)
            with e.Fori(0, KD // 2) as n:
                for s in range(2):
                    split_ready(n * 2 + (C_MIX + s))
                    e.wait_ge(mix_free, n * 2 + (s + 1))
                    steps(s, 4 * s, ocat_hi, ocat_lo, [(k, k) for k in range(PAIRS)], True, True)
                    steps(s, 4 * s + 2, ocat_hi, ocat_lo, [(k, k) for k in range(PAIRS, 2 * PAIRS)], True, True
                          ).then_inc(tile_done, 1)

            e.wait_ge(mix_free, KD + 1)
            with e.Fori(0, KD // 2) as n:
                for s in range(2):
                    split_ready(n * 2 + (C_OUT + s))
                    e.wait_ge(out_free, n * 2 + (s + 1))
                    steps(s, 2 * s, xin_hi, xin_lo, [(k, k) for k in range(KD)], True, True, ready=mix_lo
                          ).then_inc(tile_done, 1)
                    e.wait_ge(mix_free, KD + 2)
                    e.wait_ge(xT_free, n * 2 + (s + 1))
                    e.wait_ge(xk_in[s], n * 32 + 32)
                    for tt in range(TT):
                        e.transpose(ps[:, 4 + 2 * s, tt * P:tt * P + P], xk[s][:, tt, :], ident[:, :])
                    e.transpose(ps[:, 5 + 2 * s, 0:TS], xk[s][0:TS, TT, :], ident[0:TS, 0:TS]).then_inc(xT_ready, 1)

            def sum_squares(acc, pair):
                for h in range(2):
                    mm = e.matmul(ps[:, 2 * pair + h, 0:HT], ones[:, :], acc[:, h * HT:h * HT + HT], start=True, stop=True)
                mm.then_inc(n_ready, 1)

            e.wait_ge(osq_used, KD + 2)
            e.wait_ge(out_free, KD + 2)
            sum_squares(oacc[0], 0)
            e.wait_ge(f_acc, KD)
            sum_squares(oacc[1], 1)

            e.wait_ge(n_std, 2)
            e.wait_ge(xT_free, KD + 2)
            with e.Fori(0, KF // 2) as n:
                for s in range(2):
                    e.wait_ge(gu_free, n * 2 + (s + 1))
                    for c in range(2):
                        split_ready(n * 4 + (C_FFN + 2 * s + c))
                        steps(c, 4 * s + 2 * c, xin_hi, xin_lo, [(k, k) for k in range(KD)], True, True, ready=f_lo
                              ).then_inc(tile_done, 1)

            def down(m, odd, between=None):
                for c in range(3):
                    split_ready(m * 3 + (C_DOWN + c))
                    if c == 0:
                        e.wait_ge(y_free, m + 1)
                    k0 = sum(DOWN_K[:c])
                    steps((odd + c) % 2, 2 * odd, hid_hi, hid_lo, [(k, k0 + k) for k in range(DOWN_K[c])],
                          c == 0, c == 2, ready=hid_l).then_inc(tile_done, 1)
                    if c == 0 and between is not None:
                        x1_T(between, 1 - odd)
                        y_T(between, 1 - odd)

            def x1_T(m, s):
                e.wait_ge(x1s_done, m + 1)
                e.wait_ge(x1t_free, m + 2)
                for tt in range(TT):
                    e.transpose(ps[:, 4, tt * P:tt * P + P], x1s[s][:, tt * P:tt * P + P], ident[:, :])
                e.transpose(ps[0:TS, 5, 0:P], x1s[s][:, SEQ:T], ident[:, :]).then_inc(x1t_ready, 1)

            def y_T(m, s):
                e.wait_ge(y_free, m + 3)
                e.wait_ge(yt_free, m + 1)
                for tt in range(TT):
                    e.transpose(ps[:, 6, tt * P:tt * P + P], yg[s][:, tt * P:tt * P + P], ident[:, :])
                e.transpose(ps[0:TS, 7, 0:P], yg[s][:, SEQ:T], ident[:, :]).then_inc(yt_ready, 1)

            e.wait_ge(gu_free, KF + 1)
            down(0, 0)
            e.wait_ge(gu_free, KF + 2)
            with e.Fori(0, (KD - 2) // 2) as n:
                down(n * 2 + 1, 1, n * 2)
                down(n * 2 + 2, 0, n * 2 + 1)
            down(KD - 1, 1, KD - 2)
            x1_T(KD - 1, 1)
            y_T(KD - 1, 1)
            e.wait_ge(ysq_used, KD + 1)
            for tt in range(TT + 1):
                rows = P if tt < TT else TS
                mm = e.matmul(ps[0:rows, 0, tt:tt + 1], yacc[:, tt * P:tt * P + rows], ones[:, 0:1],
                              start=True, stop=True)
            mm.then_inc(yn_ready, 1)

        @block.scalar
        def _(e):
            def hi(i, i2, s, k=KD):
                e.wait_ge(w_in_slot[s], i2 * 32 + 32)
                e.wait_ge(tile_done, i + 1)
                e.activation(w_hi[s][:, 0:k, :], w_raw[s][:, 0:k, :], ACT.Copy).then_inc(hi_done, 1)

            e.dma_start(g_row[:, :], AP(norm_mix_pre.tensor, 0, [[0, P], [1, D]])).then_inc(g_in, 16)
            for src, r0, n in ((conv_w, 0, 16), (conv_b, 16, 4), (rg_b_r, 20, 4), (rg_b_i, 24, 4),
                               (rg_lambda, 28, 4), (norm_mix_post, 32, 8), (norm_ffn_pre, 40, 8), (norm_ffn_post, 48, 8)):
                e.dma_start(prow[r0:r0 + n, :], AP(src.tensor, 0, [[P, n], [1, P]])).then_inc(par_in, 16)
            e.dma_start(strow[0:24, :], state_conv[0].rearrange("b j c -> (b j) c")).then_inc(par_in, 16)
            e.dma_start(strow[24:32, :], state_h[0]).then_inc(par_in, 16)
            e.dma_start(bktab[:, :], bucket_of).then_inc(rel_in, 16)
            e.wait_ge(sp_dve, 1)
            e.dma_start(rel33[0:NB, :], rel_bias).then_inc(rel_in, 16)
            e.wait_ge(consts_v, 3)
            for tt in range(TT + 1):
                rows = P if tt < TT else TS
                e.wait_ge(x_in[tt], 16)
                e.activation(x_sq[0:rows, :], x_tok[0:rows, tt, :], ACT.Square,
                             accum_out=ssum[0:rows, tt:tt + 1]).then_inc(sq_sum, 1)
                e.wait_ge(sq_sum, tt + 1)
                e.activation(rstd_x[0:rows, tt:tt + 1], ssum[0:rows, tt:tt + 1], ACT.Sqrt,
                             bias=eps_col[0:rows, :], scale=1.0 / D).then_inc(std_x, 1)
            e.wait_ge(small_c, 4)
            e.dma_start(dist_bias, drow[:, :]).then_inc(dist_out, 16)
            for tt in range(TT + 1):
                rows = P if tt < TT else TS
                for hf in range(2 if tt < TT else 1):
                    f = 2 * tt + hf
                    e.wait_ge(xt_ready, f + 1)
                    dst, src = x_fill(xin_hi, tt, hf, f)
                    e.activation(dst, src, ACT.Copy).then_inc(xt_hi, 1)
            hi(0, 0, 0)
            e.wait_ge(dist_out, 16)
            for h in range(2):
                rows = slice(4 * h, 4 * h + 4)
                e.dma_start(bias8_rev[rows, :, TS:KS], AP(dist_bias.tensor, h * RELW + 128, [[1, 4], [2 * RELW, PAIRS], [1, PAST]])
                            ).then_inc(bias8_in, 16)
                for b0 in range(PAIRS):
                    e.dma_start(bias8_rev[rows, b0, 0:TS].rearrange("p (b t) -> p b t", t=DEC_T),
                                AP(dist_bias.tensor, (2 * b0 + h) * RELW + 124, [[1, 4], [0, DEC_B], [1, DEC_T]])
                                ).then_inc(bias8_in, 16)
            e.wait_ge(sp_dve, SP_ABS)
            e.activation(sp[2][:, :], sp[1][:, :], ACT.Exp, scale=-1.0).then_inc(sp_act, 1)

            with e.Fori(0, PAIRS) as it:
                def next_hi(j):
                    hi(it * TILES_IT + (j + 1), it * 4 + (j + 1) // 2, (j + 1) % 2)

                def done(j):
                    e.wait_ge(tile_done, it * TILES_IT + (j + 3))

                def gate(j):
                    done(j)
                    dst = gates[:, :, :].rearrange("p k t -> p (k t)")[:, bass.ds(it * (GT_IT * T) + (j - 5) * T, T)]
                    e.activation(halves(dst), two(j % 2), ACT.Tanh, scale=0.5).then_inc(tile_free[j % 2], 1)

                def cache_copy(f):
                    e.wait_ge(tp_ready, it * 13 + (f + 1))
                    e.activation(kcT[:, 2 * f:2 * f + 2, :], ps[:, T_BANK, :].rearrange("p (b k) -> p b k", b=2),
                                 ACT.Copy).then_inc(tp_free, 1)

                def exp_s():
                    e.wait_ge(logits_done, it * 9 + 2)
                    e.activation(lgt_s[0:ROWS_S, :], lgt_s[0:ROWS_S, :], ACT.Exp, bias=nmax[0:ROWS_S, 0:1], scale=-1.0,
                                 accum_out=den[0:ROWS_S, 0:1]).then_inc(exp_done, 1)

                def exp(u):
                    n = (u % TT + 1) * P
                    e.wait_ge(logits_done, it * 9 + (u + 3))
                    e.activation(lgt[:, u % 2, 0:n], lgt[:, u % 2, 0:n], ACT.Exp, bias=nmax[:, u + 1:u + 2], scale=-1.0,
                                 accum_out=den[:, u + 1:u + 2]).then_inc(exp_done, 1)

                def probs_copy(u):
                    n = (u % TT + 1) * P
                    e.wait_ge(tp_ready, it * 13 + (5 + u + 1))
                    e.activation(prT[:, u % 2, 0:n], ps[:, T_BANK, 0:n], ACT.Copy).then_inc(tp_free, 1)

                def rg_gate(use, dst):
                    g, h = (use - 4) // 2, use % 2
                    e.wait_ge(mi_ready, it * 8 + (use + 1))
                    e.activation(dst[:, EH * h:EH * h + EH], ps[:, M_BANK, 0:EH], ACT.Tanh, bias=prm_it[:, 5 + g:6 + g],
                                 scale=0.5).then_inc(mi_free, 1)

                next_hi(0); cache_copy(0)
                next_hi(1)
                done(0)
                e.activation(halves(qT[:, :]), two(0), ACT.Copy, scale=DH ** -0.5).then_inc(tile_free[0], 1)
                cache_copy(2)
                next_hi(2)
                exp_s()
                next_hi(3)
                done(2)
                e.activation(halves(vT[:, :]), two(0), ACT.Copy).then_inc(tile_free[0], 1)
                e.wait_ge(tp_ready, it * 13 + 5)
                e.activation(prT_s[:, 0:NPG, :], ps[:, T_BANK, 0:NPG * ROWS_S].rearrange("p (n r) -> p n r", n=NPG), ACT.Copy)
                e.activation(prT_s[0:TS, NPG, :], ps[0:TS, T_BANK, NPG * ROWS_S:(NPG + 1) * ROWS_S],
                             ACT.Copy).then_inc(tp_free, 1)
                exp(0); probs_copy(0); exp(1)
                next_hi(4)
                e.wait_ge(mi_ready, it * 8 + 3)
                e.activation(tok[:, 0, 0:TT, :], ps[:, M_BANK, :].rearrange("p (tt c) -> p tt c", c=P), ACT.Copy
                             ).then_inc(mi_free, 1)
                probs_copy(1); exp(2)
                probs_copy(2); exp(3)
                e.wait_ge(mi_ready, it * 8 + 4)
                for h in range(2):
                    rows = slice(DH * h, DH * h + DH)
                    last = e.activation(bt(ocat_hi[rows, :, :].rearrange("p k t -> p (k t)")[:, bass.ds(it * T + SEQ, TS)]),
                                        ps[rows, M_BANK, 0:ROWS_S].rearrange("p (b h t) -> p b h t", h=2, t=DEC_T)[:, :, h, :],
                                        ACT.Copy)
                last.then_inc(so_hi, 1)
                next_hi(5)
                done(4)
                e.activation(halves(gb[:, :]), two(0), ACT.Copy).then_inc(tile_free[0], 1)
                probs_copy(3); exp(4)
                rg_gate(4, th)
                probs_copy(4); exp(5)
                rg_gate(5, th)
                rg_gate(6, ti)
                next_hi(6)
                rg_gate(7, ti)
                gate(5)
                e.activation(th[:, :], th[:, :], ACT.Tanh, bias=prm_it[:, 7:8], scale=prm_it[:, 7:8]).then_inc(th_done, 1)
                probs_copy(5); exp(6)
                e.wait_ge(gelu_step, it * 3 + 3)
                e.activation(gp[:, :], gp[:, :], ACT.Tanh).then_inc(tg_done, 1)
                probs_copy(6); exp(7)
                next_hi(7)
                gate(6)
                probs_copy(7)
                e.wait_ge(th_done, it + 1)
                e.activation(sq[:, :], th[:, :], ACT.Sqrt, bias=tiny_col[:, :]).then_inc(sq_done, 1)
                e.wait_ge(pv_done, it + 1)
                e.activation(ocat_hi[:, bass.ds(it, 1), 0:SEQ], ps[:, O_BANK, :], ACT.Copy).then_inc(o_hi, 1)
                gate(7)
                e.wait_ge(rg_step, it * 12 + 12)
                e.activation(ocat_hi[:, bass.ds(it + PAIRS, 1), :], dd[:, 0:T], ACT.Copy).then_inc(orn_hi, 1)

            with e.Fori(0, GT_TAIL // 2) as n:
                for s in range(2):
                    i = n * 2 + (C_TAIL + s)
                    hi(i + 1, n + (C_TAIL + s + 1) // 2, 1 - s)
                    e.wait_ge(tile_done, i + 3)
                    dst = gates[:, :, :].rearrange("p k t -> p (k t)")[:, bass.ds(n * (2 * T) + (PAIRS * GT_IT + s) * T, T)]
                    e.activation(halves(dst), two(s), ACT.Tanh, scale=0.5).then_inc(tile_free[s], 1)

            with e.Fori(0, KD // 2) as n:
                for s in range(2):
                    hi(n * 2 + (C_MIX + s + 1), n + (C_MIX + s + 1) // 2, 1 - s)
                    e.wait_ge(mix_sum, n * 2 + (s + 1))
                    e.activation(tile_of(xin_hi, n * 2, s), halves(ma[s][:, :]), ACT.Copy, scale=0.5).then_inc(mix_hi, 1)

            with e.Fori(0, KD // 2) as n:
                for s in range(2):
                    i = n * 2 + (C_OUT + s)
                    hi(i + 1, n + (C_OUT + s + 1) // 2, 1 - s)
                    e.wait_ge(tile_done, i + 3)
                    e.activation(tile_of(og, n * 2, s), two(s), ACT.Identity, scale=prm[:, bass.ds(n * 2 + (32 + s), 1)])
                    e.wait_ge(osq_used, n * 2 + (s + 1))
                    e.activation(halves(osq[s][:, :]), two(s), ACT.Square).then_inc(out_free, 1)
            hi(C_FFN + 1, (C_FFN + 1) // 2, 1)

            def rms(pair, n):
                e.wait_ge(n_ready, n)
                if n > 1:
                    e.wait_ge(n_rstd, n - 1)
                e.activation(halves(std[:, :]), two(pair), ACT.Sqrt, bias=eps_col[:, :], scale=1.0 / D).then_inc(n_std, 1)

            rms(0, 1)
            for k in range(KD):
                e.wait_ge(x1_done, k + 1)
                e.activation(xin_hi[:, k, :], x1[:, k, :], ACT.Identity, scale=prm[:, 40 + k:41 + k]).then_inc(f_hi, 1)
                if k >= 2:
                    e.wait_ge(f_acc, k - 1)
                e.activation(osq[k % 2][:, :], x1[:, k, :], ACT.Square).then_inc(f_sq, 1)
            rms(1, 2)

            with e.Fori(0, KF) as m:
                hi(m * 2 + (C_FFN + 2), m + (C_FFN + 2) // 2, 0)
                e.wait_ge(gu_scaled, m + 1)
                e.activation(ft[:, :], fg[:, :], ACT.Tanh, scale=0.5).then_inc(fsil, 1)
                hi(m * 2 + (C_FFN + 3), m + (C_FFN + 2) // 2, 1)
                e.wait_ge(fprod, m * 2 + 2)
                e.activation(tile_of(hid_hi, m), halves(fg[:, :]), ACT.Copy, scale=0.5).then_inc(hid_h, 1)

            def down_hi(n, odd, c):
                q = 3 * odd + c + 2
                hi(n * 6 + (C_DOWN + q), n * 3 + (C_DOWN + q) // 2, q % 2, DOWN_K[(c + 2) % 3])

            def y_evacuate(m, s):
                e.wait_ge(tile_done, m * 3 + (C_DOWN + 5))
                e.activation(halves(yg[s][:, :]), two(s), ACT.Identity, scale=prm[:, bass.ds(m + 48, 1)])
                e.wait_ge(ysq_used, m + 1)
                e.activation(halves(ysq[:, :]), two(s), ACT.Square).then_inc(y_free, 1)

            def y_copy(m):
                e.wait_ge(yt_ready, m + 1)
                e.activation(ytok[:, 0:TT, bass.ds(m * P, P)], ps[:, 6, :].rearrange("p (tt c) -> p tt c", c=P), ACT.Copy)
                e.activation(ytok[0:TS, TT, bass.ds(m * P, P)], ps[0:TS, 7, 0:P], ACT.Copy).then_inc(yt_free, 1)

            def y_tile(n, odd, copy=True):
                m = n * 2 + odd
                down_hi(n, odd, 0)
                if copy:
                    y_copy(m - 1)
                down_hi(n, odd, 1)
                down_hi(n, odd, 2)
                y_evacuate(m, odd)

            y_tile(0, 0, copy=False)
            with e.Fori(0, (KD - 2) // 2) as n:
                y_tile(n, 1)
                y_tile(n + 1, 0)
            hi(C_DOWN + 3 * KD - 1, (C_DOWN + 3 * KD - 1) // 2, (C_DOWN + 3 * KD - 1) % 2, DOWN_K[2])
            y_copy(KD - 2)
            y_evacuate(KD - 1, 1)
            y_copy(KD - 1)
            e.wait_ge(yn_ready, 1)
            e.activation(ycol[:, 0:TT], ps[:, 0, 0:TT], ACT.Sqrt, bias=eps_col[:, :], scale=1.0 / D)
            e.activation(ycol[0:TS, TT:TT + 1], ps[0:TS, 0, TT:TT + 1], ACT.Sqrt, bias=eps_col[0:TS, :], scale=1.0 / D
                         ).then_inc(ycol_step, 1)

        @block.vector
        def _(e):
            for sem_, n in ((lo_done, 2), (tile_done, 2), (tile_free[0], 1), (tile_free[1], 1), (logits_done, 1),
                            (tp_free, 1), (mi_free, 1), (o_free, 1), (rg_done, 1), (kv_out, 64), (mix_free, 2),
                            (out_free, 2), (osq_used, 2), (xT_free, 2), (gu_free, 2), (y_free, 2), (ysq_used, 1),
                            (x1t_free, 2), (yt_free, 1)):
                e.sem_inc(sem_, n)

            def lo(i, s, k=KD):
                e.wait_ge(hi_done, i + 1)
                e.tensor_tensor(w_lo[s][:, 0:k, :], w_raw[s][:, 0:k, :], w_hi[s][:, 0:k, :].bitcast(F32), ALU.subtract
                                ).then_inc(lo_done, 1)

            e.memset(rel33[:, :], NEG).then_inc(sp_dve, 1)
            e.memset(ones[:, :], 1.0).then_inc(consts_v, 1)
            e.memset(eps_col[:, :], EPS).then_inc(consts_v, 1)
            e.memset(tiny_col[:, :], 1.0e-30).then_inc(consts_v, 1)
            e.wait_ge(g_in, 16)

            def x_norm(tt):
                rows = slice(0, P if tt < TT else TS)
                e.wait_ge(std_x, tt + 1)
                e.reciprocal(rstd_x[rows, tt:tt + 1], rstd_x[rows, tt:tt + 1]).then_inc(rx_done, 1)
                e.wait_ge(rx_done, tt + 1)
                e.scalar_tensor_tensor(x_tok[rows, tt, :], x_tok[rows, tt, :], rstd_x[rows, tt:tt + 1], g_row[rows, :],
                                       ALU.mult, ALU.mult).then_inc(xs_done, 1)

            def x_lo(tt):
                for hf in range(2 if tt < TT else 1):
                    f = 2 * tt + hf
                    e.wait_ge(xt_hi, f + 1)
                    dst, src = x_fill(xin_lo, tt, hf, f)
                    e.tensor_tensor(dst, src, x_fill(xin_hi, tt, hf, f)[0].bitcast(F32), ALU.subtract).then_inc(xt_lo, 1)

            x_norm(0)
            e.wait_ge(small_T, 3)
            e.tensor_copy(drow[:, 0:512], ps[0:HEADS, 2, 0:512]).then_inc(small_c, 1)
            e.tensor_copy(drow[:, 512:RELW], ps[0:HEADS, 3, 0:RELW - 512]).then_inc(small_c, 1)
            e.tensor_copy(prm[:, :], ps[:, 0, 0:56]).then_inc(small_c, 1)
            e.tensor_copy(stT[:, :, :], ps[:, 1, 0:P].rearrange("p (f r) -> p f r", f=PAIRS)).then_inc(small_c, 1)
            x_norm(1)
            x_norm(2)
            x_lo(0)
            x_norm(3)
            x_lo(1)
            x_norm(4)
            for tt in range(2, TT + 1):
                x_lo(tt)
            e.wait_ge(small_c, 4)
            e.tensor_scalar(prm[:, 20:28], prm[:, 20:28], 0.5, None, ALU.mult).then_inc(small_c, 1)
            nl, la, y, mx, z, z2 = (b[:, :] for b in sp)
            e.tensor_scalar(nl, prm[:, 28:32], -1.0, None, ALU.mult).then_inc(sp_dve, 1)
            e.wait_ge(sp_dve, 2)
            e.tensor_tensor(la, nl, prm[:, 28:32], ALU.max).then_inc(sp_dve, 1)
            lo(0, 0)
            e.tensor_scalar(mx, nl, 0.0, None, ALU.max).then_inc(sp_dve, 1)
            e.wait_ge(sp_act, 1)
            e.tensor_scalar(z, y, 2.0, None, ALU.add).then_inc(sp_dve, 1)
            e.wait_ge(sp_dve, 5)
            e.reciprocal(z, z).then_inc(sp_dve, 1)
            e.wait_ge(sp_dve, 6)
            e.tensor_tensor(z, y, z, ALU.mult).then_inc(sp_dve, 1)
            e.wait_ge(sp_dve, 7)
            e.tensor_tensor(z2, z, z, ALU.mult).then_inc(sp_dve, 1)
            e.wait_ge(sp_dve, 8)
            e.tensor_scalar(nl, z2, 1.0 / (2 * SERIES + 1), None, ALU.mult).then_inc(sp_dve, 1)
            for k in range(SERIES - 1, -1, -1):
                e.wait_ge(sp_dve, 8 + SERIES - k)
                e.scalar_tensor_tensor(nl, nl, 1.0 / (2 * k + 1), z2 if k else z, ALU.add, ALU.mult).then_inc(sp_dve, 1)
            e.wait_ge(sp_dve, 9 + SERIES)
            e.scalar_tensor_tensor(nl, nl, 2.0, mx, ALU.mult, ALU.add).then_inc(sp_dve, 1)
            e.wait_ge(sp_dve, 10 + SERIES)
            e.tensor_scalar(prm[:, 28:32], nl, 2.0, None, ALU.mult).then_inc(small_c, 1)

            with e.Fori(0, PAIRS) as it:
                def next_lo(j):
                    lo(it * TILES_IT + (j + 1), (j + 1) % 2)

                def cache_copy(f):
                    e.wait_ge(tp_ready, it * 13 + (f + 1))
                    e.tensor_copy(kcT[:, 2 * f:2 * f + 2, :], ps[:, T_BANK, :].rearrange("p (b k) -> p b k", b=2)
                                  ).then_inc(tp_free, 1)

                def logits(u):
                    h, n = u // TT, (u % TT + 1) * P
                    count = e.to_reg(it * 9 + (u + 2))
                    e.wait_ge(bias_in, 16)
                    e.wait_ge(s_ready, count)
                    e.tensor_tensor_reduce(lgt[:, u % 2, 0:n], ps[:, S_BANK, 0:n], biasT[:, h, 0:n][:, ::-1], -1.0, BIG,
                                           ALU.add, ALU.min, nmax[:, u + 1:u + 2]).then_inc(logits_done, 1)

                def norm(u):
                    n = (u % TT + 1) * P
                    e.wait_ge(exp_done, it * 9 + (u + 2))
                    e.reciprocal(rden[:, u + 1:u + 2], den[:, u + 1:u + 2]).then_inc(rden_done, 1)
                    e.wait_ge(rden_done, it * 9 + (u + 2))
                    e.tensor_scalar(lgt[:, u % 2, 0:n], lgt[:, u % 2, 0:n], rden[:, u + 1:u + 2], None, ALU.mult
                                    ).then_inc(probs_done, 1)

                def rg(step, ins):
                    ins.then_inc(rg_step, 1)

                def rg_wait(step):
                    e.wait_ge(rg_step, it * 12 + step)

                next_lo(0); cache_copy(1)
                next_lo(1); cache_copy(3)
                next_lo(2)
                e.wait_ge(tile_done, it * TILES_IT + 4)
                e.tensor_copy(halves(kT[:, :]), two(1)).then_inc(tile_free[1], 1)
                count = e.to_reg(it * 9 + 1)
                e.wait_ge(consts, 7)
                e.wait_ge(s_ready, count)
                e.tensor_tensor_reduce(lgt_s[0:ROWS_S, :], ps[0:ROWS_S, S_BANK, 0:KS], mask_s[0:ROWS_S, :], -1.0, BIG,
                                       ALU.add, ALU.min, nmax[0:ROWS_S, 0:1]).then_inc(logits_done, 1)
                next_lo(3)
                e.wait_ge(exp_done, it * 9 + 1)
                e.reciprocal(rden[0:ROWS_S, 0:1], den[0:ROWS_S, 0:1]).then_inc(rden_done, 1)
                e.wait_ge(rden_done, it * 9 + 1)
                e.tensor_scalar(lgt_s[0:ROWS_S, :], lgt_s[0:ROWS_S, :], rden[0:ROWS_S, 0:1], None, ALU.mult
                                ).then_inc(probs_done, 1)
                e.wait_ge(bias_in, it * 16 + 16)
                logits(0)
                e.wait_ge(mi_ready, it * 8 + 1)
                e.wait_ge(kv_out, it * 64 + 64)
                e.tensor_copy(tok[:, 1, 0:TT, :], ps[:, M_BANK, :].rearrange("p (tt c) -> p tt c", c=P)).then_inc(mi_free, 1)
                norm(0); logits(1)
                e.wait_ge(mi_ready, it * 8 + 2)
                e.tensor_copy(tok[0:TS, :, TT, :], ps[0:TS, M_BANK, 0:2 * P].rearrange("p (g c) -> p g c", g=2)
                              ).then_inc(mi_free, 1)
                norm(1)
                next_lo(4)
                e.wait_ge(tile_done, it * TILES_IT + 6)
                e.wait_ge(it_ready, it + 1)
                e.tensor_copy(xp[:, CW - 1:CW - 1 + HT], ps[:, 2, 0:HT])
                e.tensor_copy(xp[:, CW - 1 + HT:CW - 1 + SEQ], ps[:, 3, 0:SEQ - HT])
                e.tensor_copy(xps[:, :, CW - 1:CW - 1 + DEC_T], bt(ps[:, 3, SEQ - HT:HT])).then_inc(tile_free[1], 1)
                logits(2); norm(2); logits(3)
                e.wait_ge(tile_free[1], it * 4 + 3)
                for j in range(CW):
                    for g, (dst, src) in enumerate((
                            (xc[:, 0:SEQ], xp[:, j:j + SEQ]),
                            (xc[:, SEQ:EXT].rearrange("p (b k) -> p b k", b=DEC_B)[:, :, 1:1 + DEC_T],
                             xps[:, :, j:j + DEC_T]))):
                        if j == 0:
                            e.tensor_scalar(dst, src, prm_it[:, 0:1], prm_it[:, 4:5], ALU.mult, ALU.add
                                            ).then_inc(conv_step, 1)
                        else:
                            e.wait_ge(conv_step, it * 8 + (2 * j + g - 1))
                            e.scalar_tensor_tensor(dst, src, prm_it[:, j:j + 1], dst, ALU.mult, ALU.add
                                                   ).then_inc(conv_step, 1)
                norm(3)
                e.wait_ge(so_hi, it + 1)
                for h in range(2):
                    rows = slice(DH * h, DH * h + DH)
                    cols = bass.ds(it * T + SEQ, TS)
                    last = e.tensor_tensor(bt(ocat_lo[rows, :, :].rearrange("p k t -> p (k t)")[:, cols]),
                                           ps[rows, M_BANK, 0:ROWS_S].rearrange("p (b h t) -> p b h t", h=2, t=DEC_T)[:, :, h, :],
                                           bt(ocat_hi[rows, :, :].rearrange("p k t -> p (k t)")[:, cols].bitcast(F32)),
                                           ALU.subtract)
                last.then_inc(mi_free, 1)
                next_lo(5)
                logits(4); norm(4); logits(5); norm(5)
                next_lo(6)
                logits(6); norm(6)
                e.wait_ge(th_done, it + 1)
                rg(1, e.tensor_scalar(dd[:, :], th[:, :], 1.0, None, ALU.add))
                rg_wait(1)
                rg(2, e.reciprocal(dd[:, :], dd[:, :]))
                logits(7); norm(7)
                rg_wait(2)
                rg(3, e.tensor_scalar(aa[:, :], dd[:, :], 2.0, -1.0, ALU.mult, ALU.add))
                rg_wait(3)
                resets = [b[:, SEQ:EXT].rearrange("p (b k) -> p b k", b=DEC_B)[:, :, 0:1] for b in (aa, ti)]
                rg(4, e.memset(resets[0], 0.0))
                next_lo(7)
                rg(5, e.scalar_tensor_tensor(ti[:, :], ti[:, :], 1.0, xc[:, :], ALU.add, ALU.mult))
                e.wait_ge(sq_done, it + 1)
                rg(6, e.tensor_tensor(sq[:, :], sq[:, :], dd[:, :], ALU.mult))
                rg_wait(6)
                rg(7, e.tensor_tensor(ti[:, :], ti[:, :], sq[:, :], ALU.mult))
                rg_wait(7)
                rg(8, e.tensor_copy(resets[1], stT[:, bass.ds(it, 1), 24:32].rearrange("p o b -> p b o")))
                rg_wait(8)
                rg(9, e.tensor_tensor_scan(sq[:, :], aa[:, :], ti[:, :], 0.0, ALU.mult, ALU.add))
                e.wait_ge(tg_done, it + 1)
                rg(10, e.scalar_tensor_tensor(gp[:, :], gp[:, :], 1.0, gb[:, :], ALU.add, ALU.mult))
                rg_wait(10)
                rg(11, e.scalar_tensor_tensor(dd[:, 0:SEQ], sq[:, 0:SEQ], 0.5, gp[:, 0:SEQ], ALU.mult, ALU.mult))
                rg(12, e.scalar_tensor_tensor(bt(dd[:, SEQ:T]),
                                              sq[:, SEQ:EXT].rearrange("p (b k) -> p b k", b=DEC_B)[:, :, 1:1 + DEC_T], 0.5,
                                              bt(gp[:, SEQ:T]), ALU.mult, ALU.mult))
                e.wait_ge(o_hi, it + 1)
                e.tensor_tensor(ocat_lo[:, bass.ds(it, 1), 0:SEQ], ps[:, O_BANK, :],
                                ocat_hi[:, bass.ds(it, 1), 0:SEQ].bitcast(F32), ALU.subtract).then_inc(o_free, 1)
                e.wait_ge(orn_hi, it + 1)
                e.tensor_tensor(ocat_lo[:, bass.ds(it + PAIRS, 1), :], dd[:, 0:T],
                                ocat_hi[:, bass.ds(it + PAIRS, 1), :].bitcast(F32), ALU.subtract).then_inc(rg_done, 1)

            with e.Fori(0, GT_TAIL // 2) as n:
                for s in range(2):
                    lo(n * 2 + (C_TAIL + s + 1), 1 - s)
            e.wait_ge(st_ready, 1)
            e.tensor_copy(st_out[:, :], ps[0:36, M_BANK, :]).then_inc(st_copied, 1)

            e.wait_ge(kv_out, 64 * (PAIRS + 1))
            with e.Fori(0, KD // 2) as n:
                for s in range(2):
                    i = n * 2 + (C_MIX + s)
                    lo(i + 1, 1 - s)
                    e.wait_ge(tile_done, i + 3)
                    for g, dst in ((0, ma[s]), (1, mr[s])):
                        last = e.scalar_tensor_tensor(halves(dst[:, :]), tile_of(gates, n * 2, s + KD * g), 1.0,
                                                      two(2 * s + g), ALU.add, ALU.mult)
                    last.then_inc(mix_free, 1)
                    e.wait_ge(mix_free, n * 2 + (s + 3))
                    e.tensor_tensor(ma[s][:, :], ma[s][:, :], mr[s][:, :], ALU.add).then_inc(mix_sum, 1)
                    e.wait_ge(mix_hi, n * 2 + (s + 1))
                    e.scalar_tensor_tensor(tile_of(xin_lo, n * 2, s), halves(ma[s][:, :]), 0.5,
                                           tile_of(xin_hi, n * 2, s).bitcast(F32), ALU.mult, ALU.subtract
                                           ).then_inc(mix_lo, 1)

            e.wait_ge(tile_done, C_OUT + 2)
            e.memset(oacc[0][:, :], 0.0).then_inc(acc_zero, 1)
            e.wait_ge(acc_zero, 1)
            e.wait_ge(st_out_s, 64)
            with e.Fori(0, KD // 2) as n:
                for s in range(2):
                    lo(n * 2 + (C_OUT + s + 1), 1 - s)
                    e.wait_ge(xT_ready, n * 2 + (s + 1))
                    e.tensor_copy(x1[:, bass.ds(n * 2 + s, 1), 0:SEQ], ps[:, 4 + 2 * s, :])
                    e.tensor_copy(x1[:, bass.ds(n * 2 + s, 1), SEQ:T], ps[:, 5 + 2 * s, 0:TS]).then_inc(xT_free, 1)
                    e.wait_ge(out_free, n * 2 + (s + 3))
                    e.wait_ge(osq_used, n * 2 + (s + 2))
                    e.tensor_tensor(oacc[0][:, :], oacc[0][:, :], osq[s][:, :], ALU.add).then_inc(osq_used, 1)
            lo(C_FFN + 1, 1)
            e.wait_ge(n_std, 1)
            e.reciprocal(rb[0][:, :], std[:, :]).then_inc(n_rstd, 1)
            e.wait_ge(n_rstd, 1)
            for k in range(KD + 1):
                if k < KD:
                    e.tensor_tensor(og[:, k, :], og[:, k, :], rb[0][:, :], ALU.mult).then_inc(t_done, 1)
                    e.wait_ge(t_done, k + 1)
                    e.tensor_tensor(x1[:, k, :], x1[:, k, :], og[:, k, :], ALU.add).then_inc(x1_done, 1)
                if k >= 1:
                    e.wait_ge(f_hi, k)
                    e.scalar_tensor_tensor(xin_lo[:, k - 1, :], x1[:, k - 1, :], prm[:, 39 + k:40 + k],
                                           xin_hi[:, k - 1, :].bitcast(F32), ALU.mult, ALU.subtract).then_inc(f_lo, 1)
            e.wait_ge(n_std, 2)
            e.reciprocal(rb[1][:, :], std[:, :]).then_inc(n_rstd, 1)
            e.wait_ge(n_rstd, 2)

            with e.Fori(0, KF // 2) as n:
                for s in range(2):
                    m = n * 2 + s
                    rms_b = halves(rb[1][:, :])
                    lo(n * 4 + (C_FFN + 2 * s + 2), 0)
                    e.wait_ge(tile_done, n * 4 + (C_FFN + 2 * s + 3))
                    e.wait_ge(lo_done, n * 4 + (C_FFN + 2 * s + 5))
                    e.tensor_tensor(halves(fg[:, :]), two(2 * s), rms_b, ALU.mult).then_inc(gu_scaled, 1)
                    lo_next = lambda: lo(n * 4 + (C_FFN + 2 * s + 3), 1)
                    e.wait_ge(fsil, m + 1)
                    e.scalar_tensor_tensor(fg[:, :], ft[:, :], 1.0, fg[:, :], ALU.add, ALU.mult).then_inc(fprod, 1)
                    lo_next()
                    e.wait_ge(tile_done, n * 4 + (C_FFN + 2 * s + 4))
                    e.tensor_tensor(halves(fu[:, :]), two(2 * s + 1), rms_b, ALU.mult).then_inc(gu_free, 1)
                    e.wait_ge(gu_free, m + 3)
                    e.wait_ge(fprod, m * 2 + 1)
                    e.tensor_tensor(fg[:, :], fg[:, :], fu[:, :], ALU.mult).then_inc(fprod, 1)
                    e.wait_ge(hid_h, m + 1)
                    e.scalar_tensor_tensor(tile_of(hid_lo, n * 2, s), halves(fg[:, :]), 0.5,
                                           tile_of(hid_hi, n * 2, s).bitcast(F32), ALU.mult, ALU.subtract
                                           ).then_inc(hid_l, 1)

            e.wait_ge(tile_done, C_DOWN + 2)
            e.memset(yacc[:, :], 0.0).then_inc(acc_zero, 1)
            e.wait_ge(acc_zero, 2)

            def down_lo(n, odd, c):
                q = 3 * odd + c + 2
                lo(n * 6 + (C_DOWN + q), q % 2, DOWN_K[(c + 2) % 3])

            def x1_copy(m):
                e.wait_ge(x1t_ready, m + 1)
                e.tensor_copy(x1tok[:, 0:TT, bass.ds(m * P, P)], ps[:, 4, :].rearrange("p (tt c) -> p tt c", c=P))
                e.tensor_copy(x1tok[0:TS, TT, bass.ds(m * P, P)], ps[0:TS, 5, 0:P]).then_inc(x1t_free, 1)

            def y_square(m):
                e.wait_ge(y_free, m + 3)
                e.wait_ge(ysq_used, m + 1)
                e.tensor_tensor(yacc[:, :], yacc[:, :], ysq[:, :], ALU.add).then_inc(ysq_used, 1)

            def y_tile(n, odd, copy=True):
                m = n * 2 + odd
                down_lo(n, odd, 0)
                if copy:
                    x1_copy(m - 1)
                down_lo(n, odd, 1)
                down_lo(n, odd, 2)
                y_square(m)

            y_tile(0, 0, copy=False)
            with e.Fori(0, (KD - 2) // 2) as n:
                y_tile(n, 1)
                y_tile(n + 1, 0)
            lo(C_DOWN + 3 * KD - 1, (C_DOWN + 3 * KD - 1) % 2, DOWN_K[2])
            x1_copy(KD - 2)
            y_square(KD - 1)
            x1_copy(KD - 1)
            e.wait_ge(ycol_step, 1)
            e.reciprocal(ycol[:, 8:8 + TT], ycol[:, 0:TT])
            e.reciprocal(ycol[0:TS, 8 + TT:9 + TT], ycol[0:TS, TT:TT + 1]).then_inc(ycol_step, 1)
            e.wait_ge(ycol_step, 2)
            e.wait_ge(x1t_free, KD + 2)
            e.wait_ge(yt_free, KD + 1)
            for tt in range(TT + 1):
                rows = slice(0, P if tt < TT else TS)
                e.scalar_tensor_tensor(ytok[rows, tt, :], ytok[rows, tt, :], ycol[rows, 8 + tt:9 + tt], x1tok[rows, tt, :],
                                       ALU.mult, ALU.add).then_inc(z_done, 1)


_INS = ["x_prompt", "x_sample", "cache_k", "cache_v", "page_table", "state_conv", "state_h",
        "norm_mix_pre", "norm_mix_post", "w_in", "rel_bias", "conv_w", "conv_b", "rg_w_r", "rg_b_r",
        "rg_w_i", "rg_b_i", "rg_lambda", "w_proj_attn", "w_proj_rnn", "w_out", "norm_ffn_pre",
        "norm_ffn_post", "w_gate_up", "w_down"]
_OUTS = [(1, SEQ, D), (DEC_B, DEC_T, D), (1, 1, SEQ, HEADS, DH), (1, 1, SEQ, HEADS, DH),
         (1, DEC_B, DEC_T, HEADS, DH), (1, DEC_B, DEC_T, HEADS, DH), (1, 1, CW - 1, DR), (1, 1, DR),
         (1, DEC_B, CW - 1, DR), (1, DEC_B, DR)]


def kernel(**inputs):
    import numpy as _np
    import concourse.bacc as _bacc
    from concourse import mybir as _mybir
    from concourse.bass_utils import run_bass_kernel_spmd as _run

    nc = _bacc.Bacc("TRN2", target_bir_lowering=False, num_devices=1)
    arrays, args = {}, []
    for name in _INS + ["bucket_of"]:
        a = bucket_table() if name == "bucket_of" else _np.ascontiguousarray(inputs[name])
        arrays[f"in_{name}_dram"] = a
        args.append(nc.dram_tensor(f"in_{name}_dram", a.shape, _mybir.dt.from_np(a.dtype), kind="ExternalInput").ap())
    for i, shape in enumerate(_OUTS):
        args.append(nc.dram_tensor(f"out_{i}_dram", shape, _mybir.dt.float32, kind="ExternalOutput").ap())
    program(nc, *args)
    r = _run(nc, [arrays], core_ids=[0])
    return tuple(r.results[0][f"out_{i}_dram"] for i in range(len(_OUTS)))
```

```python
import math
from contextlib import ExitStack

import numpy as np

import concourse.bass as bass
from concourse import mybir

F32 = mybir.dt.float32
F32R = mybir.dt.float32r
I32 = mybir.dt.int32
ALU = mybir.AluOpType
ACT = mybir.ActivationFunctionType
AP = bass.AP

P = 128
D = 1024
KD = D // P
SEQ = 512
DEC_B, DEC_T = 8, 4
TS = DEC_B * DEC_T
T = SEQ + TS
HT = T // 2
HEADS, DH = 8, 64
DA = HEADS * DH
PAIRS = DA // P
DR = 512
RGB = 64
CW = 4
PAST = 256
PAGE = 128
NPG = PAST // PAGE
DFF = -(-8 * D // (3 * 256)) * 256
KF = DFF // P
TT = SEQ // P
NB, MAXD = 32, 128
EPS = 1e-6
NEG = -1.0e30
BIG = 3.0e38
EXT = SEQ + DEC_B * (DEC_T + 1)
EH = EXT // 2
RELW = 640
KS = PAST + TS
ROWS_S = DEC_B * 2 * DEC_T

TILES_IT = 8
GT_IT = 3
C_TAIL = PAIRS * TILES_IT
GT_TAIL = 2 * KD - PAIRS * GT_IT
C_MIX = C_TAIL + GT_TAIL
C_OUT = C_MIX + KD
C_FFN = C_OUT + 2 * KD
C_DOWN = C_FFN + 2 * KF
DOWN_K = [8, 8, KF - 16]

SERIES = 9
GELU_C1 = math.sqrt(2.0 / math.pi)
GELU_C2 = GELU_C1 * 0.044715


def bucket_table():
    n = np.arange(RELW) - 127
    pos = np.maximum(n, 1).astype(np.float32)
    half = NB // 2
    large = half + (np.log(pos / half) / math.log(MAXD / half) * (NB - half)).astype(np.int32)
    bucket = np.where(n < half, np.maximum(n, 0), np.minimum(large, NB - 1))
    table = np.zeros((NB + 1, RELW), np.float32)
    table[np.where(n < 0, NB, bucket), np.arange(RELW)] = 1.0
    return table


def program(nc, x_prompt, x_sample, cache_k, cache_v, page_table, state_conv, state_h,
            norm_mix_pre, norm_mix_post, w_in, rel_bias, conv_w, conv_b, rg_w_r, rg_b_r,
            rg_w_i, rg_b_i, rg_lambda, w_proj_attn, w_proj_rnn, w_out, norm_ffn_pre,
            norm_ffn_post, w_gate_up, w_down, bucket_of,
            y_prompt, y_sample, new_k_prompt, new_v_prompt, new_k_sample, new_v_sample,
            new_conv_prompt, new_h_prompt, new_conv_sample, new_h_sample):
    n_phys = cache_k.shape[1]
    dist_bias = nc.dram_tensor("dist_bias", (HEADS, RELW), F32, kind="Internal").ap()

    at = [-(-nc.sbuf_base // 64) * 64]

    def put(name, shape, dt=F32, where=None):
        size = 4 * int(np.prod(shape[1:]))
        size = -(-size // 32) * 32
        if where is None:
            offset, at[0] = at[0], at[0] + size
        else:
            offset, where[0] = where[0], where[0] + size
        assert offset + size <= nc.sbuf_usable_end, (name, offset + size)
        return nc.alloc_sbuf_tensor_at(name, shape, dt, offset=offset)

    ring = [[put(f"w_{part}{s}", [P, KD, P], dt) for s in range(2)]
            for part, dt in (("raw", F32), ("hi", F32R), ("lo", F32R))]
    w_raw, w_hi, w_lo = ring
    xin_at = at[0]
    xin_hi = put("xin_hi", [P, KD, T], F32R)
    xin_lo = put("xin_lo", [P, KD, T], F32R)
    ident = put("ident", [P, P])
    ones = put("ones", [P, P])
    prm = put("prm", [P, 56])
    eps_col = put("eps_col", [P, 1])
    tiny_col = put("tiny_col", [P, 1])
    big_at = at[0]

    ocat_hi = put("ocat_hi", [P, 2 * PAIRS, T], F32R)
    ocat_lo = put("ocat_lo", [P, 2 * PAIRS, T], F32R)
    gates = put("gates", [P, 2 * KD, T])
    stage_at = at[0]
    qT, kT, vT = (put(n, [P, T]) for n in ("qT", "kT", "vT"))
    tok = put("tok", [P, 2, TT + 1, P])
    q_bd = put("q_bd", [P, 72 * DEC_B])
    q_all = put("q_all", [P, ROWS_S])
    kcT = put("kcT", [P, DEC_B, PAST])
    kc = put("kc", [P, DEC_B * NPG, P])
    vc = put("vc", [P, DEC_B * NPG, P])
    biasT = put("biasT", [P, 2, SEQ])
    lgt_at = at[0]
    lgt = put("lgt", [P, 2, SEQ])
    prT = put("prT", [P, 2, SEQ])
    lgt_s = put("lgt_s", [P, KS])
    prT_s = put("prT_s", [P, 3, ROWS_S])
    mask_s = put("mask_s", [P, KS])
    bias8 = put("bias8", [P, PAIRS, KS])
    rep8 = put("rep8", [P, P])
    nmax = put("nmax", [P, 9])
    den = put("den", [P, 9])
    rden = put("rden", [P, 9])
    stT = put("stT", [P, PAIRS, 32])
    stcol = put("stcol", [P, PAIRS, 36])
    prm_it = put("prm_it", [P, 8])
    bd = put("bd", [P, 2, P])
    xp = put("xp", [P, SEQ + CW - 1])
    xps = put("xps", [P, DEC_B, DEC_T + CW - 1])
    xc = put("xc", [P, EXT])
    th = put("th", [P, EXT])
    ti = put("ti", [P, EXT])
    dd = put("dd", [P, EXT])
    aa = put("aa", [P, EXT])
    sq = put("sq", [P, EXT])
    gb = put("gb", [P, T])
    gp = put("gp", [P, T])
    st_out = put("st_out", [36, DR], where=[lgt_at])
    w = [big_at]
    x_tok = put("x_tok", [P, TT + 1, D], where=w)
    x_sq = put("x_sq", [P, D], where=w)
    g_row = put("g_row", [P, D], where=w)
    ssum = put("ssum", [P, 8], where=w)
    rstd_x = put("rstd_x", [P, 8], where=w)
    prow = put("prow", [56, P], where=w)
    strow = put("strow", [32, DR], where=w)
    rel33 = put("rel33", [NB + 1, HEADS], where=w)
    bktab = put("bktab", [NB + 1, RELW], where=w)
    drow = put("drow", [HEADS, RELW], where=w)
    pages = put("pages", [1, DEC_B * NPG], I32, where=w)
    sp = [put(f"sp{i}", [P, 4], where=w) for i in range(6)]
    bias8_rev = put("bias8_rev", [8, PAIRS, KS], where=w)
    assert w[0] <= stage_at
    w = [stage_at]
    ma = [put(f"ma{i}", [P, T], where=w) for i in range(2)]
    mr = [put(f"mr{i}", [P, T], where=w) for i in range(2)]
    xk = [put(f"xk{i}", [P, TT + 1, P], where=w) for i in range(2)]
    hid_end = big_at + 2 * 4 * KF * T
    assert w[0] <= hid_end
    w = [hid_end]
    x1 = put("x1", [P, KD, T], where=w)
    ytok = put("ytok", [P, TT + 1, D], where=w)
    rb = [put(f"rb{i}", [P, T], where=w) for i in range(2)]
    std = put("std", [P, T], where=w)
    fg, fu, ft = (put(n, [P, T], where=w) for n in ("fg", "fu", "ft"))
    w = [big_at]
    og = put("og", [P, KD, T], where=w)
    osq = [put(f"osq{i}", [P, HT], where=w) for i in range(2)]
    xsq = [put(f"xsq{i}", [P, HT], where=w) for i in range(2)]
    oacc = [put(f"oacc{i}", [P, T], where=w) for i in range(2)]
    assert w[0] <= stage_at
    w = [big_at]
    hid_hi = put("hid_hi", [P, KF, T], F32R, where=w)
    hid_lo = put("hid_lo", [P, KF, T], F32R, where=w)
    w = [xin_at]
    x1tok = put("x1tok", [P, TT + 1, D], where=w)
    yg = [put(f"yg{i}", [P, T], where=w) for i in range(2)]
    x1s = [put(f"x1s{i}", [P, T], where=w) for i in range(2)]
    ysq = put("ysq", [P, T], where=w)
    yacc = put("yacc", [P, T], where=w)
    ycol = put("ycol", [P, 16], where=w)
    assert w[0] <= xin_at + 2 * 4 * KD * T

    with ExitStack() as ctx:
        def sem(name):
            return ctx.enter_context(nc.semaphore(name))

        ps = ctx.enter_context(nc.psum_tensor("ps", [P, 8, 512], F32))
        S_BANK, T_BANK, O_BANK, M_BANK = 4, 5, 6, 7

        w_in_slot = [sem("w_slot0"), sem("w_slot1")]
        hi_done = sem("hi_done")
        lo_done = sem("lo_done")
        tile_done = sem("tile_done")
        tile_free = [sem("tile_free0"), sem("tile_free1")]
        x_in = [sem(f"x_in{i}") for i in range(TT + 1)]
        par_in = sem("par_in")
        rel_in = sem("rel_in")
        g_in = sem("g_in")
        page_in = sem("page_in")
        bias8_in = sem("bias8_in")
        dist_out = sem("dist_out")
        consts = sem("consts")
        consts_v = sem("consts_v")
        sq_sum = sem("sq_sum")
        std_x = sem("std_x")
        rx_done = sem("rx_done")
        xs_done = sem("xs_done")
        xt_ready = sem("xt_ready")
        xt_hi = sem("xt_hi")
        xt_lo = sem("xt_lo")
        small_T = sem("small_T")
        small_c = sem("small_c")
        sp_act = sem("sp_act")
        sp_dve = sem("sp_dve")
        kc_in = sem("kc_in")
        vc_in = sem("vc_in")
        bias_in = sem("bias_in")
        bd_in = sem("bd_in")
        kv_out = sem("kv_out")
        it_ready = sem("it_ready")
        q_spread = sem("q_spread")
        s_ready = sem("s_ready")
        logits_done = sem("logits_done")
        exp_done = sem("exp_done")
        rden_done = sem("rden_done")
        probs_done = sem("probs_done")
        tp_ready = sem("tp_ready")
        tp_free = sem("tp_free")
        mi_ready = sem("mi_ready")
        mi_free = sem("mi_free")
        so_hi = sem("so_hi")
        pv_done = sem("pv_done")
        o_hi = sem("o_hi")
        o_free = sem("o_free")
        conv_step = sem("conv_step")
        th_done = sem("th_done")
        sq_done = sem("sq_done")
        gelu_step = sem("gelu_step")
        tg_done = sem("tg_done")
        rg_step = sem("rg_step")
        orn_hi = sem("orn_hi")
        rg_done = sem("rg_done")
        st_saved = sem("st_saved")
        st_ready = sem("st_ready")
        st_copied = sem("st_copied")
        st_out_s = sem("st_out_s")
        xk_in = [sem("xk_in0"), sem("xk_in1")]
        mix_free = sem("mix_free")
        mix_sum = sem("mix_sum")
        mix_hi = sem("mix_hi")
        mix_lo = sem("mix_lo")
        out_free = sem("out_free")
        osq_used = sem("osq_used")
        xT_ready = sem("xT_ready")
        xT_free = sem("xT_free")
        n_ready = sem("n_ready")
        n_std = sem("n_std")
        n_rstd = sem("n_rstd")
        t_done = sem("t_done")
        x1_done = sem("x1_done")
        f_hi = sem("f_hi")
        f_sq = sem("f_sq")
        f_lo = sem("f_lo")
        f_acc = sem("f_acc")
        gu_scaled = sem("gu_scaled")
        gu_free = sem("gu_free")
        fsil = sem("fsil")
        fprod = sem("fprod")
        hid_h = sem("hid_h")
        hid_l = sem("hid_l")
        y_free = sem("y_free")
        ysq_used = sem("ysq_used")
        acc_zero = sem("acc_zero")
        x1s_done = sem("x1s_done")
        x1t_ready = sem("x1t_ready")
        x1t_free = sem("x1t_free")
        yt_ready = sem("yt_ready")
        yt_free = sem("yt_free")
        ycol_step = sem("ycol_step")
        yn_ready = sem("yn_ready")
        z_done = sem("z_done")
        y_out = sem("y_out")

        def two(pair):
            return ps[:, 2 * pair:2 * pair + 2, 0:HT]

        def halves(buf):
            return buf.rearrange("p (h t) -> p h t", h=2)

        def bt(ap):
            return ap.rearrange("p (b t) -> p b t", b=DEC_B)

        def x_fill(dst, tt, hf, f):
            if tt < TT:
                return (dst[:, 4 * hf:4 * hf + 4, tt * P:(tt + 1) * P],
                        ps[:, 4 + f % 4, :].rearrange("p (k c) -> p k c", c=P))
            return dst[:, :, SEQ:T], ps[:, 4 + f % 4, 0:KD * TS].rearrange("p (k c) -> p k c", c=TS)

        def half_of(buf, k, h, k0=0):
            flat = buf[:, :, :].rearrange("p k t -> p (k t)")
            return flat[:, bass.ds(k * T + (k0 * T + h * HT), HT)]

        def tile_of(buf, k, k0=0):
            flat = buf[:, :, :].rearrange("p k t -> p (k t)")
            return halves(flat[:, bass.ds(k * T + k0 * T, T)])

        SP_ABS = 3
        block = ctx.enter_context(nc.Block())

        @block.sync
        def _(sp_):
            e = sp_
            wi = w_in[0].rearrange("(kt p) n -> p kt n", p=P)
            wpa = w_proj_attn[0].rearrange("(kt p) n -> p kt n", p=P)
            wpr = w_proj_rnn[0].rearrange("(kt p) n -> p kt n", p=P)
            wo = w_out[0].rearrange("(kt p) n -> p kt n", p=P)
            wgu = w_gate_up[0].rearrange("(kt p) n -> p kt n", p=P)
            wd = w_down[0].rearrange("(kt p) n -> p kt n", p=P)

            def load(i, s, src, k=KD):
                e.wait_ge(lo_done, i + 1)
                for k0, k1 in ((0, 4), (4, k)):
                    e.dma_start(w_raw[s][:, k0:k1, :], src[:, k0:k1, :]).then_inc(w_in_slot[s], 16)

            for tt in range(TT):
                e.dma_start(x_tok[:, tt, :], x_prompt[0, tt * P:(tt + 1) * P, :]).then_inc(x_in[tt], 16)
            e.dma_start(x_tok[0:TS, TT, :], x_sample.rearrange("b t d -> (b t) d")).then_inc(x_in[TT], 16)
            for i in range(2):
                load(i, i, wi[:, :, 512 * i:512 * i + P])
            e.dma_start(pages[:, :], page_table.rearrange("b n -> (b n)").rearrange("(a n) -> a n", a=1)
                        ).then_inc(page_in, 16)
            e.wait_ge(page_in, 16)
            page = [e.value_load(pages[0:1, j:j + 1], min_val=0, max_val=n_phys - 1)
                    for j in range(DEC_B * NPG)]

            def load_pages(cache, dst, done, it, part):
                for j in range(8 * part, 8 * part + 8):
                    src = cache[0].rearrange("n t h d -> n t (h d)")[bass.ds(page[j], 1), :, bass.ds(it * P, P)]
                    e.dma_start(dst[:, j, :], src.rearrange("o t c -> t (o c)")).then_inc(done, 16)

            def iteration(it, first=False, last=False):
                for j in range(TILES_IT):
                    if first and j < 2:
                        pass
                    elif j < 5:
                        load(it * TILES_IT + j, j % 2, wi[:, :, bass.ds(it * P + 512 * j, P)])
                    else:
                        load(it * TILES_IT + j, j % 2, wi[:, :, bass.ds(it * (GT_IT * P) + 2560 + (j - 5) * P, P)])
                    if j == 1:
                        e.wait_ge(consts, 12)
                        e.wait_ge(logits_done, it * 9 + 1)
                        src = AP(dist_bias.tensor, it * (2 * RELW), [[1, P], [RELW, 2], [1, SEQ]])
                        e.wait_ge(dist_out, 16)
                        e.dma_start(biasT[:, :, :], src).then_inc(bias_in, 16)
                        e.wait_ge(mi_free, it * 8 + 1)
                        for g, wrg in enumerate((rg_w_r, rg_w_i)):
                            for blk in range(2):
                                rows = slice(RGB * blk, RGB * blk + RGB)
                                e.dma_start(bd[rows, g, rows],
                                            wrg[0][bass.ds(it * 2 + blk, 1)].rearrange("o c d -> c (o d)")
                                            ).then_inc(bd_in, 16)
                    if j in (2, 3) and first:
                        load_pages(cache_v, vc, vc_in, 0, j - 2)
                    if j in (5, 6) and not last:
                        e.wait_ge(s_ready, it * 9 + 1)
                        load_pages(cache_k, kc, kc_in, it + 1, j - 5)
                e.wait_ge(mi_free, it * 8 + 4)
                for g, (op, os) in enumerate(((new_k_prompt, new_k_sample), (new_v_prompt, new_v_sample))):
                    dst = op[0, 0].rearrange("(tt p) h d -> p tt (h d)", p=P)[:, :, bass.ds(it * P, P)]
                    e.dma_start(dst, tok[:, g, 0:TT, :]).then_inc(kv_out, 16)
                    dst = os[0].rearrange("b t h d -> (b t) (h d)")[:, bass.ds(it * P, P)]
                    e.dma_start(dst, tok[0:TS, g, TT, :]).then_inc(kv_out, 16)
                if not last:
                    e.wait_ge(mi_ready, it * 8 + 4)
                    load_pages(cache_v, vc, vc_in, it + 1, 0)
                    load_pages(cache_v, vc, vc_in, it + 1, 1)

            for part in range(2):
                load_pages(cache_k, kc, kc_in, 0, part)
            iteration(0, first=True)
            with e.Fori(1, PAIRS - 1) as it:
                iteration(it)
            iteration(PAIRS - 1, last=True)
            with e.Fori(0, GT_TAIL // 2) as n:
                for s in range(2):
                    load(n * 2 + (C_TAIL + s), s, wi[:, :, bass.ds(n * (2 * P) + 2560 + (PAIRS * GT_IT + s) * P, P)])
            with e.Fori(0, KD // 2) as n:
                for s in range(2):
                    e.wait_ge(lo_done, n * 2 + (C_MIX + s + 1))
                    for k0, wp in ((0, wpa), (PAIRS, wpr)):
                        e.dma_start(w_raw[s][:, k0:k0 + PAIRS, :], wp[:, :, bass.ds(n * (2 * P) + s * P, P)]
                                    ).then_inc(w_in_slot[s], 16)
            e.wait_ge(st_copied, 1)
            e.dma_start(new_conv_prompt[0, 0], st_out[0:3, :]).then_inc(st_out_s, 16)
            e.dma_start(new_conv_sample[0].rearrange("b j d -> (b j) d"), st_out[3:27, :]).then_inc(st_out_s, 16)
            e.dma_start(new_h_prompt[0], st_out[27:28, :]).then_inc(st_out_s, 16)
            e.dma_start(new_h_sample[0], st_out[28:36, :]).then_inc(st_out_s, 16)
            with e.Fori(0, KD // 2) as n:
                for s in range(2):
                    load(n * 2 + (C_OUT + s), s, wo[:, :, bass.ds(n * (2 * P) + s * P, P)])
            with e.Fori(0, KD // 2) as n:
                for s in range(2):
                    load(n * 2 + (C_OUT + KD + s), s, wo[:, :, bass.ds(n * (2 * P) + s * P, P)])
            with e.Fori(0, KF) as m:
                for s in range(2):
                    load(m * 2 + (C_FFN + s), s, wgu[:, :, bass.ds(m * P + s * DFF, P)])

            def load_down(m, c, s):
                k0 = sum(DOWN_K[:c])
                load(m * 3 + (C_DOWN + c), s, wd[:, k0:k0 + DOWN_K[c], bass.ds(m * P, P)], DOWN_K[c])

            with e.Fori(0, KD // 2) as n:
                for m2 in range(2):
                    for c in range(3):
                        load_down(n * 2 + m2, c, (m2 * 3 + c) % 2)
            for tt in range(TT + 1):
                e.wait_ge(z_done, tt + 1)
                if tt < TT:
                    e.dma_start(y_prompt[0, tt * P:(tt + 1) * P, :], ytok[:, tt, :]).then_inc(y_out, 16)
                else:
                    e.dma_start(y_sample.rearrange("b t d -> (b t) d"), ytok[0:TS, TT, :]).then_inc(y_out, 16)
            e.wait_ge(kv_out, 64 * (PAIRS + 1))
            e.wait_ge(st_out_s, 64)
            e.wait_ge(y_out, 16 * (TT + 1))

        @block.gpsimd
        def _(e):
            e.memset(ident[:, :], 0.0).then_inc(consts, 1)
            e.wait_ge(consts, 1)
            e.affine_select(out=ident[:, :], in_=ident[:, :], compare_op=ALU.not_equal, fill=1.0,
                            base=0, pattern=[[-1, P]], channel_multiplier=1).then_inc(consts, 1)
            for src, r0, n in ((conv_w, 0, 16), (conv_b, 16, 4), (rg_b_r, 20, 4), (rg_b_i, 24, 4),
                               (rg_lambda, 28, 4), (norm_mix_post, 32, 8), (norm_ffn_pre, 40, 8), (norm_ffn_post, 48, 8)):
                e.dma_start(prow[r0:r0 + n, :], AP(src.tensor, 0, [[P, n], [1, P]])).then_inc(par_in, 16)
            e.dma_start(strow[0:24, :], state_conv[0].rearrange("b j c -> (b j) c")).then_inc(par_in, 16)
            e.dma_start(strow[24:32, :], state_h[0]).then_inc(par_in, 16)
            e.memset(rep8[:, :], 0.0).then_inc(consts, 1)
            e.wait_ge(consts, 3)
            rep = rep8[:, :].rearrange("p (b k) -> p b k", k=8)
            e.affine_select(out=rep, in_=rep, compare_op=ALU.not_equal, fill=1.0,
                            base=0, pattern=[[0, P // 8], [-1, 8]], channel_multiplier=1).then_inc(consts, 1)
            e.memset(mask_s[:, :], 0.0).then_inc(consts, 1)
            e.wait_ge(consts, 5)
            own = mask_s[:, PAST:KS].rearrange("p (b t) -> p b t", b=DEC_B)
            e.affine_select(out=own, in_=own, compare_op=ALU.is_ge, fill=NEG,
                            base=0, pattern=[[-8, DEC_B], [0, DEC_T]], channel_multiplier=1).then_inc(consts, 1)
            e.wait_ge(consts, 6)
            e.affine_select(out=own, in_=own, compare_op=ALU.is_ge, fill=NEG,
                            base=7, pattern=[[8, DEC_B], [0, DEC_T]], channel_multiplier=-1).then_inc(consts, 1)
            e.memset(q_bd[:, :], 0.0).then_inc(consts, 1)
            e.memset(q_all[:, :], 0.0).then_inc(consts, 1)
            e.memset(bd[:, :, :], 0.0).then_inc(consts, 1)
            e.memset(xp[:, 0:CW - 1], 0.0).then_inc(consts, 1)
            e.memset(xc[:, :], 0.0).then_inc(consts, 1)
            e.wait_ge(dist_out, 16)
            for h in range(2):
                rows = slice(4 * h, 4 * h + 4)
                e.dma_start(bias8_rev[rows, :, TS:KS], AP(dist_bias.tensor, h * RELW + 128, [[1, 4], [2 * RELW, PAIRS], [1, PAST]])
                            ).then_inc(bias8_in, 16)
                for b0 in range(PAIRS):
                    e.dma_start(bias8_rev[rows, b0, 0:TS].rearrange("p (b t) -> p b t", t=DEC_T),
                                AP(dist_bias.tensor, (2 * b0 + h) * RELW + 124, [[1, 4], [0, DEC_B], [1, DEC_T]])
                                ).then_inc(bias8_in, 16)
            e.wait_ge(bias8_in, 160)
            for b0 in range(PAIRS):
                e.tensor_copy(bias8[0:8, b0, :], bias8_rev[0:8, b0, ::-1]).then_inc(consts, 1)

            with e.Fori(0, PAIRS) as it:
                count = e.to_reg(it + 1)
                e.wait_ge(small_c, 6)
                e.wait_ge(rg_done, count)
                e.tensor_copy(prm_it[:, :], prm[:, 0:32].rearrange("p (c f) -> p c f", f=PAIRS)[:, :, bass.ds(it, 1)])
                e.tensor_copy(xps[:, :, 0:CW - 1],
                              stT[:, bass.ds(it, 1), 0:24].rearrange("p o (b j) -> p (o b) j", b=DEC_B)
                              ).then_inc(it_ready, 1)
                count = e.to_reg(it * 4 + 2)
                e.wait_ge(consts, 12)
                e.wait_ge(tile_free[0], count)
                e.wait_ge(it_ready, it + 1)
                for h in range(2):
                    rows = slice(DH * h, DH * h + DH)
                    src = bt(qT[rows, SEQ:T])
                    e.tensor_copy(q_all[rows, :].rearrange("p (b k) -> p b k", b=DEC_B)[:, :, 4 * h:4 * h + 4], src)
                    last = e.tensor_copy(q_bd[rows, :].rearrange("p (b k) -> p b k", b=DEC_B)[:, :, 4 * h:4 * h + 4],
                                         src)
                last.then_inc(q_spread, 1)
                count = e.to_reg(it * 4 + 3)
                e.wait_ge(consts, 12)
                e.wait_ge(tile_free[1], count)
                e.wait_ge(q_spread, it + 1)
                e.tensor_copy(stcol[:, bass.ds(it, 1), 0:3], xp[:, SEQ:SEQ + 3])
                e.tensor_copy(stcol[:, bass.ds(it, 1), 3:27].rearrange("p o (b j) -> p (o b) j", b=DEC_B),
                              xps[:, :, DEC_T:DEC_T + 3])
                e.wait_ge(tile_free[0], it * 4 + 4)
                e.tensor_tensor(gp[:, :], gb[:, :], gb[:, :], ALU.mult).then_inc(gelu_step, 1)
                count = e.to_reg(it * 3 + 1)
                e.wait_ge(consts, 12)
                e.wait_ge(gelu_step, count)
                e.tensor_scalar(gp[:, :], gp[:, :], GELU_C2, GELU_C1, ALU.mult, ALU.add).then_inc(gelu_step, 1)
                e.wait_ge(gelu_step, it * 3 + 2)
                e.tensor_tensor(gp[:, :], gp[:, :], gb[:, :], ALU.mult).then_inc(gelu_step, 1)
                count = e.to_reg(it * 12 + 9)
                e.wait_ge(small_c, 6)
                e.wait_ge(rg_step, count)
                e.tensor_copy(stcol[:, bass.ds(it, 1), 27:28], sq[:, SEQ - 1:SEQ])
                e.tensor_copy(stcol[:, bass.ds(it, 1), 28:36],
                              sq[:, SEQ:EXT].rearrange("p (b k) -> p b k", b=DEC_B)[:, :, DEC_T]
                              ).then_inc(st_saved, 1)
            xpt = x_prompt[0].rearrange("(tt p) d -> p tt d", p=P)
            xst = x_sample.rearrange("b t d -> (b t) d")
            e.wait_ge(tile_done, C_MIX + 3)
            e.wait_ge(kv_out, 64 * (PAIRS + 1))
            with e.Fori(0, KD // 2) as n:
                for s in range(2):
                    count = e.to_reg(n * 2 + (s + 1))
                    e.wait_ge(st_copied, 1)
                    e.wait_ge(xT_free, count)
                    cols = bass.ds(n * (2 * P) + s * P, P)
                    e.dma_start(xk[s][:, 0:TT, :], xpt[:, :, cols]).then_inc(xk_in[s], 16)
                    e.dma_start(xk[s][0:TS, TT, :], xst[:, cols]).then_inc(xk_in[s], 16)
            e.wait_ge(n_ready, 1)
            for h in range(2):
                acc = oacc[1][:, h * HT:h * HT + HT]
                for k in range(KD):
                    j = KD * h + k
                    e.wait_ge(f_sq, j + 1)
                    if k >= 1:
                        e.wait_ge(f_acc, j + 2)
                        e.tensor_tensor(acc, acc, xsq[j % 2][:, :], ALU.add).then_inc(f_acc, 1)
                    else:
                        e.tensor_copy(acc, xsq[j % 2][:, :]).then_inc(f_acc, 1)
            with e.Fori(0, KD // 2) as n:
                for s in range(2):
                    count = e.to_reg(n * 2 + (s + 1))
                    e.wait_ge(tile_done, C_DOWN + 2)
                    e.wait_ge(x1t_free, count)
                    e.tensor_copy(x1s[s][:, :], x1[:, bass.ds(n * 2 + s, 1), :]).then_inc(x1s_done, 1)

        @block.tensor
        def _(e):
            def steps(s, bank, xh, xl, ks, first, last, ready=None, base=1, hs=(0, 1)):
                for kw, kx in ks:
                    if ready is not None:
                        e.wait_ge(ready, kx + base)
                    for wt, xt in ((w_hi, xh), (w_hi, xl), (w_lo, xh)):
                        for h in hs:
                            mm = e.matmul(ps[:, bank + h, 0:HT], wt[s][:, kw, :], xt[:, kx, h * HT:h * HT + HT],
                                          start=first and wt is w_hi and xt is xh,
                                          stop=last and (kw, kx) == ks[-1] and wt is w_lo)
                    first = False
                return mm

            def split_ready(i):
                e.wait_ge(lo_done, i + 3)

            e.wait_ge(consts, 2)

            def x_T(tt):
                e.wait_ge(xs_done, tt + 1)
                rows = P if tt < TT else TS
                for hf in range(2 if tt < TT else 1):
                    f = 2 * tt + hf
                    if f >= 4:
                        e.wait_ge(xt_lo, f - 3)
                    kts = range(4 * hf, 4 * hf + 4) if tt < TT else range(KD)
                    for n, kt in enumerate(kts):
                        mm = e.transpose(ps[:, 4 + f % 4, n * rows:(n + 1) * rows],
                                         x_tok[0:rows, tt, kt * P:kt * P + P], ident[0:rows, 0:rows])
                    mm.then_inc(xt_ready, 1)

            x_T(0)
            x_T(1)
            x_T(2)
            e.wait_ge(par_in, 160)
            e.transpose(ps[:, 0, 0:56], prow[:, :], ident[0:56, 0:56]).then_inc(small_T, 1)
            for f in range(PAIRS):
                mm = e.transpose(ps[:, 1, 32 * f:32 * f + 32], strow[:, f * P:f * P + P], ident[0:32, 0:32])
            mm.then_inc(small_T, 1)
            e.wait_ge(rel_in, 32)
            e.matmul(ps[0:HEADS, 2, 0:512], rel33[:, :], bktab[:, 0:512], start=True, stop=True)
            e.matmul(ps[0:HEADS, 3, 0:RELW - 512], rel33[:, :], bktab[:, 512:RELW], start=True,
                     stop=True).then_inc(small_T, 1)
            for tt in range(3, TT + 1):
                x_T(tt)
            e.wait_ge(small_c, 4)
            e.wait_ge(xt_lo, 9)

            with e.Fori(0, PAIRS) as it:
                i0 = it * TILES_IT

                def begin(j):
                    split_ready(i0 + j)
                    e.wait_ge(tile_free[j % 2], it * 4 + (j // 2 + 1))

                def part(j, k0, k1):
                    mm = steps(j % 2, 2 * (j % 2), xin_hi, xin_lo, [(k, k) for k in range(k0, k1)], k0 == 0, k1 == KD)
                    if k1 == KD:
                        mm.then_inc(tile_done, 1)

                def tp_wait(use):
                    e.wait_ge(tp_free, it * 13 + (use + 1))

                def mi_wait(use):
                    e.wait_ge(mi_free, it * 8 + (use + 1))

                def cache_T(f):
                    if f == 0:
                        e.wait_ge(kc_in, it * 256 + 256)
                    tp_wait(f)
                    for n in range(4):
                        mm = e.transpose(ps[:, T_BANK, n * P:n * P + P], kc[:, 4 * f + n, :], ident[:, :])
                    mm.then_inc(tp_ready, 1)

                def scores_s():
                    e.wait_ge(q_spread, it + 1)
                    e.wait_ge(consts, 16)
                    e.wait_ge(tile_free[1], it * 4 + 2)
                    tp_wait(4)
                    e.wait_ge(logits_done, it * 9 + 1)
                    e.matmul(ps[:, S_BANK, 0:KS], rep8[0:8, :], bias8[0:8, :, :].rearrange("p f k -> p (f k)")[:, bass.ds(it * KS, KS)], start=True, stop=False,
                             skip_group_check=True)
                    for b in range(DEC_B):
                        e.matmul(ps[0:ROWS_S, S_BANK, 0:PAST], q_bd[:, ROWS_S * b:ROWS_S * b + ROWS_S], kcT[:, b, :],
                                 start=False, stop=False, skip_group_check=True)
                    e.matmul(ps[0:ROWS_S, S_BANK, PAST:KS], q_all[:, :], kT[:, SEQ:T], start=False, stop=True,
                             skip_group_check=True).then_inc(s_ready, 1)

                def scores(u):
                    h, qt = u // TT, u % TT
                    rows = slice(DH * h, DH * h + DH)
                    e.wait_ge(logits_done, it * 9 + (u + 2))
                    e.matmul(ps[:, S_BANK, 0:(qt + 1) * P], qT[rows, qt * P:(qt + 1) * P], kT[rows, 0:(qt + 1) * P],
                             start=True, stop=True).then_inc(s_ready, 1)

                def probs_T(u):
                    e.wait_ge(probs_done, it * 9 + (u + 2))
                    tp_wait(5 + u)
                    for kt in range(u % TT + 1):
                        mm = e.transpose(ps[:, T_BANK, kt * P:kt * P + P], lgt[:, u % 2, kt * P:kt * P + P], ident[:, :])
                    mm.then_inc(tp_ready, 1)

                def probs_T_s():
                    e.wait_ge(consts, 2)
                    e.wait_ge(probs_done, it * 9 + 1)
                    tp_wait(4)
                    for n in range(NPG):
                        e.transpose(ps[:, T_BANK, n * ROWS_S:(n + 1) * ROWS_S], lgt_s[0:ROWS_S, n * P:n * P + P],
                                    ident[0:ROWS_S, 0:ROWS_S])
                    e.transpose(ps[0:TS, T_BANK, NPG * ROWS_S:(NPG + 1) * ROWS_S], lgt_s[0:ROWS_S, PAST:KS],
                                ident[0:ROWS_S, 0:ROWS_S]).then_inc(tp_ready, 1)

                def values(u):
                    h, qt = u // TT, u % TT
                    if u == 0:
                        e.wait_ge(o_free, it + 1)
                    e.wait_ge(tp_free, it * 13 + (5 + u + 2))
                    for kt in range(qt + 1):
                        mm = e.matmul(ps[DH * h:DH * h + DH, O_BANK, qt * P:(qt + 1) * P],
                                      tok[:, 1, kt, DH * h:DH * h + DH], prT[:, u % 2, kt * P:kt * P + P],
                                      start=kt == 0, stop=kt == qt)
                    if u == 2 * TT - 1:
                        mm.then_inc(pv_done, 1)

                def values_s():
                    e.wait_ge(vc_in, it * 256 + 256)
                    mi_wait(3)
                    e.matmul(ps[:, M_BANK, 0:ROWS_S], tok[0:TS, 1, TT, :], prT_s[0:TS, 2, :], start=True, stop=False,
                             skip_group_check=True)
                    for b in range(DEC_B):
                        for n in range(NPG):
                            mm = e.matmul(ps[:, M_BANK, 8 * b:8 * b + 8], vc[:, NPG * b + n, :],
                                          prT_s[:, n, 8 * b:8 * b + 8], start=False, stop=b == DEC_B - 1 and n == NPG - 1,
                                          skip_group_check=True)
                    mm.then_inc(mi_ready, 1)

                def tok_prompt(use, src, free, n_free):
                    e.wait_ge(tile_free[free], it * 4 + n_free)
                    mi_wait(use)
                    for tt in range(TT):
                        mm = e.transpose(ps[:, M_BANK, tt * P:tt * P + P], src[:, tt * P:tt * P + P], ident[:, :])
                    mm.then_inc(mi_ready, 1)

                def tok_sample():
                    mi_wait(1)
                    e.transpose(ps[0:TS, M_BANK, 0:P], kT[:, SEQ:T], ident[:, :])
                    e.transpose(ps[0:TS, M_BANK, P:2 * P], vT[:, SEQ:T], ident[:, :]).then_inc(mi_ready, 1)

                def rg(g, h):
                    if g == 0 and h == 0:
                        e.wait_ge(conv_step, it * 8 + 8)
                        e.wait_ge(bd_in, it * 64 + 64)
                    mi_wait(4 + 2 * g + h)
                    e.matmul(ps[:, M_BANK, 0:EH], bd[:, g, :], xc[:, EH * h:EH * h + EH], start=True,
                             stop=True).then_inc(mi_ready, 1)

                begin(0); part(0, 0, 4); cache_T(0); part(0, 4, 8)
                begin(1); cache_T(1); part(1, 0, 4); cache_T(2); part(1, 4, 8)
                begin(2); cache_T(3); part(2, 0, 5); scores_s(); part(2, 5, 8)
                begin(3); scores(0); part(3, 0, 2); probs_T_s(); part(3, 2, 4)
                tok_prompt(0, vT, 0, 3); probs_T(0); scores(1); part(3, 4, 6); tok_sample(); part(3, 6, 8)
                begin(4); tok_prompt(2, kT, 1, 2); values(0); probs_T(1); scores(2); part(4, 0, 4)
                values_s(); values(1); probs_T(2); scores(3); part(4, 4, 8)
                begin(5); values(2); probs_T(3); scores(4); part(5, 0, 2); rg(0, 0); part(5, 2, 4)
                values(3); probs_T(4); scores(5); rg(0, 1); part(5, 4, 6); rg(1, 0); part(5, 6, 8)
                begin(6); values(4); probs_T(5); scores(6); rg(1, 1); part(6, 0, 4)
                values(5); probs_T(6); scores(7); part(6, 4, 8)
                begin(7); values(6); probs_T(7); part(7, 0, 4); values(7); part(7, 4, 8)

            with e.Fori(0, GT_TAIL // 2) as n:
                for s in range(2):
                    split_ready(n * 2 + (C_TAIL + s))
                    e.wait_ge(tile_free[s], n + (4 * PAIRS + 1))
                    steps(s, 2 * s, xin_hi, xin_lo, [(k, k) for k in range(KD)], True, True).then_inc(tile_done, 1)
            e.wait_ge(st_saved, PAIRS)
            e.wait_ge(mi_free, 8 * PAIRS + 1)
            for f in range(PAIRS):
                mm = e.transpose(ps[0:36, M_BANK, f * P:f * P + P], stcol[:, f, :], ident[:, :])
            mm.then_inc(st_ready, 1)

            e.wait_ge(o_free, PAIRS + 1)
            e.wait_ge(rg_done, PAIRS + 1)
            e.wait_ge(logits_done, 9 * PAIRS + 1)
            e.wait_ge(tp_free, 13 * PAIRS + 1)
            e.wait_ge(st_copied, 1)
            for s in range(2):
                e.wait_ge(tile_free[s], 4 * PAIRS + GT_TAIL // 2 + 1)
            with e.Fori(0, KD // 2) as n:
                for s in range(2):
                    split_ready(n * 2 + (C_MIX + s))
                    e.wait_ge(mix_free, n * 2 + (s + 1))
                    steps(s, 4 * s, ocat_hi, ocat_lo, [(k, k) for k in range(PAIRS)], True, True)
                    steps(s, 4 * s + 2, ocat_hi, ocat_lo, [(k, k) for k in range(PAIRS, 2 * PAIRS)], True, True
                          ).then_inc(tile_done, 1)

            KS_D = [(k, k) for k in range(KD)]

            def out_tile(m, s, h, ready=None):
                split_ready(m + (C_OUT + KD * h))
                e.wait_ge(out_free, m + (KD * h + 1))
                steps(s, s - h, xin_hi, xin_lo, KS_D, True, True, ready=ready, hs=(h,)).then_inc(tile_done, 1)

            def sum_squares(acc, bank, hs):
                for h in hs:
                    mm = e.matmul(ps[:, bank + h, 0:HT], ones[:, :], acc[:, h * HT:h * HT + HT], start=True, stop=True)
                mm.then_inc(n_ready, 1)

            e.wait_ge(mix_free, KD + 1)
            with e.Fori(0, KD // 2) as n:
                for s in range(2):
                    out_tile(n * 2 + s, s, 0, ready=mix_lo)
                    e.wait_ge(mix_free, KD + 2)
                    e.wait_ge(xT_free, n * 2 + (s + 1))
                    e.wait_ge(xk_in[s], n * 32 + 32)
                    for tt in range(TT):
                        e.transpose(ps[:, 4 + 2 * s, tt * P:tt * P + P], xk[s][:, tt, :], ident[:, :])
                    e.transpose(ps[:, 5 + 2 * s, 0:TS], xk[s][0:TS, TT, :], ident[0:TS, 0:TS]).then_inc(xT_ready, 1)
            out_tile(0, 0, 1)
            e.wait_ge(osq_used, KD + 2)
            sum_squares(oacc[0], 2, (0,))
            out_tile(1, 1, 1)
            with e.Fori(0, KD // 2 - 1) as n:
                for s in range(2):
                    out_tile(n * 2 + (s + 2), s, 1)

            split_ready(C_FFN)
            e.wait_ge(out_free, 2 * KD + 1)
            steps(0, 0, xin_hi, xin_lo, KS_D[:2], True, False, ready=f_lo, hs=(0,))
            e.wait_ge(osq_used, 2 * KD + 2)
            sum_squares(oacc[0], 2, (1,))
            steps(0, 0, xin_hi, xin_lo, KS_D[2:], False, True, ready=f_lo, hs=(0,))
            split_ready(C_FFN + 1)
            e.wait_ge(n_std, 1)
            steps(1, 2, xin_hi, xin_lo, KS_D, True, True, hs=(0,))
            e.wait_ge(out_free, 2 * KD + 2)
            e.wait_ge(n_std, 2)
            for k in KS_D:
                for c in range(2):
                    mm = steps(c, 2 * c, xin_hi, xin_lo, [k], k[0] == 0, k[0] == KD - 1, ready=f_lo, base=KD + 1, hs=(1,))
                    if k[0] == KD - 1:
                        mm.then_inc(tile_done, 1)
            e.wait_ge(xT_free, KD + 2)
            e.wait_ge(f_acc, 2 * KD + 2)
            sum_squares(oacc[1], 6, (0, 1))
            for c in range(2):
                split_ready(C_FFN + 2 + c)
                if c == 1:
                    e.wait_ge(n_std, 3)
                steps(c, 4 + 2 * c, xin_hi, xin_lo, KS_D, True, True).then_inc(tile_done, 1)
            with e.Fori(1, KF // 2) as n:
                for s in range(2):
                    e.wait_ge(gu_free, n * 2 + (s + 1))
                    for c in range(2):
                        split_ready(n * 4 + (C_FFN + 2 * s + c))
                        steps(c, 4 * s + 2 * c, xin_hi, xin_lo, KS_D, True, True).then_inc(tile_done, 1)

            def down(m, odd, between=None):
                for c in range(3):
                    split_ready(m * 3 + (C_DOWN + c))
                    if c == 0:
                        e.wait_ge(y_free, m + 1)
                    k0 = sum(DOWN_K[:c])
                    steps((odd + c) % 2, 2 * odd, hid_hi, hid_lo, [(k, k0 + k) for k in range(DOWN_K[c])],
                          c == 0, c == 2, ready=hid_l).then_inc(tile_done, 1)
                    if c == 0 and between is not None:
                        x1_T(between, 1 - odd)
                        y_T(between, 1 - odd)

            def x1_T(m, s):
                e.wait_ge(x1s_done, m + 1)
                e.wait_ge(x1t_free, m + 2)
                for tt in range(TT):
                    e.transpose(ps[:, 4, tt * P:tt * P + P], x1s[s][:, tt * P:tt * P + P], ident[:, :])
                e.transpose(ps[0:TS, 5, 0:P], x1s[s][:, SEQ:T], ident[:, :]).then_inc(x1t_ready, 1)

            def y_T(m, s):
                e.wait_ge(y_free, m + 3)
                e.wait_ge(yt_free, m + 1)
                for tt in range(TT):
                    e.transpose(ps[:, 6, tt * P:tt * P + P], yg[s][:, tt * P:tt * P + P], ident[:, :])
                e.transpose(ps[0:TS, 7, 0:P], yg[s][:, SEQ:T], ident[:, :]).then_inc(yt_ready, 1)

            e.wait_ge(gu_free, KF + 1)
            down(0, 0)
            e.wait_ge(gu_free, KF + 2)
            with e.Fori(0, (KD - 2) // 2) as n:
                down(n * 2 + 1, 1, n * 2)
                down(n * 2 + 2, 0, n * 2 + 1)
            down(KD - 1, 1, KD - 2)
            x1_T(KD - 1, 1)
            y_T(KD - 1, 1)
            e.wait_ge(ysq_used, KD + 1)
            for tt in range(TT + 1):
                rows = P if tt < TT else TS
                mm = e.matmul(ps[0:rows, 0, tt:tt + 1], yacc[:, tt * P:tt * P + rows], ones[:, 0:1],
                              start=True, stop=True)
            mm.then_inc(yn_ready, 1)

        @block.scalar
        def _(e):
            def hi(i, i2, s, k=KD):
                e.wait_ge(w_in_slot[s], i2 * 32 + 32)
                e.wait_ge(tile_done, i + 1)
                e.activation(w_hi[s][:, 0:k, :], w_raw[s][:, 0:k, :], ACT.Copy).then_inc(hi_done, 1)

            e.dma_start(g_row[:, :], AP(norm_mix_pre.tensor, 0, [[0, P], [1, D]])).then_inc(g_in, 16)
            e.dma_start(bktab[:, :], bucket_of).then_inc(rel_in, 16)
            e.wait_ge(sp_dve, 1)
            e.dma_start(rel33[0:NB, :], rel_bias).then_inc(rel_in, 16)
            e.wait_ge(consts_v, 3)
            e.activation(ycol[:, 0:1], eps_col[:, :], ACT.Sqrt)

            def x_rms(tt):
                rows = P if tt < TT else TS
                e.wait_ge(x_in[tt], 16)
                e.activation(x_sq[0:rows, :], x_tok[0:rows, tt, :], ACT.Square,
                             accum_out=ssum[0:rows, tt:tt + 1]).then_inc(sq_sum, 1)
                e.wait_ge(sq_sum, tt + 1)
                e.activation(rstd_x[0:rows, tt:tt + 1], ssum[0:rows, tt:tt + 1], ACT.Sqrt,
                             bias=eps_col[0:rows, :], scale=1.0 / D).then_inc(std_x, 1)

            def x_hi(tt):
                for hf in range(2 if tt < TT else 1):
                    f = 2 * tt + hf
                    e.wait_ge(xt_ready, f + 1)
                    dst, src = x_fill(xin_hi, tt, hf, f)
                    e.activation(dst, src, ACT.Copy).then_inc(xt_hi, 1)

            x_rms(0); x_rms(1); x_rms(2); x_hi(0)
            x_rms(3); x_hi(1); x_rms(4)
            hi(0, 0, 0)
            x_hi(2)
            e.wait_ge(sp_dve, SP_ABS)
            e.activation(sp[2][:, :], sp[1][:, :], ACT.Exp, scale=-1.0).then_inc(sp_act, 1)
            e.wait_ge(small_c, 4)
            e.dma_start(dist_bias, drow[:, :]).then_inc(dist_out, 16)
            x_hi(3); x_hi(4)

            with e.Fori(0, PAIRS) as it:
                def next_hi(j):
                    hi(it * TILES_IT + (j + 1), it * 4 + (j + 1) // 2, (j + 1) % 2)

                def done(j):
                    e.wait_ge(tile_done, it * TILES_IT + (j + 3))

                def gate(j):
                    done(j)
                    dst = gates[:, :, :].rearrange("p k t -> p (k t)")[:, bass.ds(it * (GT_IT * T) + (j - 5) * T, T)]
                    e.activation(halves(dst), two(j % 2), ACT.Tanh, scale=0.5).then_inc(tile_free[j % 2], 1)

                def cache_copy(f):
                    e.wait_ge(tp_ready, it * 13 + (f + 1))
                    e.activation(kcT[:, 2 * f:2 * f + 2, :], ps[:, T_BANK, :].rearrange("p (b k) -> p b k", b=2),
                                 ACT.Copy).then_inc(tp_free, 1)

                def exp_s():
                    e.wait_ge(logits_done, it * 9 + 2)
                    e.activation(lgt_s[0:ROWS_S, :], lgt_s[0:ROWS_S, :], ACT.Exp, bias=nmax[0:ROWS_S, 0:1], scale=-1.0,
                                 accum_out=den[0:ROWS_S, 0:1]).then_inc(exp_done, 1)

                def exp(u):
                    n = (u % TT + 1) * P
                    e.wait_ge(logits_done, it * 9 + (u + 3))
                    e.activation(lgt[:, u % 2, 0:n], lgt[:, u % 2, 0:n], ACT.Exp, bias=nmax[:, u + 1:u + 2], scale=-1.0,
                                 accum_out=den[:, u + 1:u + 2]).then_inc(exp_done, 1)

                def probs_copy(u):
                    n = (u % TT + 1) * P
                    e.wait_ge(tp_ready, it * 13 + (5 + u + 1))
                    e.activation(prT[:, u % 2, 0:n], ps[:, T_BANK, 0:n], ACT.Copy).then_inc(tp_free, 1)

                def rg_gate(use, dst):
                    g, h = (use - 4) // 2, use % 2
                    e.wait_ge(mi_ready, it * 8 + (use + 1))
                    e.activation(dst[:, EH * h:EH * h + EH], ps[:, M_BANK, 0:EH], ACT.Tanh, bias=prm_it[:, 5 + g:6 + g],
                                 scale=0.5).then_inc(mi_free, 1)

                next_hi(0); cache_copy(0)
                next_hi(1)
                done(0)
                e.activation(halves(qT[:, :]), two(0), ACT.Copy, scale=DH ** -0.5).then_inc(tile_free[0], 1)
                cache_copy(2)
                next_hi(2)
                exp_s()
                next_hi(3)
                done(2)
                e.activation(halves(vT[:, :]), two(0), ACT.Copy).then_inc(tile_free[0], 1)
                e.wait_ge(tp_ready, it * 13 + 5)
                e.activation(prT_s[:, 0:NPG, :], ps[:, T_BANK, 0:NPG * ROWS_S].rearrange("p (n r) -> p n r", n=NPG), ACT.Copy)
                e.activation(prT_s[0:TS, NPG, :], ps[0:TS, T_BANK, NPG * ROWS_S:(NPG + 1) * ROWS_S],
                             ACT.Copy).then_inc(tp_free, 1)
                exp(0); probs_copy(0); exp(1)
                next_hi(4)
                e.wait_ge(mi_ready, it * 8 + 3)
                e.activation(tok[:, 0, 0:TT, :], ps[:, M_BANK, :].rearrange("p (tt c) -> p tt c", c=P), ACT.Copy
                             ).then_inc(mi_free, 1)
                probs_copy(1); exp(2)
                probs_copy(2); exp(3)
                e.wait_ge(mi_ready, it * 8 + 4)
                for h in range(2):
                    rows = slice(DH * h, DH * h + DH)
                    last = e.activation(bt(ocat_hi[rows, :, :].rearrange("p k t -> p (k t)")[:, bass.ds(it * T + SEQ, TS)]),
                                        ps[rows, M_BANK, 0:ROWS_S].rearrange("p (b h t) -> p b h t", h=2, t=DEC_T)[:, :, h, :],
                                        ACT.Copy)
                last.then_inc(so_hi, 1)
                next_hi(5)
                done(4)
                e.activation(halves(gb[:, :]), two(0), ACT.Copy).then_inc(tile_free[0], 1)
                probs_copy(3); exp(4)
                rg_gate(4, th)
                probs_copy(4); exp(5)
                rg_gate(5, th)
                rg_gate(6, ti)
                next_hi(6)
                rg_gate(7, ti)
                gate(5)
                e.activation(th[:, :], th[:, :], ACT.Tanh, bias=prm_it[:, 7:8], scale=prm_it[:, 7:8]).then_inc(th_done, 1)
                probs_copy(5); exp(6)
                e.wait_ge(gelu_step, it * 3 + 3)
                e.activation(gp[:, :], gp[:, :], ACT.Tanh).then_inc(tg_done, 1)
                probs_copy(6); exp(7)
                next_hi(7)
                gate(6)
                probs_copy(7)
                e.wait_ge(th_done, it + 1)
                e.activation(sq[:, :], th[:, :], ACT.Sqrt, bias=tiny_col[:, :]).then_inc(sq_done, 1)
                e.wait_ge(pv_done, it + 1)
                e.activation(ocat_hi[:, bass.ds(it, 1), 0:SEQ], ps[:, O_BANK, :], ACT.Copy).then_inc(o_hi, 1)
                gate(7)
                e.wait_ge(rg_step, it * 12 + 12)
                e.activation(ocat_hi[:, bass.ds(it + PAIRS, 1), :], dd[:, 0:T], ACT.Copy).then_inc(orn_hi, 1)

            with e.Fori(0, GT_TAIL // 2) as n:
                for s in range(2):
                    i = n * 2 + (C_TAIL + s)
                    hi(i + 1, n + (C_TAIL + s + 1) // 2, 1 - s)
                    e.wait_ge(tile_done, i + 3)
                    dst = gates[:, :, :].rearrange("p k t -> p (k t)")[:, bass.ds(n * (2 * T) + (PAIRS * GT_IT + s) * T, T)]
                    e.activation(halves(dst), two(s), ACT.Tanh, scale=0.5).then_inc(tile_free[s], 1)

            with e.Fori(0, KD // 2) as n:
                for s in range(2):
                    hi(n * 2 + (C_MIX + s + 1), n + (C_MIX + s + 1) // 2, 1 - s)
                    e.wait_ge(mix_sum, n * 2 + (s + 1))
                    e.activation(tile_of(xin_hi, n * 2, s), halves(ma[s][:, :]), ACT.Copy, scale=0.5).then_inc(mix_hi, 1)

            def out_evacuate(m, s, h):
                i = m + (C_OUT + KD * h)
                e.wait_ge(tile_done, i + 3)
                e.activation(half_of(og, m, h), ps[:, s, 0:HT], ACT.Identity, scale=prm[:, bass.ds(m + 32, 1)])
                e.wait_ge(osq_used, m + (KD * h + 1))
                e.activation(osq[s][:, :], ps[:, s, 0:HT], ACT.Square).then_inc(out_free, 1)

            def out_hi(n, s, h):
                hi(n * 2 + (C_OUT + KD * h + s + 2), n + (C_OUT + KD * h + 2) // 2, s)

            def rms(n, out, src):
                e.wait_ge(n_ready, n)
                if n == 3:
                    e.wait_ge(n_rstd, 2)
                e.activation(out, src, ACT.Sqrt, bias=eps_col[:, :], scale=1.0 / D).then_inc(n_std, 1)

            def x1_high(k, j, slot, h):
                e.wait_ge(x1_done, j + 1)
                e.wait_ge(f_acc, j + 1)
                e.activation(half_of(xin_hi, k, h), half_of(x1, k, h), ACT.Identity, scale=prm[:, bass.ds(k + 40, 1)]
                             ).then_inc(f_hi, 1)
                e.activation(xsq[slot][:, :], half_of(x1, k, h), ACT.Square).then_inc(f_sq, 1)

            hi(C_OUT + 1, (C_OUT + 1) // 2, 1)
            with e.Fori(0, KD // 2) as n:
                for s in range(2):
                    out_hi(n, s, 0)
                    out_evacuate(n * 2 + s, s, 0)
            out_hi(0, 0, 1)
            out_evacuate(0, 0, 1)
            rms(1, std[:, 0:HT], ps[:, 2, 0:HT])
            out_hi(0, 1, 1)
            out_evacuate(1, 1, 1)
            with e.Fori(0, KD // 2 - 1) as n:
                for s in range(2):
                    out_hi(n + 1, s, 1)
                    out_evacuate(n * 2 + (s + 2), s, 1)
                    x1_high(n * 2 + s, n * 2 + s, s, 0)
            x1_high(KD - 2, KD - 2, 0, 0)
            rms(2, std[:, HT:T], ps[:, 3, 0:HT])
            x1_high(KD - 1, KD - 1, 1, 0)
            for k in range(KD):
                x1_high(k, KD + k, k % 2, 1)

            def ffn_hi(m, c):
                hi(m * 2 + (C_FFN + 2 + c), m + (C_FFN + 2) // 2, c)

            def ffn_tanh(m):
                e.wait_ge(gu_scaled, m + 1)
                e.activation(ft[:, :], fg[:, :], ACT.Tanh, scale=0.5).then_inc(fsil, 1)

            def ffn_high(m):
                e.wait_ge(fprod, m * 2 + 2)
                e.activation(tile_of(hid_hi, m), halves(fg[:, :]), ACT.Copy, scale=0.5).then_inc(hid_h, 1)

            ffn_hi(0, 0)
            ffn_hi(0, 1)
            rms(3, halves(std[:, :]), two(3))
            ffn_tanh(0)
            ffn_high(0)
            with e.Fori(1, KF) as m:
                ffn_hi(m, 0)
                ffn_tanh(m)
                ffn_hi(m, 1)
                ffn_high(m)

            def down_hi(n, odd, c):
                q = 3 * odd + c + 2
                hi(n * 6 + (C_DOWN + q), n * 3 + (C_DOWN + q) // 2, q % 2, DOWN_K[(c + 2) % 3])

            def y_evacuate(m, s):
                e.wait_ge(tile_done, m * 3 + (C_DOWN + 5))
                e.activation(halves(yg[s][:, :]), two(s), ACT.Identity, scale=prm[:, bass.ds(m + 48, 1)])
                e.wait_ge(ysq_used, m + 1)
                e.activation(halves(ysq[:, :]), two(s), ACT.Square).then_inc(y_free, 1)

            def y_copy(m):
                e.wait_ge(yt_ready, m + 1)
                e.activation(ytok[:, 0:TT, bass.ds(m * P, P)], ps[:, 6, :].rearrange("p (tt c) -> p tt c", c=P), ACT.Copy)
                e.activation(ytok[0:TS, TT, bass.ds(m * P, P)], ps[0:TS, 7, 0:P], ACT.Copy).then_inc(yt_free, 1)

            def y_tile(n, odd, copy=True):
                m = n * 2 + odd
                down_hi(n, odd, 0)
                if copy:
                    y_copy(m - 1)
                down_hi(n, odd, 1)
                down_hi(n, odd, 2)
                y_evacuate(m, odd)

            y_tile(0, 0, copy=False)
            with e.Fori(0, (KD - 2) // 2) as n:
                y_tile(n, 1)
                y_tile(n + 1, 0)
            hi(C_DOWN + 3 * KD - 1, (C_DOWN + 3 * KD - 1) // 2, (C_DOWN + 3 * KD - 1) % 2, DOWN_K[2])
            y_copy(KD - 2)
            y_evacuate(KD - 1, 1)
            y_copy(KD - 1)
            e.wait_ge(yn_ready, 1)
            e.activation(ycol[:, 0:TT], ps[:, 0, 0:TT], ACT.Sqrt, bias=eps_col[:, :], scale=1.0 / D)
            e.activation(ycol[0:TS, TT:TT + 1], ps[0:TS, 0, TT:TT + 1], ACT.Sqrt, bias=eps_col[0:TS, :], scale=1.0 / D
                         ).then_inc(ycol_step, 1)

        @block.vector
        def _(e):
            for sem_, n in ((lo_done, 2), (tile_done, 2), (tile_free[0], 1), (tile_free[1], 1), (logits_done, 1),
                            (tp_free, 1), (mi_free, 1), (o_free, 1), (rg_done, 1), (kv_out, 64), (mix_free, 2),
                            (out_free, 2), (osq_used, 2), (xT_free, 2), (gu_free, 2), (y_free, 2), (ysq_used, 1),
                            (x1t_free, 2), (yt_free, 1), (f_acc, 2)):
                e.sem_inc(sem_, n)

            def lo(i, s, k=KD):
                e.wait_ge(hi_done, i + 1)
                e.tensor_tensor(w_lo[s][:, 0:k, :], w_raw[s][:, 0:k, :], w_hi[s][:, 0:k, :].bitcast(F32), ALU.subtract
                                ).then_inc(lo_done, 1)

            e.memset(rel33[:, :], NEG).then_inc(sp_dve, 1)
            e.memset(ones[:, :], 1.0).then_inc(consts_v, 1)
            e.memset(eps_col[:, :], EPS).then_inc(consts_v, 1)
            e.memset(tiny_col[:, :], 1.0e-30).then_inc(consts_v, 1)
            e.wait_ge(g_in, 16)

            def x_norm(tt):
                rows = slice(0, P if tt < TT else TS)
                e.wait_ge(std_x, tt + 1)
                e.reciprocal(rstd_x[rows, tt:tt + 1], rstd_x[rows, tt:tt + 1]).then_inc(rx_done, 1)
                e.wait_ge(rx_done, tt + 1)
                e.scalar_tensor_tensor(x_tok[rows, tt, :], x_tok[rows, tt, :], rstd_x[rows, tt:tt + 1], g_row[rows, :],
                                       ALU.mult, ALU.mult).then_inc(xs_done, 1)

            def x_lo(tt):
                for hf in range(2 if tt < TT else 1):
                    f = 2 * tt + hf
                    e.wait_ge(xt_hi, f + 1)
                    dst, src = x_fill(xin_lo, tt, hf, f)
                    e.tensor_tensor(dst, src, x_fill(xin_hi, tt, hf, f)[0].bitcast(F32), ALU.subtract).then_inc(xt_lo, 1)

            x_norm(0)
            x_norm(1)
            x_lo(0)
            x_norm(2)
            x_lo(1)
            x_norm(3)
            e.wait_ge(small_T, 3)
            e.tensor_copy(drow[:, 0:512], ps[0:HEADS, 2, 0:512]).then_inc(small_c, 1)
            e.tensor_copy(drow[:, 512:RELW], ps[0:HEADS, 3, 0:RELW - 512]).then_inc(small_c, 1)
            e.tensor_copy(prm[:, :], ps[:, 0, 0:56]).then_inc(small_c, 1)
            e.tensor_copy(stT[:, :, :], ps[:, 1, 0:P].rearrange("p (f r) -> p f r", f=PAIRS)).then_inc(small_c, 1)
            e.wait_ge(small_c, 4)
            e.tensor_scalar(prm[:, 20:28], prm[:, 20:28], 0.5, None, ALU.mult).then_inc(small_c, 1)
            nl, la, y, mx, z, z2 = (b[:, :] for b in sp)
            e.tensor_scalar(nl, prm[:, 28:32], -1.0, None, ALU.mult).then_inc(sp_dve, 1)
            e.wait_ge(sp_dve, 2)
            e.tensor_tensor(la, nl, prm[:, 28:32], ALU.max).then_inc(sp_dve, 1)
            x_lo(2)
            x_norm(4)
            lo(0, 0)
            x_lo(3)
            x_lo(4)
            e.tensor_scalar(mx, nl, 0.0, None, ALU.max).then_inc(sp_dve, 1)
            e.wait_ge(sp_act, 1)
            e.tensor_scalar(z, y, 2.0, None, ALU.add).then_inc(sp_dve, 1)
            e.wait_ge(sp_dve, 5)
            e.reciprocal(z, z).then_inc(sp_dve, 1)
            e.wait_ge(sp_dve, 6)
            e.tensor_tensor(z, y, z, ALU.mult).then_inc(sp_dve, 1)
            e.wait_ge(sp_dve, 7)
            e.tensor_tensor(z2, z, z, ALU.mult).then_inc(sp_dve, 1)
            e.wait_ge(sp_dve, 8)
            e.tensor_scalar(nl, z2, 1.0 / (2 * SERIES + 1), None, ALU.mult).then_inc(sp_dve, 1)
            for k in range(SERIES - 1, -1, -1):
                e.wait_ge(sp_dve, 8 + SERIES - k)
                e.scalar_tensor_tensor(nl, nl, 1.0 / (2 * k + 1), z2 if k else z, ALU.add, ALU.mult).then_inc(sp_dve, 1)
            e.wait_ge(sp_dve, 9 + SERIES)
            e.scalar_tensor_tensor(nl, nl, 2.0, mx, ALU.mult, ALU.add).then_inc(sp_dve, 1)
            e.wait_ge(sp_dve, 10 + SERIES)
            e.tensor_scalar(prm[:, 28:32], nl, 2.0, None, ALU.mult).then_inc(small_c, 1)

            with e.Fori(0, PAIRS) as it:
                def next_lo(j):
                    lo(it * TILES_IT + (j + 1), (j + 1) % 2)

                def cache_copy(f):
                    e.wait_ge(tp_ready, it * 13 + (f + 1))
                    e.tensor_copy(kcT[:, 2 * f:2 * f + 2, :], ps[:, T_BANK, :].rearrange("p (b k) -> p b k", b=2)
                                  ).then_inc(tp_free, 1)

                def logits(u):
                    h, n = u // TT, (u % TT + 1) * P
                    count = e.to_reg(it * 9 + (u + 2))
                    e.wait_ge(bias_in, 16)
                    e.wait_ge(s_ready, count)
                    e.tensor_tensor_reduce(lgt[:, u % 2, 0:n], ps[:, S_BANK, 0:n], biasT[:, h, 0:n][:, ::-1], -1.0, BIG,
                                           ALU.add, ALU.min, nmax[:, u + 1:u + 2]).then_inc(logits_done, 1)

                def norm(u):
                    n = (u % TT + 1) * P
                    e.wait_ge(exp_done, it * 9 + (u + 2))
                    e.reciprocal(rden[:, u + 1:u + 2], den[:, u + 1:u + 2]).then_inc(rden_done, 1)
                    e.wait_ge(rden_done, it * 9 + (u + 2))
                    e.tensor_scalar(lgt[:, u % 2, 0:n], lgt[:, u % 2, 0:n], rden[:, u + 1:u + 2], None, ALU.mult
                                    ).then_inc(probs_done, 1)

                def rg(step, ins):
                    ins.then_inc(rg_step, 1)

                def rg_wait(step):
                    e.wait_ge(rg_step, it * 12 + step)

                next_lo(0); cache_copy(1)
                next_lo(1); cache_copy(3)
                next_lo(2)
                e.wait_ge(tile_done, it * TILES_IT + 4)
                e.tensor_copy(halves(kT[:, :]), two(1)).then_inc(tile_free[1], 1)
                count = e.to_reg(it * 9 + 1)
                e.wait_ge(consts, 7)
                e.wait_ge(s_ready, count)
                e.tensor_tensor_reduce(lgt_s[0:ROWS_S, :], ps[0:ROWS_S, S_BANK, 0:KS], mask_s[0:ROWS_S, :], -1.0, BIG,
                                       ALU.add, ALU.min, nmax[0:ROWS_S, 0:1]).then_inc(logits_done, 1)
                next_lo(3)
                e.wait_ge(exp_done, it * 9 + 1)
                e.reciprocal(rden[0:ROWS_S, 0:1], den[0:ROWS_S, 0:1]).then_inc(rden_done, 1)
                e.wait_ge(rden_done, it * 9 + 1)
                e.tensor_scalar(lgt_s[0:ROWS_S, :], lgt_s[0:ROWS_S, :], rden[0:ROWS_S, 0:1], None, ALU.mult
                                ).then_inc(probs_done, 1)
                e.wait_ge(bias_in, it * 16 + 16)
                logits(0)
                e.wait_ge(mi_ready, it * 8 + 1)
                e.wait_ge(kv_out, it * 64 + 64)
                e.tensor_copy(tok[:, 1, 0:TT, :], ps[:, M_BANK, :].rearrange("p (tt c) -> p tt c", c=P)).then_inc(mi_free, 1)
                norm(0); logits(1)
                e.wait_ge(mi_ready, it * 8 + 2)
                e.tensor_copy(tok[0:TS, :, TT, :], ps[0:TS, M_BANK, 0:2 * P].rearrange("p (g c) -> p g c", g=2)
                              ).then_inc(mi_free, 1)
                norm(1)
                next_lo(4)
                e.wait_ge(tile_done, it * TILES_IT + 6)
                e.wait_ge(it_ready, it + 1)
                e.tensor_copy(xp[:, CW - 1:CW - 1 + HT], ps[:, 2, 0:HT])
                e.tensor_copy(xp[:, CW - 1 + HT:CW - 1 + SEQ], ps[:, 3, 0:SEQ - HT])
                e.tensor_copy(xps[:, :, CW - 1:CW - 1 + DEC_T], bt(ps[:, 3, SEQ - HT:HT])).then_inc(tile_free[1], 1)
                logits(2); norm(2); logits(3)
                e.wait_ge(tile_free[1], it * 4 + 3)
                for j in range(CW):
                    for g, (dst, src) in enumerate((
                            (xc[:, 0:SEQ], xp[:, j:j + SEQ]),
                            (xc[:, SEQ:EXT].rearrange("p (b k) -> p b k", b=DEC_B)[:, :, 1:1 + DEC_T],
                             xps[:, :, j:j + DEC_T]))):
                        if j == 0:
                            e.tensor_scalar(dst, src, prm_it[:, 0:1], prm_it[:, 4:5], ALU.mult, ALU.add
                                            ).then_inc(conv_step, 1)
                        else:
                            e.wait_ge(conv_step, it * 8 + (2 * j + g - 1))
                            e.scalar_tensor_tensor(dst, src, prm_it[:, j:j + 1], dst, ALU.mult, ALU.add
                                                   ).then_inc(conv_step, 1)
                norm(3)
                e.wait_ge(so_hi, it + 1)
                for h in range(2):
                    rows = slice(DH * h, DH * h + DH)
                    cols = bass.ds(it * T + SEQ, TS)
                    last = e.tensor_tensor(bt(ocat_lo[rows, :, :].rearrange("p k t -> p (k t)")[:, cols]),
                                           ps[rows, M_BANK, 0:ROWS_S].rearrange("p (b h t) -> p b h t", h=2, t=DEC_T)[:, :, h, :],
                                           bt(ocat_hi[rows, :, :].rearrange("p k t -> p (k t)")[:, cols].bitcast(F32)),
                                           ALU.subtract)
                last.then_inc(mi_free, 1)
                next_lo(5)
                logits(4); norm(4); logits(5); norm(5)
                next_lo(6)
                logits(6); norm(6)
                e.wait_ge(th_done, it + 1)
                rg(1, e.tensor_scalar(dd[:, :], th[:, :], 1.0, None, ALU.add))
                rg_wait(1)
                rg(2, e.reciprocal(dd[:, :], dd[:, :]))
                logits(7); norm(7)
                rg_wait(2)
                rg(3, e.tensor_scalar(aa[:, :], dd[:, :], 2.0, -1.0, ALU.mult, ALU.add))
                rg_wait(3)
                resets = [b[:, SEQ:EXT].rearrange("p (b k) -> p b k", b=DEC_B)[:, :, 0:1] for b in (aa, ti)]
                rg(4, e.memset(resets[0], 0.0))
                next_lo(7)
                rg(5, e.scalar_tensor_tensor(ti[:, :], ti[:, :], 1.0, xc[:, :], ALU.add, ALU.mult))
                e.wait_ge(sq_done, it + 1)
                rg(6, e.tensor_tensor(sq[:, :], sq[:, :], dd[:, :], ALU.mult))
                rg_wait(6)
                rg(7, e.tensor_tensor(ti[:, :], ti[:, :], sq[:, :], ALU.mult))
                rg_wait(7)
                rg(8, e.tensor_copy(resets[1], stT[:, bass.ds(it, 1), 24:32].rearrange("p o b -> p b o")))
                rg_wait(8)
                rg(9, e.tensor_tensor_scan(sq[:, :], aa[:, :], ti[:, :], 0.0, ALU.mult, ALU.add))
                e.wait_ge(tg_done, it + 1)
                rg(10, e.scalar_tensor_tensor(gp[:, :], gp[:, :], 1.0, gb[:, :], ALU.add, ALU.mult))
                rg_wait(10)
                rg(11, e.scalar_tensor_tensor(dd[:, 0:SEQ], sq[:, 0:SEQ], 0.5, gp[:, 0:SEQ], ALU.mult, ALU.mult))
                rg(12, e.scalar_tensor_tensor(bt(dd[:, SEQ:T]),
                                              sq[:, SEQ:EXT].rearrange("p (b k) -> p b k", b=DEC_B)[:, :, 1:1 + DEC_T], 0.5,
                                              bt(gp[:, SEQ:T]), ALU.mult, ALU.mult))
                e.wait_ge(o_hi, it + 1)
                e.tensor_tensor(ocat_lo[:, bass.ds(it, 1), 0:SEQ], ps[:, O_BANK, :],
                                ocat_hi[:, bass.ds(it, 1), 0:SEQ].bitcast(F32), ALU.subtract).then_inc(o_free, 1)
                e.wait_ge(orn_hi, it + 1)
                e.tensor_tensor(ocat_lo[:, bass.ds(it + PAIRS, 1), :], dd[:, 0:T],
                                ocat_hi[:, bass.ds(it + PAIRS, 1), :].bitcast(F32), ALU.subtract).then_inc(rg_done, 1)

            with e.Fori(0, GT_TAIL // 2) as n:
                for s in range(2):
                    lo(n * 2 + (C_TAIL + s + 1), 1 - s)
            e.wait_ge(st_ready, 1)
            e.tensor_copy(st_out[:, :], ps[0:36, M_BANK, :]).then_inc(st_copied, 1)

            e.wait_ge(kv_out, 64 * (PAIRS + 1))
            with e.Fori(0, KD // 2) as n:
                for s in range(2):
                    i = n * 2 + (C_MIX + s)
                    lo(i + 1, 1 - s)
                    e.wait_ge(tile_done, i + 3)
                    for g, dst in ((0, ma[s]), (1, mr[s])):
                        last = e.scalar_tensor_tensor(halves(dst[:, :]), tile_of(gates, n * 2, s + KD * g), 1.0,
                                                      two(2 * s + g), ALU.add, ALU.mult)
                    last.then_inc(mix_free, 1)
                    e.wait_ge(mix_free, n * 2 + (s + 3))
                    e.tensor_tensor(ma[s][:, :], ma[s][:, :], mr[s][:, :], ALU.add).then_inc(mix_sum, 1)
                    e.wait_ge(mix_hi, n * 2 + (s + 1))
                    e.scalar_tensor_tensor(tile_of(xin_lo, n * 2, s), halves(ma[s][:, :]), 0.5,
                                           tile_of(xin_hi, n * 2, s).bitcast(F32), ALU.mult, ALU.subtract
                                           ).then_inc(mix_lo, 1)

            e.wait_ge(tile_done, C_OUT + 2)
            e.memset(oacc[0][:, :], 0.0).then_inc(acc_zero, 1)
            e.wait_ge(acc_zero, 1)
            e.wait_ge(st_out_s, 64)

            def out_square(m, s, h):
                e.wait_ge(out_free, m + (KD * h + 3))
                e.wait_ge(osq_used, m + (KD * h + 2))
                acc = oacc[0][:, h * HT:h * HT + HT]
                e.tensor_tensor(acc, acc, osq[s][:, :], ALU.add).then_inc(osq_used, 1)

            def residual(k, j, h):
                o, x = half_of(og, k, h), half_of(x1, k, h)
                e.tensor_tensor(o, o, rb[0][:, h * HT:h * HT + HT], ALU.mult).then_inc(t_done, 1)
                e.wait_ge(t_done, j + 1)
                e.tensor_tensor(x, x, o, ALU.add).then_inc(x1_done, 1)

            def x1_low(k, j, h):
                e.wait_ge(f_hi, j + 1)
                e.scalar_tensor_tensor(half_of(xin_lo, k, h), half_of(x1, k, h), prm[:, bass.ds(k + 40, 1)],
                                       half_of(xin_hi, k, h).bitcast(F32), ALU.mult, ALU.subtract).then_inc(f_lo, 1)

            def inverse(n, out, src):
                e.wait_ge(n_std, n)
                e.reciprocal(out, src).then_inc(n_rstd, 1)
                e.wait_ge(n_rstd, n)

            lo(C_OUT + 1, 1)
            with e.Fori(0, KD // 2) as n:
                for s in range(2):
                    lo(n * 2 + (C_OUT + s + 2), s)
                    e.wait_ge(xT_ready, n * 2 + (s + 1))
                    e.tensor_copy(x1[:, bass.ds(n * 2 + s, 1), 0:SEQ], ps[:, 4 + 2 * s, :])
                    e.tensor_copy(x1[:, bass.ds(n * 2 + s, 1), SEQ:T], ps[:, 5 + 2 * s, 0:TS]).then_inc(xT_free, 1)
                    out_square(n * 2 + s, s, 0)
            lo(C_OUT + KD + 2, 0)
            out_square(0, 0, 1)
            inverse(1, rb[0][:, 0:HT], std[:, 0:HT])
            lo(C_OUT + KD + 3, 1)
            out_square(1, 1, 1)
            residual(0, 0, 0)
            with e.Fori(0, KD // 2 - 1) as n:
                for s in range(2):
                    lo(n * 2 + (C_OUT + KD + s + 4), s)
                    residual(n * 2 + (s + 1), n * 2 + (s + 1), 0)
                    out_square(n * 2 + (s + 2), s, 1)
                    x1_low(n * 2 + s, n * 2 + s, 0)
            x1_low(KD - 2, KD - 2, 0)
            residual(KD - 1, KD - 1, 0)
            inverse(2, rb[0][:, HT:T], std[:, HT:T])
            x1_low(KD - 1, KD - 1, 0)
            for k in range(KD + 1):
                if k < KD:
                    residual(k, KD + k, 1)
                if k >= 1:
                    x1_low(k - 1, KD + k - 1, 1)

            rms_b = halves(rb[1][:, :])

            def ffn_lo(n, s, c):
                lo(n * 4 + (C_FFN + 2 * s + 2 + c), c)

            def ffn_gate(n, s):
                e.wait_ge(tile_done, n * 4 + (C_FFN + 2 * s + 3))
                e.wait_ge(lo_done, n * 4 + (C_FFN + 2 * s + 5))
                e.tensor_tensor(halves(fg[:, :]), two(2 * s), rms_b, ALU.mult).then_inc(gu_scaled, 1)

            def ffn_silu(n, s):
                e.wait_ge(fsil, n * 2 + (s + 1))
                e.scalar_tensor_tensor(fg[:, :], ft[:, :], 1.0, fg[:, :], ALU.add, ALU.mult).then_inc(fprod, 1)

            def ffn_up(n, s):
                e.wait_ge(tile_done, n * 4 + (C_FFN + 2 * s + 4))
                e.tensor_tensor(halves(fu[:, :]), two(2 * s + 1), rms_b, ALU.mult).then_inc(gu_free, 1)
                e.wait_ge(gu_free, n * 2 + (s + 3))
                e.wait_ge(fprod, n * 4 + (2 * s + 1))
                e.tensor_tensor(fg[:, :], fg[:, :], fu[:, :], ALU.mult).then_inc(fprod, 1)
                e.wait_ge(hid_h, n * 2 + (s + 1))
                e.scalar_tensor_tensor(tile_of(hid_lo, n * 2, s), halves(fg[:, :]), 0.5,
                                       tile_of(hid_hi, n * 2, s).bitcast(F32), ALU.mult, ALU.subtract
                                       ).then_inc(hid_l, 1)

            def ffn_tile(n, s):
                ffn_lo(n, s, 0)
                ffn_gate(n, s)
                ffn_silu(n, s)
                ffn_lo(n, s, 1)
                ffn_up(n, s)

            ffn_lo(0, 0, 0)
            ffn_lo(0, 0, 1)
            inverse(3, rb[1][:, :], std[:, :])
            ffn_gate(0, 0)
            ffn_silu(0, 0)
            ffn_up(0, 0)
            ffn_tile(0, 1)
            with e.Fori(1, KF // 2) as n:
                ffn_tile(n, 0)
                ffn_tile(n, 1)

            e.wait_ge(tile_done, C_DOWN + 2)
            e.memset(yacc[:, :], 0.0).then_inc(acc_zero, 1)
            e.wait_ge(acc_zero, 2)

            def down_lo(n, odd, c):
                q = 3 * odd + c + 2
                lo(n * 6 + (C_DOWN + q), q % 2, DOWN_K[(c + 2) % 3])

            def x1_copy(m):
                e.wait_ge(x1t_ready, m + 1)
                e.tensor_copy(x1tok[:, 0:TT, bass.ds(m * P, P)], ps[:, 4, :].rearrange("p (tt c) -> p tt c", c=P))
                e.tensor_copy(x1tok[0:TS, TT, bass.ds(m * P, P)], ps[0:TS, 5, 0:P]).then_inc(x1t_free, 1)

            def y_square(m):
                e.wait_ge(y_free, m + 3)
                e.wait_ge(ysq_used, m + 1)
                e.tensor_tensor(yacc[:, :], yacc[:, :], ysq[:, :], ALU.add).then_inc(ysq_used, 1)

            def y_tile(n, odd, copy=True):
                m = n * 2 + odd
                down_lo(n, odd, 0)
                if copy:
                    x1_copy(m - 1)
                down_lo(n, odd, 1)
                down_lo(n, odd, 2)
                y_square(m)

            y_tile(0, 0, copy=False)
            with e.Fori(0, (KD - 2) // 2) as n:
                y_tile(n, 1)
                y_tile(n + 1, 0)
            lo(C_DOWN + 3 * KD - 1, (C_DOWN + 3 * KD - 1) % 2, DOWN_K[2])
            x1_copy(KD - 2)
            y_square(KD - 1)
            x1_copy(KD - 1)
            e.wait_ge(ycol_step, 1)
            e.reciprocal(ycol[:, 8:8 + TT], ycol[:, 0:TT])
            e.reciprocal(ycol[0:TS, 8 + TT:9 + TT], ycol[0:TS, TT:TT + 1]).then_inc(ycol_step, 1)
            e.wait_ge(ycol_step, 2)
            e.wait_ge(x1t_free, KD + 2)
            e.wait_ge(yt_free, KD + 1)
            for tt in range(TT + 1):
                rows = slice(0, P if tt < TT else TS)
                e.scalar_tensor_tensor(ytok[rows, tt, :], ytok[rows, tt, :], ycol[rows, 8 + tt:9 + tt], x1tok[rows, tt, :],
                                       ALU.mult, ALU.add).then_inc(z_done, 1)


_INS = ["x_prompt", "x_sample", "cache_k", "cache_v", "page_table", "state_conv", "state_h",
        "norm_mix_pre", "norm_mix_post", "w_in", "rel_bias", "conv_w", "conv_b", "rg_w_r", "rg_b_r",
        "rg_w_i", "rg_b_i", "rg_lambda", "w_proj_attn", "w_proj_rnn", "w_out", "norm_ffn_pre",
        "norm_ffn_post", "w_gate_up", "w_down"]
_OUTS = [(1, SEQ, D), (DEC_B, DEC_T, D), (1, 1, SEQ, HEADS, DH), (1, 1, SEQ, HEADS, DH),
         (1, DEC_B, DEC_T, HEADS, DH), (1, DEC_B, DEC_T, HEADS, DH), (1, 1, CW - 1, DR), (1, 1, DR),
         (1, DEC_B, CW - 1, DR), (1, DEC_B, DR)]


def kernel(**inputs):
    import numpy as _np
    import concourse.bacc as _bacc
    from concourse import mybir as _mybir
    from concourse.bass_utils import run_bass_kernel_spmd as _run

    nc = _bacc.Bacc("TRN2", target_bir_lowering=False, num_devices=1)
    arrays, args = {}, []
    for name in _INS + ["bucket_of"]:
        a = bucket_table() if name == "bucket_of" else _np.ascontiguousarray(inputs[name])
        arrays[f"in_{name}_dram"] = a
        args.append(nc.dram_tensor(f"in_{name}_dram", a.shape, _mybir.dt.from_np(a.dtype), kind="ExternalInput").ap())
    for i, shape in enumerate(_OUTS):
        args.append(nc.dram_tensor(f"out_{i}_dram", shape, _mybir.dt.float32, kind="ExternalOutput").ap())
    program(nc, *args)
    r = _run(nc, [arrays], core_ids=[0])
    return tuple(r.results[0][f"out_{i}_dram"] for i in range(len(_OUTS)))
```

```python
import math
from contextlib import ExitStack

import numpy as np

import concourse.bass as bass
from concourse import mybir

F32 = mybir.dt.float32
F32R = mybir.dt.float32r
I32 = mybir.dt.int32
ALU = mybir.AluOpType
ACT = mybir.ActivationFunctionType
AP = bass.AP

P = 128
D = 1024
KD = D // P
SEQ = 512
DEC_B, DEC_T = 8, 4
TS = DEC_B * DEC_T
T = SEQ + TS
HT = T // 2
HEADS, DH = 8, 64
DA = HEADS * DH
PAIRS = DA // P
DR = 512
RGB = 64
CW = 4
PAST = 256
PAGE = 128
NPG = PAST // PAGE
DFF = -(-8 * D // (3 * 256)) * 256
KF = DFF // P
TT = SEQ // P
NB, MAXD = 32, 128
EPS = 1e-6
NEG = -1.0e30
BIG = 3.0e38
EXT = SEQ + DEC_B * (DEC_T + 1)
EH = EXT // 2
RELW = 640
KS = PAST + TS
GR, NG = 32, 4
NJ = DEC_B // NG

TILES_IT = 8
GT_IT = 3
C_TAIL = PAIRS * TILES_IT
GT_TAIL = 2 * KD - PAIRS * GT_IT
C_MIX = C_TAIL + GT_TAIL
C_OUT = C_MIX + KD
C_FFN = C_OUT + 2 * KD
C_DOWN = C_FFN + 2 * KF
DOWN_K = [8, 8, KF - 16]

SERIES = 9
GELU_C1 = math.sqrt(2.0 / math.pi)
GELU_C2 = GELU_C1 * 0.044715


def bucket_table():
    n = np.arange(RELW) - 127
    pos = np.maximum(n, 1).astype(np.float32)
    half = NB // 2
    large = half + (np.log(pos / half) / math.log(MAXD / half) * (NB - half)).astype(np.int32)
    bucket = np.where(n < half, np.maximum(n, 0), np.minimum(large, NB - 1))
    table = np.zeros((NB + 1, RELW), np.float32)
    table[np.where(n < 0, NB, bucket), np.arange(RELW)] = 1.0
    return table


def program(nc, x_prompt, x_sample, cache_k, cache_v, page_table, state_conv, state_h,
            norm_mix_pre, norm_mix_post, w_in, rel_bias, conv_w, conv_b, rg_w_r, rg_b_r,
            rg_w_i, rg_b_i, rg_lambda, w_proj_attn, w_proj_rnn, w_out, norm_ffn_pre,
            norm_ffn_post, w_gate_up, w_down, bucket_of,
            y_prompt, y_sample, new_k_prompt, new_v_prompt, new_k_sample, new_v_sample,
            new_conv_prompt, new_h_prompt, new_conv_sample, new_h_sample):
    n_phys = cache_k.shape[1]
    dist_bias = nc.dram_tensor("dist_bias", (HEADS, RELW), F32, kind="Internal").ap()

    at = [-(-nc.sbuf_base // 64) * 64]

    def put(name, shape, dt=F32, where=None):
        size = 4 * int(np.prod(shape[1:]))
        size = -(-size // 32) * 32
        if where is None:
            offset, at[0] = at[0], at[0] + size
        else:
            offset, where[0] = where[0], where[0] + size
        assert offset + size <= nc.sbuf_usable_end, (name, offset + size)
        return nc.alloc_sbuf_tensor_at(name, shape, dt, offset=offset)

    ring = [[put(f"w_{part}{s}", [P, KD, P], dt) for s in range(2)]
            for part, dt in (("raw", F32), ("hi", F32R), ("lo", F32R))]
    w_raw, w_hi, w_lo = ring
    xin_at = at[0]
    xin_hi = put("xin_hi", [P, KD, T], F32R)
    xin_lo = put("xin_lo", [P, KD, T], F32R)
    ident = put("ident", [P, P])
    ones = put("ones", [P, P])
    prm = put("prm", [P, 56])
    eps_col = put("eps_col", [P, 1])
    tiny_col = put("tiny_col", [P, 1])
    big_at = at[0]

    ocat_hi = put("ocat_hi", [P, 2 * PAIRS, T], F32R)
    ocat_lo = put("ocat_lo", [P, 2 * PAIRS, T], F32R)
    gates = put("gates", [P, 2 * KD, T])
    stage_at = at[0]
    qT, kT, vT = (put(n, [P, T]) for n in ("qT", "kT", "vT"))
    tok = put("tok", [P, 2, TT + 1, P])
    q_bd = put("q_bd", [P, DEC_B, GR])
    q_all = put("q_all", [P, NG, GR])
    kcT_at = at[0]
    kcT = put("kcT", [P, DEC_B, PAST])
    kc = put("kc", [P, DEC_B * NPG, P])
    vc = put("vc", [P, DEC_B * NPG, P])
    biasT = put("biasT", [P, 2, SEQ])
    lgt_at = at[0]
    lgt = put("lgt", [P, 2, SEQ])
    prT = put("prT", [P, 2, SEQ])
    lgt_s = put("lgt_s", [P, KS])
    prT_s = put("prT_s", [P, 3, P])
    mask_s = put("mask_s", [P, KS])
    bias8 = put("bias8", [P, PAIRS, KS])
    rep8 = put("rep8", [P, P])
    nmax = put("nmax", [P, 9])
    den = put("den", [P, 9])
    rden = put("rden", [P, 9])
    stT = put("stT", [P, PAIRS, 32])
    stcol = put("stcol", [P, PAIRS, 36])
    prm_it = put("prm_it", [P, 8])
    bd = put("bd", [P, 2, P])
    xp = put("xp", [P, SEQ + CW - 1])
    xps = put("xps", [P, DEC_B, DEC_T + CW - 1])
    xc = put("xc", [P, EXT])
    th = put("th", [P, EXT])
    ti = put("ti", [P, EXT])
    dd = put("dd", [P, EXT])
    aa = put("aa", [P, EXT])
    sq = put("sq", [P, EXT])
    gb = put("gb", [P, T])
    gp = put("gp", [P, T])
    st_out = put("st_out", [36, DR], where=[lgt_at])
    w = [kcT_at]
    o_tok = put("o_tok", [P, SEQ], where=w)
    o_s = put("o_s", [P, NJ * P], where=w)
    w = [big_at]
    x_tok = put("x_tok", [P, TT + 1, D], where=w)
    x_sq = put("x_sq", [P, D], where=w)
    g_row = put("g_row", [P, D], where=w)
    ssum = put("ssum", [P, 8], where=w)
    rstd_x = put("rstd_x", [P, 8], where=w)
    prow = put("prow", [56, P], where=w)
    strow = put("strow", [32, DR], where=w)
    rel33 = put("rel33", [NB + 1, HEADS], where=w)
    bktab = put("bktab", [NB + 1, RELW], where=w)
    drow = put("drow", [HEADS, RELW], where=w)
    pages = put("pages", [1, DEC_B * NPG], I32, where=w)
    sp = [put(f"sp{i}", [P, 4], where=w) for i in range(6)]
    bias8_rev = put("bias8_rev", [8, PAIRS, DEC_T + PAST], where=w)
    assert w[0] <= stage_at
    w = [stage_at]
    ma = [put(f"ma{i}", [P, T], where=w) for i in range(2)]
    mr = [put(f"mr{i}", [P, T], where=w) for i in range(2)]
    xk = [put(f"xk{i}", [P, TT + 1, P], where=w) for i in range(2)]
    hid_end = big_at + 2 * 4 * KF * T
    tmp_end = w[0]
    assert w[0] <= hid_end
    w = [hid_end]
    x1 = put("x1", [P, KD, T], where=w)
    ytok = put("ytok", [P, TT + 1, D], where=w)
    rb = [put(f"rb{i}", [P, T], where=w) for i in range(2)]
    std = put("std", [P, T], where=w)
    fg, fu, ft = (put(n, [P, T], where=w) for n in ("fg", "fu", "ft"))
    w = [big_at]
    og = put("og", [P, KD, T], where=w)
    osq = [put(f"osq{i}", [P, HT], where=w) for i in range(2)]
    xsq = [put(f"xsq{i}", [P, HT], where=w) for i in range(2)]
    oacc = [put(f"oacc{i}", [P, T], where=w) for i in range(2)]
    assert w[0] <= stage_at
    w = [big_at]
    hid_hi = put("hid_hi", [P, KF, T], F32R, where=w)
    hid_lo = put("hid_lo", [P, KF, T], F32R, where=w)
    def keep(name, where):
        return put(name + "_hi", [P, KD, P], F32R, where), put(name + "_lo", [P, KD, P], F32R, where)

    w = [hid_end + 4 * KD * T]
    w_keep = {m: keep(f"w_keep{m}", w) for m in (2, 3)}
    assert w[0] <= hid_end + 4 * KD * T + 4 * (TT + 1) * D
    w_keep[4] = keep("w_keep4", [tmp_end])
    assert tmp_end + 8 * KD * P <= hid_end
    w = [big_at + 4 * 2 * PAIRS * T * 2]
    w_keep.update({m: keep(f"w_keep{m}", w) for m in (5, 6, 7)})
    assert w[0] <= stage_at
    w_out_of = [(w_hi[m], w_lo[m]) if m < 2 else w_keep[m] for m in range(KD)]
    w = [xin_at]
    x1tok = put("x1tok", [P, TT + 1, D], where=w)
    yg = [put(f"yg{i}", [P, T], where=w) for i in range(2)]
    x1s = [put(f"x1s{i}", [P, T], where=w) for i in range(2)]
    ysq = put("ysq", [P, T], where=w)
    yacc = put("yacc", [P, T], where=w)
    ycol = put("ycol", [P, 16], where=w)
    assert w[0] <= xin_at + 2 * 4 * KD * T

    with ExitStack() as ctx:
        def sem(name):
            return ctx.enter_context(nc.semaphore(name))

        ps = ctx.enter_context(nc.psum_tensor("ps", [P, 8, 512], F32))
        S_BANK, T_BANK, O_BANK, M_BANK = 4, 5, 6, 7

        w_in_slot = [sem("w_slot0"), sem("w_slot1")]
        hi_done = sem("hi_done")
        lo_done = sem("lo_done")
        tile_done = sem("tile_done")
        tile_free = [sem("tile_free0"), sem("tile_free1")]
        x_in = [sem(f"x_in{i}") for i in range(TT + 1)]
        par_in = sem("par_in")
        rel_in = sem("rel_in")
        g_in = sem("g_in")
        page_in = sem("page_in")
        bias8_in = sem("bias8_in")
        dist_out = sem("dist_out")
        consts = sem("consts")
        consts_v = sem("consts_v")
        sq_sum = sem("sq_sum")
        std_x = sem("std_x")
        rx_done = sem("rx_done")
        xs_done = sem("xs_done")
        xt_ready = sem("xt_ready")
        xt_hi = sem("xt_hi")
        xt_lo = sem("xt_lo")
        small_T = sem("small_T")
        small_c = sem("small_c")
        sp_act = sem("sp_act")
        sp_dve = sem("sp_dve")
        kc_in = sem("kc_in")
        vc_in = sem("vc_in")
        bias_in = sem("bias_in")
        bd_in = sem("bd_in")
        kv_out = sem("kv_out")
        it_ready = sem("it_ready")
        q_spread = sem("q_spread")
        s_ready = sem("s_ready")
        logits_done = sem("logits_done")
        exp_done = sem("exp_done")
        rden_done = sem("rden_done")
        probs_done = sem("probs_done")
        tp_ready = sem("tp_ready")
        tp_free = sem("tp_free")
        mi_ready = sem("mi_ready")
        mi_free = sem("mi_free")
        so_hi = sem("so_hi")
        pv_done = sem("pv_done")
        v_ready = sem("v_ready")
        ov_done = sem("ov_done")
        o_hi = sem("o_hi")
        o_free = sem("o_free")
        conv_step = sem("conv_step")
        th_done = sem("th_done")
        sq_done = sem("sq_done")
        gelu_step = sem("gelu_step")
        tg_done = sem("tg_done")
        rg_step = sem("rg_step")
        orn_hi = sem("orn_hi")
        rg_done = sem("rg_done")
        st_saved = sem("st_saved")
        st_ready = sem("st_ready")
        st_copied = sem("st_copied")
        st_out_s = sem("st_out_s")
        xk_in = [sem("xk_in0"), sem("xk_in1")]
        mix_free = sem("mix_free")
        mix_sum = sem("mix_sum")
        mix_hi = sem("mix_hi")
        mix_lo = sem("mix_lo")
        out_free = sem("out_free")
        osq_used = sem("osq_used")
        xT_ready = sem("xT_ready")
        xT_free = sem("xT_free")
        n_ready = sem("n_ready")
        n_std = sem("n_std")
        n_rstd = sem("n_rstd")
        t_done = sem("t_done")
        x1_done = sem("x1_done")
        f_hi = sem("f_hi")
        f_sq = sem("f_sq")
        f_lo = sem("f_lo")
        f_acc = sem("f_acc")
        gu_scaled = sem("gu_scaled")
        gu_free = sem("gu_free")
        fsil = sem("fsil")
        fprod = sem("fprod")
        hid_h = sem("hid_h")
        hid_l = sem("hid_l")
        y_free = sem("y_free")
        y_sq_last = sem("y_sq_last")
        ysq_used = sem("ysq_used")
        acc_zero = sem("acc_zero")
        x1s_done = sem("x1s_done")
        x1t_ready = sem("x1t_ready")
        x1t_free = sem("x1t_free")
        yt_ready = sem("yt_ready")
        yt_free = sem("yt_free")
        ycol_step = sem("ycol_step")
        yn_ready = sem("yn_ready")
        z_done = sem("z_done")
        y_out = sem("y_out")

        def two(pair):
            return ps[:, 2 * pair:2 * pair + 2, 0:HT]

        def halves(buf):
            return buf.rearrange("p (h t) -> p h t", h=2)

        def bt(ap):
            return ap.rearrange("p (b t) -> p b t", b=DEC_B)

        def sample_rows(h):
            v = ps[DH * h:DH * h + DH, M_BANK, 4 * h:4 * h + NJ * (P + 8)].rearrange("p (j r) -> p j r", j=NJ)
            return v[:, :, 0:P].rearrange("p j (g r) -> p j g r", g=NG)[:, :, :, 0:DEC_T]

        def sample_cols(buf, it, h):
            flat = buf[DH * h:DH * h + DH, :, :].rearrange("p k t -> p (k t)")
            return flat[:, bass.ds(it * T + SEQ, TS)].rearrange("p (j g t) -> p j g t", j=NJ, g=NG)

        def x_fill(dst, tt, hf, f):
            if tt < TT:
                return (dst[:, 4 * hf:4 * hf + 4, tt * P:(tt + 1) * P],
                        ps[:, 4 + f % 4, :].rearrange("p (k c) -> p k c", c=P))
            return dst[:, :, SEQ:T], ps[:, 4 + f % 4, 0:KD * TS].rearrange("p (k c) -> p k c", c=TS)

        def half_of(buf, k, h, k0=0):
            flat = buf[:, :, :].rearrange("p k t -> p (k t)")
            return flat[:, bass.ds(k * T + (k0 * T + h * HT), HT)]

        def tile_of(buf, k, k0=0):
            flat = buf[:, :, :].rearrange("p k t -> p (k t)")
            return halves(flat[:, bass.ds(k * T + k0 * T, T)])

        RESIDUALS = [[], [0], [1], [2], [3], [4], [5, 6], [7]]
        SP_ABS = 3
        block = ctx.enter_context(nc.Block())

        @block.sync
        def _(sp_):
            e = sp_
            wi = w_in[0].rearrange("(kt p) n -> p kt n", p=P)
            wpa = w_proj_attn[0].rearrange("(kt p) n -> p kt n", p=P)
            wpr = w_proj_rnn[0].rearrange("(kt p) n -> p kt n", p=P)
            wo = w_out[0].rearrange("(kt p) n -> p kt n", p=P)
            wgu = w_gate_up[0].rearrange("(kt p) n -> p kt n", p=P)
            wd = w_down[0].rearrange("(kt p) n -> p kt n", p=P)

            def load(i, s, src, k=KD):
                e.wait_ge(lo_done, i + 1)
                for k0, k1 in ((0, 4), (4, k)):
                    e.dma_start(w_raw[s][:, k0:k1, :], src[:, k0:k1, :]).then_inc(w_in_slot[s], 16)

            e.dma_start(pages[:, :], page_table.rearrange("b n -> (b n)").rearrange("(a n) -> a n", a=1)
                        ).then_inc(page_in, 16)
            for tt in range(TT):
                e.dma_start(x_tok[:, tt, :], x_prompt[0, tt * P:(tt + 1) * P, :]).then_inc(x_in[tt], 16)
            e.dma_start(x_tok[0:TS, TT, :], x_sample.rearrange("b t d -> (b t) d")).then_inc(x_in[TT], 16)
            for i in range(2):
                load(i, i, wi[:, :, 512 * i:512 * i + P])
            e.wait_ge(page_in, 16)
            page = [e.value_load(pages[0:1, j:j + 1], min_val=0, max_val=n_phys - 1)
                    for j in range(DEC_B * NPG)]

            def load_pages(cache, dst, done, it, part):
                for j in range(8 * part, 8 * part + 8):
                    src = cache[0].rearrange("n t h d -> n t (h d)")[bass.ds(page[j], 1), :, bass.ds(it * P, P)]
                    e.dma_start(dst[:, j, :], src.rearrange("o t c -> t (o c)")).then_inc(done, 16)

            def iteration(it, first=False, last=False):
                for j in range(TILES_IT):
                    if first and j < 2:
                        pass
                    elif j < 5:
                        load(it * TILES_IT + j, j % 2, wi[:, :, bass.ds(it * P + 512 * j, P)])
                    else:
                        load(it * TILES_IT + j, j % 2, wi[:, :, bass.ds(it * (GT_IT * P) + 2560 + (j - 5) * P, P)])
                    if j == 1:
                        e.wait_ge(consts, 12)
                        e.wait_ge(logits_done, it * 9 + 1)
                        src = AP(dist_bias.tensor, it * (2 * RELW), [[1, P], [RELW, 2], [1, SEQ]])
                        e.wait_ge(dist_out, 16)
                        e.dma_start(biasT[:, :, :], src).then_inc(bias_in, 16)
                        e.wait_ge(mi_free, it * 9 + 1)
                        for g, wrg in enumerate((rg_w_r, rg_w_i)):
                            for blk in range(2):
                                rows = slice(RGB * blk, RGB * blk + RGB)
                                e.dma_start(bd[rows, g, rows],
                                            wrg[0][bass.ds(it * 2 + blk, 1)].rearrange("o c d -> c (o d)")
                                            ).then_inc(bd_in, 16)
                    if j in (2, 3) and first:
                        load_pages(cache_v, vc, vc_in, 0, j - 2)
                    if j in (5, 6) and not last:
                        e.wait_ge(s_ready, it * 9 + 1)
                        load_pages(cache_k, kc, kc_in, it + 1, j - 5)
                e.wait_ge(mi_free, it * 9 + 4)
                for g, (op, os) in enumerate(((new_k_prompt, new_k_sample), (new_v_prompt, new_v_sample))):
                    dst = op[0, 0].rearrange("(tt p) h d -> p tt (h d)", p=P)[:, :, bass.ds(it * P, P)]
                    e.dma_start(dst, tok[:, g, 0:TT, :]).then_inc(kv_out, 16)
                    dst = os[0].rearrange("b t h d -> (b t) (h d)")[:, bass.ds(it * P, P)]
                    e.dma_start(dst, tok[0:TS, g, TT, :]).then_inc(kv_out, 16)
                if not last:
                    e.wait_ge(mi_ready, it * 9 + 4)
                    load_pages(cache_v, vc, vc_in, it + 1, 0)
                    load_pages(cache_v, vc, vc_in, it + 1, 1)

            for part in range(2):
                load_pages(cache_k, kc, kc_in, 0, part)
            iteration(0, first=True)
            with e.Fori(1, PAIRS - 1) as it:
                iteration(it)
            iteration(PAIRS - 1, last=True)
            with e.Fori(0, GT_TAIL // 2) as n:
                for s in range(2):
                    load(n * 2 + (C_TAIL + s), s, wi[:, :, bass.ds(n * (2 * P) + 2560 + (PAIRS * GT_IT + s) * P, P)])
            with e.Fori(0, KD // 2) as n:
                for s in range(2):
                    e.wait_ge(lo_done, n * 2 + (C_MIX + s + 1))
                    for k0, wp in ((0, wpa), (PAIRS, wpr)):
                        e.dma_start(w_raw[s][:, k0:k0 + PAIRS, :], wp[:, :, bass.ds(n * (2 * P) + s * P, P)]
                                    ).then_inc(w_in_slot[s], 16)
            e.wait_ge(st_copied, 1)
            e.dma_start(new_conv_prompt[0, 0], st_out[0:3, :]).then_inc(st_out_s, 16)
            e.dma_start(new_conv_sample[0].rearrange("b j d -> (b j) d"), st_out[3:27, :]).then_inc(st_out_s, 16)
            e.dma_start(new_h_prompt[0], st_out[27:28, :]).then_inc(st_out_s, 16)
            e.dma_start(new_h_sample[0], st_out[28:36, :]).then_inc(st_out_s, 16)
            with e.Fori(0, KD // 2) as n:
                for s in range(2):
                    load(n * 2 + (C_OUT + s), s, wo[:, :, bass.ds(n * (2 * P) + s * P, P)])
            with e.Fori(0, KF) as m:
                for s in range(2):
                    load(m * 2 + (C_FFN + s), s, wgu[:, :, bass.ds(m * P + s * DFF, P)])

            def load_down(m, c, s):
                k0 = sum(DOWN_K[:c])
                load(m * 3 + (C_DOWN + c), s, wd[:, k0:k0 + DOWN_K[c], bass.ds(m * P, P)], DOWN_K[c])

            with e.Fori(0, KD // 2) as n:
                for m2 in range(2):
                    for c in range(3):
                        load_down(n * 2 + m2, c, (m2 * 3 + c) % 2)
            for tt in range(TT + 1):
                e.wait_ge(z_done, tt + 1)
                if tt < TT:
                    e.dma_start(y_prompt[0, tt * P:(tt + 1) * P, :], ytok[:, tt, :]).then_inc(y_out, 16)
                else:
                    e.dma_start(y_sample.rearrange("b t d -> (b t) d"), ytok[0:TS, TT, :]).then_inc(y_out, 16)
            e.wait_ge(kv_out, 64 * (PAIRS + 1))
            e.wait_ge(st_out_s, 64)
            e.wait_ge(y_out, 16 * (TT + 1))

        @block.gpsimd
        def _(e):
            e.memset(ident[:, :], 0.0).then_inc(consts, 1)
            e.wait_ge(consts, 1)
            e.affine_select(out=ident[:, :], in_=ident[:, :], compare_op=ALU.not_equal, fill=1.0,
                            base=0, pattern=[[-1, P]], channel_multiplier=1).then_inc(consts, 1)
            for src, r0, n in ((conv_w, 0, 16), (conv_b, 16, 4), (rg_b_r, 20, 4), (rg_b_i, 24, 4),
                               (rg_lambda, 28, 4), (norm_mix_post, 32, 8), (norm_ffn_pre, 40, 8), (norm_ffn_post, 48, 8)):
                e.dma_start(prow[r0:r0 + n, :], AP(src.tensor, 0, [[P, n], [1, P]])).then_inc(par_in, 16)
            e.dma_start(strow[0:24, :], state_conv[0].rearrange("b j c -> (b j) c")).then_inc(par_in, 16)
            e.dma_start(strow[24:32, :], state_h[0]).then_inc(par_in, 16)
            e.memset(rep8[:, :], 0.0).then_inc(consts, 1)
            e.wait_ge(consts, 3)
            rep = rep8[:, :].rearrange("p (b k) -> p b k", k=8)
            e.affine_select(out=rep, in_=rep, compare_op=ALU.not_equal, fill=1.0,
                            base=0, pattern=[[0, P // 8], [-1, 8]], channel_multiplier=1).then_inc(consts, 1)
            e.memset(mask_s[:, :], 0.0).then_inc(consts, 1)
            e.wait_ge(consts, 5)
            own = mask_s[:, PAST:KS].rearrange("p (j g t) -> p j g t", j=NJ, g=NG)
            e.affine_select(out=own, in_=own, compare_op=ALU.is_ge, fill=NEG,
                            base=0, pattern=[[-8, NJ], [-GR, NG], [0, DEC_T]], channel_multiplier=1).then_inc(consts, 1)
            e.wait_ge(consts, 6)
            e.affine_select(out=own, in_=own, compare_op=ALU.is_ge, fill=NEG,
                            base=7, pattern=[[8, NJ], [GR, NG], [0, DEC_T]], channel_multiplier=-1).then_inc(consts, 1)
            e.memset(q_bd[:, :, :], 0.0).then_inc(consts, 1)
            e.memset(q_all[:, :, :], 0.0).then_inc(consts, 1)
            e.memset(bd[:, :, :], 0.0).then_inc(consts, 1)
            e.memset(xp[:, 0:CW - 1], 0.0).then_inc(consts, 1)
            e.memset(xc[:, :], 0.0).then_inc(consts, 1)
            e.wait_ge(dist_out, 16)
            for h in range(2):
                rows = slice(4 * h, 4 * h + 4)
                e.dma_start(bias8_rev[rows, :, DEC_T:DEC_T + PAST], AP(dist_bias.tensor, h * RELW + 128, [[1, 4], [2 * RELW, PAIRS], [1, PAST]])
                            ).then_inc(bias8_in, 16)
                e.dma_start(bias8_rev[rows, :, 0:DEC_T],
                            AP(dist_bias.tensor, h * RELW + 124, [[1, 4], [2 * RELW, PAIRS], [1, DEC_T]])).then_inc(bias8_in, 16)
            e.wait_ge(bias8_in, 64)
            e.tensor_copy(bias8[0:8, :, 0:PAST], bias8_rev[0:8, :, DEC_T:DEC_T + PAST][:, :, ::-1]).then_inc(consts, 1)
            for b in range(DEC_B):
                e.tensor_copy(bias8[0:8, :, PAST + b * DEC_T:PAST + (b + 1) * DEC_T], bias8_rev[0:8, :, 0:DEC_T][:, :, ::-1]
                              ).then_inc(consts, 1)

            with e.Fori(0, PAIRS) as it:
                count = e.to_reg(it + 1)
                e.wait_ge(small_c, 6)
                e.wait_ge(rg_done, count)
                e.tensor_copy(prm_it[:, :], prm[:, 0:32].rearrange("p (c f) -> p c f", f=PAIRS)[:, :, bass.ds(it, 1)])
                e.tensor_copy(xps[:, :, 0:CW - 1],
                              stT[:, bass.ds(it, 1), 0:24].rearrange("p o (b j) -> p (o b) j", b=DEC_B)
                              ).then_inc(it_ready, 1)
                count = e.to_reg(it * 4 + 2)
                e.wait_ge(consts, 12)
                e.wait_ge(tile_free[0], count)
                e.wait_ge(it_ready, it + 1)
                for h in range(2):
                    rows = slice(DH * h, DH * h + DH)
                    for j in range(NJ):
                        src = bt(qT[rows, SEQ:T])[:, NG * j:NG * j + NG, :]
                        cols = slice(8 * j + 4 * h, 8 * j + 4 * h + DEC_T)
                        e.tensor_copy(q_all[rows, :, cols], src)
                        last = e.tensor_copy(q_bd[rows, NG * j:NG * j + NG, cols], src)
                last.then_inc(q_spread, 1)
                count = e.to_reg(it * 4 + 3)
                e.wait_ge(consts, 12)
                e.wait_ge(tile_free[1], count)
                e.wait_ge(q_spread, it + 1)
                e.tensor_copy(stcol[:, bass.ds(it, 1), 0:3], xp[:, SEQ:SEQ + 3])
                e.tensor_copy(stcol[:, bass.ds(it, 1), 3:27].rearrange("p o (b j) -> p (o b) j", b=DEC_B),
                              xps[:, :, DEC_T:DEC_T + 3])
                e.wait_ge(tile_free[0], it * 4 + 4)
                e.tensor_tensor(gp[:, :], gb[:, :], gb[:, :], ALU.mult).then_inc(gelu_step, 1)
                count = e.to_reg(it * 3 + 1)
                e.wait_ge(consts, 12)
                e.wait_ge(gelu_step, count)
                e.tensor_scalar(gp[:, :], gp[:, :], GELU_C2, GELU_C1, ALU.mult, ALU.add).then_inc(gelu_step, 1)
                e.wait_ge(gelu_step, it * 3 + 2)
                e.tensor_tensor(gp[:, :], gp[:, :], gb[:, :], ALU.mult).then_inc(gelu_step, 1)
                count = e.to_reg(it * 12 + 9)
                e.wait_ge(small_c, 6)
                e.wait_ge(rg_step, count)
                e.tensor_copy(stcol[:, bass.ds(it, 1), 27:28], sq[:, SEQ - 1:SEQ])
                e.tensor_copy(stcol[:, bass.ds(it, 1), 28:36],
                              sq[:, SEQ:EXT].rearrange("p (b k) -> p b k", b=DEC_B)[:, :, DEC_T]
                              ).then_inc(st_saved, 1)
            xpt = x_prompt[0].rearrange("(tt p) d -> p tt d", p=P)
            xst = x_sample.rearrange("b t d -> (b t) d")
            e.wait_ge(tile_done, C_MIX + 3)
            e.wait_ge(kv_out, 64 * (PAIRS + 1))
            with e.Fori(0, KD // 2) as n:
                for s in range(2):
                    count = e.to_reg(n * 2 + (s + 1))
                    e.wait_ge(st_copied, 1)
                    e.wait_ge(xT_free, count)
                    cols = bass.ds(n * (2 * P) + s * P, P)
                    e.dma_start(xk[s][:, 0:TT, :], xpt[:, :, cols]).then_inc(xk_in[s], 16)
                    e.dma_start(xk[s][0:TS, TT, :], xst[:, cols]).then_inc(xk_in[s], 16)
            e.wait_ge(n_ready, 1)
            for h in range(2):
                acc = oacc[1][:, h * HT:h * HT + HT]
                for k in range(KD):
                    j = KD * h + k
                    e.wait_ge(f_sq, j + 1)
                    if k >= 1:
                        e.wait_ge(f_acc, j + 2)
                        e.tensor_tensor(acc, acc, xsq[j % 2][:, :], ALU.add).then_inc(f_acc, 1)
                    else:
                        e.tensor_copy(acc, xsq[j % 2][:, :]).then_inc(f_acc, 1)
            with e.Fori(0, KD // 2) as n:
                for s in range(2):
                    count = e.to_reg(n * 2 + (s + 1))
                    e.wait_ge(tile_done, C_DOWN + 2)
                    e.wait_ge(x1t_free, count)
                    e.tensor_copy(x1s[s][:, :], x1[:, bass.ds(n * 2 + s, 1), :]).then_inc(x1s_done, 1)

        @block.tensor
        def _(e):
            def steps(s, bank, xh, xl, ks, first, last, ready=None, base=1, hs=(0, 1), w=None):
                wh, wl = w or (w_hi[s], w_lo[s])
                for kw, kx in ks:
                    if ready is not None:
                        e.wait_ge(ready, kx + base)
                    for wt, xt in ((wh, xh), (wh, xl), (wl, xh)):
                        for h in hs:
                            mm = e.matmul(ps[:, bank + h, 0:HT], wt[:, kw, :], xt[:, kx, h * HT:h * HT + HT],
                                          start=first and wt is wh and xt is xh,
                                          stop=last and (kw, kx) == ks[-1] and wt is wl)
                    first = False
                return mm

            def split_ready(i):
                e.wait_ge(lo_done, i + 3)

            e.wait_ge(consts, 2)

            def x_T(tt):
                e.wait_ge(xs_done, tt + 1)
                rows = P if tt < TT else TS
                for hf in range(2 if tt < TT else 1):
                    f = 2 * tt + hf
                    if f >= 4:
                        e.wait_ge(xt_lo, f - 3)
                    kts = range(4 * hf, 4 * hf + 4) if tt < TT else range(KD)
                    for n, kt in enumerate(kts):
                        mm = e.transpose(ps[:, 4 + f % 4, n * rows:(n + 1) * rows],
                                         x_tok[0:rows, tt, kt * P:kt * P + P], ident[0:rows, 0:rows])
                    mm.then_inc(xt_ready, 1)

            for tt in range(TT + 1):
                x_T(tt)
            e.wait_ge(par_in, 160)
            e.transpose(ps[:, 2, 0:56], prow[:, :], ident[0:56, 0:56]).then_inc(small_T, 1)
            for f in range(PAIRS):
                mm = e.transpose(ps[:, 2, 64 + 32 * f:96 + 32 * f], strow[:, f * P:f * P + P], ident[0:32, 0:32])
            mm.then_inc(small_T, 1)
            e.wait_ge(rel_in, 32)
            e.matmul(ps[0:HEADS, 3, 0:512], rel33[:, :], bktab[:, 0:512], start=True, stop=True)
            e.matmul(ps[0:HEADS, 2, 192:192 + RELW - 512], rel33[:, :], bktab[:, 512:RELW], start=True,
                     stop=True).then_inc(small_T, 1)
            e.wait_ge(xt_lo, 9)

            with e.Fori(0, PAIRS) as it:
                i0 = it * TILES_IT

                def begin(j):
                    split_ready(i0 + j)
                    e.wait_ge(tile_free[j % 2], it * 4 + (j // 2 + 1))

                def part(j, k0, k1):
                    mm = steps(j % 2, 2 * (j % 2), xin_hi, xin_lo, [(k, k) for k in range(k0, k1)], k0 == 0, k1 == KD)
                    if k1 == KD:
                        mm.then_inc(tile_done, 1)

                def tp_wait(use):
                    e.wait_ge(tp_free, it * 13 + (use + 1))

                def mi_wait(use):
                    e.wait_ge(mi_free, it * 9 + (use + 1))

                def cache_T(f):
                    if f == 0:
                        e.wait_ge(kc_in, it * 256 + 256)
                    tp_wait(f)
                    for n in range(4):
                        mm = e.transpose(ps[:, T_BANK, n * P:n * P + P], kc[:, 4 * f + n, :], ident[:, :])
                    mm.then_inc(tp_ready, 1)

                def scores_s():
                    e.wait_ge(q_spread, it + 1)
                    e.wait_ge(consts, 12 + 1 + DEC_B)
                    e.wait_ge(tile_free[1], it * 4 + 2)
                    tp_wait(4)
                    e.wait_ge(logits_done, it * 9 + 1)
                    e.matmul(ps[:, S_BANK, 0:KS], rep8[0:8, :], bias8[0:8, :, :].rearrange("p f k -> p (f k)")[:, bass.ds(it * KS, KS)], start=True, stop=False,
                             skip_group_check=True)
                    for b in range(DEC_B):
                        g = b % NG
                        e.matmul(ps[GR * g:GR * g + GR, S_BANK, 0:PAST], q_bd[:, b, :], kcT[:, b, :],
                                 start=False, stop=False, skip_group_check=True)
                    e.matmul(ps[:, S_BANK, PAST:KS], q_all[:, :, :].rearrange("p g r -> p (g r)"), kT[:, SEQ:T], start=False,
                             stop=True, skip_group_check=True).then_inc(s_ready, 1)

                def scores(u):
                    h, qt = u // TT, u % TT
                    rows = slice(DH * h, DH * h + DH)
                    e.wait_ge(logits_done, it * 9 + (u + 2))
                    e.matmul(ps[:, S_BANK, 0:(qt + 1) * P], qT[rows, qt * P:(qt + 1) * P], kT[rows, 0:(qt + 1) * P],
                             start=True, stop=True).then_inc(s_ready, 1)

                def probs_T(u):
                    e.wait_ge(exp_done, it * 9 + (u + 2))
                    tp_wait(5 + u)
                    for kt in range(u % TT + 1):
                        mm = e.transpose(ps[:, T_BANK, kt * P:kt * P + P], lgt[:, u % 2, kt * P:kt * P + P], ident[:, :])
                    mm.then_inc(tp_ready, 1)

                def probs_T_s():
                    e.wait_ge(consts, 2)
                    e.wait_ge(probs_done, it + 1)
                    tp_wait(4)
                    for n in range(NPG):
                        e.transpose(ps[:, T_BANK, n * P:(n + 1) * P], lgt_s[:, n * P:n * P + P], ident[:, :])
                    e.transpose(ps[0:TS, T_BANK, NPG * P:(NPG + 1) * P], lgt_s[:, PAST:KS], ident[:, :]).then_inc(tp_ready, 1)

                def values(u):
                    h, qt = u // TT, u % TT
                    if u == 0:
                        e.wait_ge(o_free, it + 1)
                    else:
                        e.wait_ge(ov_done, it * 8 + u)
                    e.wait_ge(tp_free, it * 13 + (5 + u + 2))
                    for kt in range(qt + 1):
                        mm = e.matmul(ps[:, O_BANK, qt * P + DH * h:qt * P + DH * h + DH], prT[:, u % 2, kt * P:kt * P + P],
                                      tok[:, 1, kt, DH * h:DH * h + DH], start=kt == 0, stop=kt == qt)
                    mm.then_inc(v_ready, 1)

                def out_T():
                    e.wait_ge(ov_done, it * 8 + 8)
                    for qt in range(TT):
                        mm = e.transpose(ps[:, O_BANK, qt * P:(qt + 1) * P], o_tok[:, qt * P:(qt + 1) * P], ident[:, :])
                    mm.then_inc(pv_done, 1)

                def values_s():
                    e.wait_ge(vc_in, it * 256 + 256)
                    mi_wait(3)
                    for j in range(NJ):
                        e.matmul(ps[:, M_BANK, P * j:P * j + P], prT_s[0:TS, NPG, :], tok[0:TS, 1, TT, :], start=True,
                                 stop=False, skip_group_check=True)
                        for n in range(NPG):
                            for g in range(NG):
                                mm = e.matmul(ps[GR * g:GR * g + GR, M_BANK, P * j:P * j + P], prT_s[:, n, GR * g:GR * g + GR],
                                              vc[:, NPG * (NG * j + g) + n, :], start=False, stop=n == NPG - 1,
                                              skip_group_check=True)
                    mm.then_inc(mi_ready, 1)

                def out_s_T():
                    mi_wait(4)
                    for j in range(NJ):
                        mm = e.transpose(ps[:, M_BANK, P * j:P * j + P], o_s[:, P * j:P * j + P], ident[:, :])
                    mm.then_inc(mi_ready, 1)

                def tok_prompt(use, src, free, n_free):
                    e.wait_ge(tile_free[free], it * 4 + n_free)
                    mi_wait(use)
                    for tt in range(TT):
                        mm = e.transpose(ps[:, M_BANK, tt * P:tt * P + P], src[:, tt * P:tt * P + P], ident[:, :])
                    mm.then_inc(mi_ready, 1)

                def tok_sample():
                    mi_wait(1)
                    e.transpose(ps[0:TS, M_BANK, 0:P], kT[:, SEQ:T], ident[:, :])
                    e.transpose(ps[0:TS, M_BANK, P:2 * P], vT[:, SEQ:T], ident[:, :]).then_inc(mi_ready, 1)

                def rg(g, h):
                    if g == 0 and h == 0:
                        e.wait_ge(conv_step, it * 8 + 8)
                        e.wait_ge(bd_in, it * 64 + 64)
                    mi_wait(5 + 2 * g + h)
                    e.matmul(ps[:, M_BANK, 0:EH], bd[:, g, :], xc[:, EH * h:EH * h + EH], start=True,
                             stop=True).then_inc(mi_ready, 1)

                begin(0); part(0, 0, 4); cache_T(0); part(0, 4, 8)
                e.wait_ge(small_c, 4)
                begin(1); cache_T(1); part(1, 0, 4); cache_T(2); part(1, 4, 8)
                begin(2); cache_T(3); part(2, 0, 5); scores_s(); part(2, 5, 8)
                begin(3); scores(0); part(3, 0, 2); probs_T_s(); part(3, 2, 4)
                tok_prompt(0, vT, 0, 3); probs_T(0); scores(1); part(3, 4, 6); tok_sample(); part(3, 6, 8)
                begin(4); tok_prompt(2, kT, 1, 2); values(0); probs_T(1); scores(2); part(4, 0, 4)
                values_s(); values(1); probs_T(2); scores(3); part(4, 4, 8)
                begin(5); out_s_T(); values(2); probs_T(3); scores(4); part(5, 0, 2); rg(0, 0); part(5, 2, 4)
                values(3); probs_T(4); scores(5); rg(0, 1); part(5, 4, 6); rg(1, 0); part(5, 6, 8)
                begin(6); values(4); probs_T(5); scores(6); rg(1, 1); part(6, 0, 4)
                values(5); probs_T(6); scores(7); part(6, 4, 8)
                begin(7); values(6); probs_T(7); part(7, 0, 3); values(7); part(7, 3, 8); out_T()

            with e.Fori(0, GT_TAIL // 2) as n:
                for s in range(2):
                    split_ready(n * 2 + (C_TAIL + s))
                    e.wait_ge(tile_free[s], n + (4 * PAIRS + 1))
                    steps(s, 2 * s, xin_hi, xin_lo, [(k, k) for k in range(KD)], True, True).then_inc(tile_done, 1)
            e.wait_ge(st_saved, PAIRS)
            e.wait_ge(mi_free, 9 * PAIRS + 1)
            for f in range(PAIRS):
                mm = e.transpose(ps[0:36, M_BANK, f * P:f * P + P], stcol[:, f, :], ident[:, :])
            mm.then_inc(st_ready, 1)

            e.wait_ge(o_free, PAIRS + 1)
            e.wait_ge(rg_done, PAIRS + 1)
            e.wait_ge(logits_done, 9 * PAIRS + 1)
            e.wait_ge(tp_free, 13 * PAIRS + 1)
            e.wait_ge(st_copied, 1)
            for s in range(2):
                e.wait_ge(tile_free[s], 4 * PAIRS + GT_TAIL // 2 + 1)
            with e.Fori(0, KD // 2) as n:
                for s in range(2):
                    split_ready(n * 2 + (C_MIX + s))
                    e.wait_ge(mix_free, n * 2 + (s + 1))
                    steps(s, 4 * s, ocat_hi, ocat_lo, [(k, k) for k in range(PAIRS)], True, True)
                    steps(s, 4 * s + 2, ocat_hi, ocat_lo, [(k, k) for k in range(PAIRS, 2 * PAIRS)], True, True
                          ).then_inc(tile_done, 1)

            KS_D = [(k, k) for k in range(KD)]

            def out_tile(m, h, ready=None):
                split_ready(m + C_OUT)
                e.wait_ge(out_free, m + (KD * h + 1))
                steps(None, m % 2 - h, xin_hi, xin_lo, KS_D, True, True, ready=ready, hs=(h,), w=w_out_of[m]
                      ).then_inc(tile_done, 1)

            def sum_squares(acc, bank, hs):
                for h in hs:
                    mm = e.matmul(ps[:, bank + h, 0:HT], ones[:, :], acc[:, h * HT:h * HT + HT], start=True, stop=True)
                mm.then_inc(n_ready, 1)

            e.wait_ge(mix_free, KD + 1)
            for m in range(KD):
                out_tile(m, 0, ready=mix_lo if m == 0 else None)
                s = m % 2
                e.wait_ge(mix_free, KD + 2)
                e.wait_ge(xT_free, m + 1)
                e.wait_ge(xk_in[s], m // 2 * 32 + 32)
                for tt in range(TT):
                    e.transpose(ps[:, 4 + 2 * s, tt * P:tt * P + P], xk[s][:, tt, :], ident[:, :])
                e.transpose(ps[:, 5 + 2 * s, 0:TS], xk[s][0:TS, TT, :], ident[0:TS, 0:TS]).then_inc(xT_ready, 1)
            out_tile(0, 1)
            e.wait_ge(osq_used, KD + 2)
            sum_squares(oacc[0], 2, (0,))
            for m in range(1, KD):
                out_tile(m, 1)

            split_ready(C_FFN)
            e.wait_ge(out_free, 2 * KD + 1)
            steps(0, 0, xin_hi, xin_lo, KS_D[:2], True, False, ready=f_lo, hs=(0,))
            e.wait_ge(osq_used, 2 * KD + 2)
            sum_squares(oacc[0], 2, (1,))
            steps(0, 0, xin_hi, xin_lo, KS_D[2:], False, True, ready=f_lo, hs=(0,))
            split_ready(C_FFN + 1)
            e.wait_ge(n_std, 1)
            steps(1, 2, xin_hi, xin_lo, KS_D, True, True, hs=(0,))
            e.wait_ge(out_free, 2 * KD + 2)
            e.wait_ge(n_std, 2)
            for k in KS_D:
                for c in range(2):
                    mm = steps(c, 2 * c, xin_hi, xin_lo, [k], k[0] == 0, k[0] == KD - 1, ready=f_lo, base=KD + 1, hs=(1,))
                    if k[0] == KD - 1:
                        mm.then_inc(tile_done, 1)
            e.wait_ge(xT_free, KD + 2)
            e.wait_ge(f_acc, 2 * KD + 2)
            sum_squares(oacc[1], 6, (0, 1))
            for c in range(2):
                split_ready(C_FFN + 2 + c)
                if c == 1:
                    e.wait_ge(n_std, 3)
                steps(c, 4 + 2 * c, xin_hi, xin_lo, KS_D, True, True, w=w_keep[2 + c]).then_inc(tile_done, 1)
            with e.Fori(1, KF // 2) as n:
                for s in range(2):
                    e.wait_ge(gu_free, n * 2 + (s + 1))
                    for c in range(2):
                        split_ready(n * 4 + (C_FFN + 2 * s + c))
                        steps(c, 4 * s + 2 * c, xin_hi, xin_lo, KS_D, True, True).then_inc(tile_done, 1)

            def down(m, odd, between=None, last=False):
                for c in range(3):
                    split_ready(m * 3 + (C_DOWN + c))
                    if c == 0:
                        e.wait_ge(y_free, m + 1)
                    k0 = sum(DOWN_K[:c])
                    steps((odd + c) % 2, 2 * odd, hid_hi, hid_lo, [(k, k0 + k) for k in range(DOWN_K[c])],
                          c == 0, c == 2, ready=hid_l).then_inc(tile_done, 1)
                    if c == 0 and between is not None:
                        x1_T(between, 1 - odd)
                        y_T(between, 1 - odd)
                    if c == 1 and last:
                        x1_T(m, odd)

            def x1_T(m, s):
                e.wait_ge(x1s_done, m + 1)
                e.wait_ge(x1t_free, m + 2)
                for tt in range(TT):
                    e.transpose(ps[:, 4, tt * P:tt * P + P], x1s[s][:, tt * P:tt * P + P], ident[:, :])
                e.transpose(ps[0:TS, 5, 0:P], x1s[s][:, SEQ:T], ident[:, :]).then_inc(x1t_ready, 1)

            def y_T(m, s):
                e.wait_ge(y_free, m + 3)
                e.wait_ge(yt_free, m + 1)
                for tt in range(TT):
                    e.transpose(ps[:, 6, tt * P:tt * P + P], yg[s][:, tt * P:tt * P + P], ident[:, :])
                e.transpose(ps[0:TS, 7, 0:P], yg[s][:, SEQ:T], ident[:, :]).then_inc(yt_ready, 1)

            e.wait_ge(gu_free, KF + 1)
            down(0, 0)
            e.wait_ge(gu_free, KF + 2)
            with e.Fori(0, (KD - 2) // 2) as n:
                down(n * 2 + 1, 1, n * 2)
                down(n * 2 + 2, 0, n * 2 + 1)
            down(KD - 1, 1, KD - 2, last=True)
            y_T(KD - 1, 1)
            e.wait_ge(ysq_used, KD + 1)
            for tt in range(TT + 1):
                rows = P if tt < TT else TS
                mm = e.matmul(ps[0:rows, 0, tt:tt + 1], yacc[:, tt * P:tt * P + rows], ones[:, 0:1],
                              start=True, stop=True)
            mm.then_inc(yn_ready, 1)

        @block.scalar
        def _(e):
            def hi(i, i2, s, k=KD, to=None, free=None, count=1):
                e.wait_ge(w_in_slot[s], i2 * 32 + 32)
                e.wait_ge(tile_done, i + 1 if free is None else free)
                e.activation((to or w_hi[s])[:, 0:k, :], w_raw[s][:, 0:k, :], ACT.Copy).then_inc(hi_done, count)

            e.dma_start(g_row[:, :], AP(norm_mix_pre.tensor, 0, [[0, P], [1, D]])).then_inc(g_in, 16)
            e.dma_start(bktab[:, :], bucket_of).then_inc(rel_in, 16)
            e.wait_ge(sp_dve, 1)
            e.dma_start(rel33[0:NB, :], rel_bias).then_inc(rel_in, 16)
            e.wait_ge(consts_v, 3)
            e.activation(ycol[:, 0:1], eps_col[:, :], ACT.Sqrt)

            def x_rms(tt):
                rows = P if tt < TT else TS
                e.wait_ge(x_in[tt], 16)
                e.activation(x_sq[0:rows, :], x_tok[0:rows, tt, :], ACT.Square,
                             accum_out=ssum[0:rows, tt:tt + 1]).then_inc(sq_sum, 1)
                e.wait_ge(sq_sum, tt + 1)
                e.activation(rstd_x[0:rows, tt:tt + 1], ssum[0:rows, tt:tt + 1], ACT.Sqrt,
                             bias=eps_col[0:rows, :], scale=1.0 / D).then_inc(std_x, 1)

            def x_hi(tt):
                for hf in range(2 if tt < TT else 1):
                    f = 2 * tt + hf
                    e.wait_ge(xt_ready, f + 1)
                    dst, src = x_fill(xin_hi, tt, hf, f)
                    e.activation(dst, src, ACT.Copy).then_inc(xt_hi, 1)

            x_rms(0); x_rms(1); x_rms(2); x_hi(0)
            x_rms(3); x_hi(1); x_rms(4)
            hi(0, 0, 0)
            x_hi(2); x_hi(3); x_hi(4)
            e.wait_ge(sp_dve, SP_ABS)
            e.activation(sp[2][:, :], sp[1][:, :], ACT.Exp, scale=-1.0).then_inc(sp_act, 1)
            e.wait_ge(small_c, 4)
            e.dma_start(dist_bias, drow[:, :]).then_inc(dist_out, 16)

            with e.Fori(0, PAIRS) as it:
                def next_hi(j):
                    hi(it * TILES_IT + (j + 1), it * 4 + (j + 1) // 2, (j + 1) % 2)

                def done(j):
                    e.wait_ge(tile_done, it * TILES_IT + (j + 3))

                def gate(j):
                    done(j)
                    dst = gates[:, :, :].rearrange("p k t -> p (k t)")[:, bass.ds(it * (GT_IT * T) + (j - 5) * T, T)]
                    e.activation(halves(dst), two(j % 2), ACT.Tanh, scale=0.5).then_inc(tile_free[j % 2], 1)

                def cache_copy(f):
                    e.wait_ge(tp_ready, it * 13 + (f + 1))
                    e.activation(kcT[:, 2 * f:2 * f + 2, :], ps[:, T_BANK, :].rearrange("p (b k) -> p b k", b=2),
                                 ACT.Copy).then_inc(tp_free, 1)

                def exp_s():
                    e.wait_ge(logits_done, it * 9 + 2)
                    e.activation(lgt_s[:, :], lgt_s[:, :], ACT.Exp, bias=nmax[:, 0:1], scale=-1.0, accum_out=den[:, 0:1]).then_inc(exp_done, 1)

                def exp(u):
                    n = (u % TT + 1) * P
                    e.wait_ge(logits_done, it * 9 + (u + 3))
                    e.activation(lgt[:, u % 2, 0:n], lgt[:, u % 2, 0:n], ACT.Exp, bias=nmax[:, u + 1:u + 2], scale=-1.0,
                                 accum_out=den[:, u + 1:u + 2]).then_inc(exp_done, 1)

                def probs_copy(u):
                    n = (u % TT + 1) * P
                    e.wait_ge(tp_ready, it * 13 + (5 + u + 1))
                    e.activation(prT[:, u % 2, 0:n], ps[:, T_BANK, 0:n], ACT.Copy).then_inc(tp_free, 1)

                def rg_gate(use, dst):
                    g, h = divmod(use - 5, 2)
                    e.wait_ge(mi_ready, it * 9 + (use + 1))
                    e.activation(dst[:, EH * h:EH * h + EH], ps[:, M_BANK, 0:EH], ACT.Tanh, bias=prm_it[:, 5 + g:6 + g],
                                 scale=0.5).then_inc(mi_free, 1)

                next_hi(0); cache_copy(0)
                next_hi(1)
                done(0)
                e.activation(halves(qT[:, :]), two(0), ACT.Copy, scale=DH ** -0.5).then_inc(tile_free[0], 1)
                cache_copy(2)
                next_hi(2)
                exp_s()
                next_hi(3)
                done(2)
                e.activation(halves(vT[:, :]), two(0), ACT.Copy).then_inc(tile_free[0], 1)
                e.wait_ge(tp_ready, it * 13 + 5)
                e.activation(prT_s[:, 0:NPG, :], ps[:, T_BANK, 0:NPG * P].rearrange("p (n r) -> p n r", n=NPG), ACT.Copy)
                e.activation(prT_s[0:TS, NPG, :], ps[0:TS, T_BANK, NPG * P:(NPG + 1) * P], ACT.Copy).then_inc(tp_free, 1)
                exp(0); probs_copy(0); exp(1)
                next_hi(4)
                e.wait_ge(mi_ready, it * 9 + 3)
                e.activation(tok[:, 0, 0:TT, :], ps[:, M_BANK, :].rearrange("p (tt c) -> p tt c", c=P), ACT.Copy
                             ).then_inc(mi_free, 1)
                probs_copy(1); exp(2)
                probs_copy(2); exp(3)
                e.wait_ge(mi_ready, it * 9 + 4)
                e.activation(o_s[:, :], ps[:, M_BANK, 0:NJ * P], ACT.Copy).then_inc(mi_free, 1)
                next_hi(5)
                done(4)
                e.activation(halves(gb[:, :]), two(0), ACT.Copy).then_inc(tile_free[0], 1)
                e.wait_ge(mi_ready, it * 9 + 5)
                for h in range(2):
                    last = e.activation(sample_cols(ocat_hi, it, h), sample_rows(h), ACT.Copy)
                last.then_inc(so_hi, 1)
                probs_copy(3); exp(4)
                rg_gate(5, th)
                probs_copy(4); exp(5)
                rg_gate(6, th)
                rg_gate(7, ti)
                next_hi(6)
                rg_gate(8, ti)
                gate(5)
                e.activation(th[:, :], th[:, :], ACT.Tanh, bias=prm_it[:, 7:8], scale=prm_it[:, 7:8]).then_inc(th_done, 1)
                probs_copy(5); exp(6)
                e.wait_ge(gelu_step, it * 3 + 3)
                e.activation(gp[:, :], gp[:, :], ACT.Tanh).then_inc(tg_done, 1)
                probs_copy(6); exp(7)
                next_hi(7)
                gate(6)
                probs_copy(7)
                e.wait_ge(th_done, it + 1)
                e.activation(sq[:, :], th[:, :], ACT.Sqrt, bias=tiny_col[:, :]).then_inc(sq_done, 1)
                e.wait_ge(pv_done, it + 1)
                e.activation(ocat_hi[:, bass.ds(it, 1), 0:SEQ], ps[:, O_BANK, :], ACT.Copy).then_inc(o_hi, 1)
                gate(7)
                e.wait_ge(rg_step, it * 12 + 12)
                e.activation(ocat_hi[:, bass.ds(it + PAIRS, 1), :], dd[:, 0:T], ACT.Copy).then_inc(orn_hi, 1)

            with e.Fori(0, GT_TAIL // 2) as n:
                for s in range(2):
                    i = n * 2 + (C_TAIL + s)
                    hi(i + 1, n + (C_TAIL + s + 1) // 2, 1 - s)
                    e.wait_ge(tile_done, i + 3)
                    dst = gates[:, :, :].rearrange("p k t -> p (k t)")[:, bass.ds(n * (2 * T) + (PAIRS * GT_IT + s) * T, T)]
                    e.activation(halves(dst), two(s), ACT.Tanh, scale=0.5).then_inc(tile_free[s], 1)

            with e.Fori(0, KD // 2) as n:
                for s in range(2):
                    hi(n * 2 + (C_MIX + s + 1), n + (C_MIX + s + 1) // 2, 1 - s)
                    e.wait_ge(mix_sum, n * 2 + (s + 1))
                    e.activation(tile_of(xin_hi, n * 2, s), halves(ma[s][:, :]), ACT.Copy, scale=0.5).then_inc(mix_hi, 1)

            def out_evacuate(m, s, h):
                i = m + (C_OUT + KD * h)
                e.wait_ge(tile_done, i + 3)
                e.activation(half_of(og, m, h), ps[:, s, 0:HT], ACT.Identity, scale=prm[:, bass.ds(m + 32, 1)])
                e.wait_ge(osq_used, m + (KD * h + 1))
                e.activation(osq[s][:, :], ps[:, s, 0:HT], ACT.Square).then_inc(out_free, 1)

            def out_hi(m):
                if m == 2:
                    e.wait_ge(st_out_s, 64)
                if m == 5:
                    e.wait_ge(mix_free, KD + 2)
                hi(C_OUT + m, (C_OUT + m) // 2, m % 2, to=w_out_of[m][0], free=C_OUT + 2, count=1 if m < KD - 1 else 1 + KD)
                if m == KD - 1:
                    for s in range(2):
                        e.sem_inc(w_in_slot[s], 16 * KD)

            def gu_hi(c):
                hi(C_FFN + c, (C_FFN + c) // 2, c % 2, to=w_out_of[c][0], free=C_OUT + KD + c + 3)

            def rms(n, out, src):
                e.wait_ge(n_ready, n)
                if n == 3:
                    e.wait_ge(n_rstd, 2)
                e.activation(out, src, ACT.Sqrt, bias=eps_col[:, :], scale=1.0 / D).then_inc(n_std, 1)

            def x1_high(k, j, slot, h):
                e.wait_ge(x1_done, j + 1)
                e.wait_ge(f_acc, j + 1)
                e.activation(half_of(xin_hi, k, h), half_of(x1, k, h), ACT.Identity, scale=prm[:, bass.ds(k + 40, 1)]
                             ).then_inc(f_hi, 1)
                e.activation(xsq[slot][:, :], half_of(x1, k, h), ACT.Square).then_inc(f_sq, 1)

            hi(C_OUT + 1, (C_OUT + 1) // 2, 1)
            for m in range(KD):
                if m + 2 < KD:
                    out_hi(m + 2)
                out_evacuate(m, m % 2, 0)
            out_evacuate(0, 0, 1)
            rms(1, std[:, 0:HT], ps[:, 2, 0:HT])
            for m in range(1, KD):
                if m <= 4:
                    gu_hi(m - 1)
                out_evacuate(m, m % 2, 1)
                for k in RESIDUALS[m - 1]:
                    x1_high(k, k, k % 2, 0)
            rms(2, std[:, HT:T], ps[:, 3, 0:HT])
            for k in RESIDUALS[KD - 1]:
                x1_high(k, k, k % 2, 0)
            for k in range(KD):
                x1_high(k, KD + k, k % 2, 1)

            def ffn_hi(m, c):
                hi(m * 2 + (C_FFN + 2 + c), m + (C_FFN + 2) // 2, c)

            def ffn_tanh(m):
                e.wait_ge(gu_scaled, m + 1)
                e.activation(ft[:, :], fg[:, :], ACT.Tanh, scale=0.5).then_inc(fsil, 1)

            def ffn_high(m):
                e.wait_ge(fprod, m * 2 + 2)
                e.activation(tile_of(hid_hi, m), halves(fg[:, :]), ACT.Copy, scale=0.5).then_inc(hid_h, 1)

            rms(3, halves(std[:, :]), two(3))
            ffn_tanh(0)
            ffn_high(0)
            with e.Fori(1, KF) as m:
                ffn_hi(m, 0)
                ffn_tanh(m)
                ffn_hi(m, 1)
                ffn_high(m)

            def down_hi(n, odd, c):
                q = 3 * odd + c + 2
                hi(n * 6 + (C_DOWN + q), n * 3 + (C_DOWN + q) // 2, q % 2, DOWN_K[(c + 2) % 3])

            def y_evacuate(m, s):
                e.wait_ge(tile_done, m * 3 + (C_DOWN + 5))
                e.activation(halves(yg[s][:, :]), two(s), ACT.Identity, scale=prm[:, bass.ds(m + 48, 1)])
                e.wait_ge(ysq_used, m + 1)
                e.activation(halves(ysq[:, :]), two(s), ACT.Square).then_inc(y_free, 1)

            def y_last(m, s):
                e.activation(ycol[:, 15:16], eps_col[:, :], ACT.Sqrt)
                e.wait_ge(tile_done, m * 3 + (C_DOWN + 5))
                e.wait_ge(ysq_used, m + 1)
                e.activation(halves(ysq[:, :]), two(s), ACT.Square).then_inc(y_sq_last, 1)
                e.activation(halves(yg[s][:, :]), two(s), ACT.Identity, scale=prm[:, m + 48:m + 49]).then_inc(y_free, 1)

            def y_copy(m):
                e.wait_ge(yt_ready, m + 1)
                e.activation(ytok[:, 0:TT, bass.ds(m * P, P)], ps[:, 6, :].rearrange("p (tt c) -> p tt c", c=P), ACT.Copy)
                e.activation(ytok[0:TS, TT, bass.ds(m * P, P)], ps[0:TS, 7, 0:P], ACT.Copy).then_inc(yt_free, 1)

            def y_tile(n, odd, copy=True):
                m = n * 2 + odd
                down_hi(n, odd, 0)
                if copy:
                    y_copy(m - 1)
                down_hi(n, odd, 1)
                down_hi(n, odd, 2)
                y_evacuate(m, odd)

            y_tile(0, 0, copy=False)
            with e.Fori(0, (KD - 2) // 2) as n:
                y_tile(n, 1)
                y_tile(n + 1, 0)
            hi(C_DOWN + 3 * KD - 1, (C_DOWN + 3 * KD - 1) // 2, (C_DOWN + 3 * KD - 1) % 2, DOWN_K[2])
            y_copy(KD - 2)
            y_last(KD - 1, 1)
            y_copy(KD - 1)
            e.wait_ge(yn_ready, 1)
            e.activation(ycol[:, 0:TT], ps[:, 0, 0:TT], ACT.Sqrt, bias=eps_col[:, :], scale=1.0 / D)
            e.activation(ycol[0:TS, TT:TT + 1], ps[0:TS, 0, TT:TT + 1], ACT.Sqrt, bias=eps_col[0:TS, :], scale=1.0 / D
                         ).then_inc(ycol_step, 1)

        @block.vector
        def _(e):
            for sem_, n in ((lo_done, 2), (tile_done, 2), (tile_free[0], 1), (tile_free[1], 1), (logits_done, 1),
                            (tp_free, 1), (mi_free, 1), (o_free, 1), (rg_done, 1), (kv_out, 64), (mix_free, 2),
                            (out_free, 2), (osq_used, 2), (xT_free, 2), (gu_free, 2), (y_free, 2), (ysq_used, 1),
                            (x1t_free, 2), (yt_free, 1), (f_acc, 2)):
                e.sem_inc(sem_, n)

            def lo(i, s, k=KD, w=None, count=1):
                wh, wl = w or (w_hi[s], w_lo[s])
                e.wait_ge(hi_done, i + 1)
                e.tensor_tensor(wl[:, 0:k, :], w_raw[s][:, 0:k, :], wh[:, 0:k, :].bitcast(F32), ALU.subtract
                                ).then_inc(lo_done, count)

            e.memset(rel33[:, :], NEG).then_inc(sp_dve, 1)
            e.memset(ones[:, :], 1.0).then_inc(consts_v, 1)
            e.memset(eps_col[:, :], EPS).then_inc(consts_v, 1)
            e.memset(tiny_col[:, :], 1.0e-30).then_inc(consts_v, 1)
            e.wait_ge(g_in, 16)

            def x_norm(tt):
                rows = slice(0, P if tt < TT else TS)
                e.wait_ge(std_x, tt + 1)
                e.reciprocal(rstd_x[rows, tt:tt + 1], rstd_x[rows, tt:tt + 1]).then_inc(rx_done, 1)
                e.wait_ge(rx_done, tt + 1)
                e.scalar_tensor_tensor(x_tok[rows, tt, :], x_tok[rows, tt, :], rstd_x[rows, tt:tt + 1], g_row[rows, :],
                                       ALU.mult, ALU.mult).then_inc(xs_done, 1)

            def x_lo(tt):
                for hf in range(2 if tt < TT else 1):
                    f = 2 * tt + hf
                    e.wait_ge(xt_hi, f + 1)
                    dst, src = x_fill(xin_lo, tt, hf, f)
                    e.tensor_tensor(dst, src, x_fill(xin_hi, tt, hf, f)[0].bitcast(F32), ALU.subtract).then_inc(xt_lo, 1)

            x_norm(0)
            x_norm(1)
            x_lo(0)
            x_norm(2)
            x_lo(1)
            x_norm(3)
            x_lo(2)
            x_norm(4)
            lo(0, 0)
            x_lo(3)
            x_lo(4)
            e.wait_ge(small_T, 3)
            e.tensor_copy(drow[:, 0:512], ps[0:HEADS, 3, 0:512]).then_inc(small_c, 1)
            e.tensor_copy(drow[:, 512:RELW], ps[0:HEADS, 2, 192:192 + RELW - 512]).then_inc(small_c, 1)
            e.tensor_copy(prm[:, :], ps[:, 2, 0:56]).then_inc(small_c, 1)
            e.tensor_copy(stT[:, :, :], ps[:, 2, 64:64 + P].rearrange("p (f r) -> p f r", f=PAIRS)).then_inc(small_c, 1)
            e.wait_ge(small_c, 4)
            e.tensor_scalar(prm[:, 20:28], prm[:, 20:28], 0.5, None, ALU.mult).then_inc(small_c, 1)
            nl, la, y, mx, z, z2 = (b[:, :] for b in sp)
            e.tensor_scalar(nl, prm[:, 28:32], -1.0, None, ALU.mult).then_inc(sp_dve, 1)
            e.wait_ge(sp_dve, 2)
            e.tensor_tensor(la, nl, prm[:, 28:32], ALU.max).then_inc(sp_dve, 1)
            e.tensor_scalar(mx, nl, 0.0, None, ALU.max).then_inc(sp_dve, 1)
            e.wait_ge(sp_act, 1)
            e.tensor_scalar(z, y, 2.0, None, ALU.add).then_inc(sp_dve, 1)
            e.wait_ge(sp_dve, 5)
            e.reciprocal(z, z).then_inc(sp_dve, 1)
            e.wait_ge(sp_dve, 6)
            e.tensor_tensor(z, y, z, ALU.mult).then_inc(sp_dve, 1)
            e.wait_ge(sp_dve, 7)
            e.tensor_tensor(z2, z, z, ALU.mult).then_inc(sp_dve, 1)
            e.wait_ge(sp_dve, 8)
            e.tensor_scalar(nl, z2, 1.0 / (2 * SERIES + 1), None, ALU.mult).then_inc(sp_dve, 1)
            for k in range(SERIES - 1, -1, -1):
                e.wait_ge(sp_dve, 8 + SERIES - k)
                e.scalar_tensor_tensor(nl, nl, 1.0 / (2 * k + 1), z2 if k else z, ALU.add, ALU.mult).then_inc(sp_dve, 1)
            e.wait_ge(sp_dve, 9 + SERIES)
            e.scalar_tensor_tensor(nl, nl, 2.0, mx, ALU.mult, ALU.add).then_inc(sp_dve, 1)
            e.wait_ge(sp_dve, 10 + SERIES)
            e.tensor_scalar(prm[:, 28:32], nl, 2.0, None, ALU.mult).then_inc(small_c, 1)

            with e.Fori(0, PAIRS) as it:
                def next_lo(j):
                    lo(it * TILES_IT + (j + 1), (j + 1) % 2)

                def cache_copy(f):
                    e.wait_ge(tp_ready, it * 13 + (f + 1))
                    e.tensor_copy(kcT[:, 2 * f:2 * f + 2, :], ps[:, T_BANK, :].rearrange("p (b k) -> p b k", b=2)
                                  ).then_inc(tp_free, 1)

                def logits(u):
                    h, n = u // TT, (u % TT + 1) * P
                    count = e.to_reg(it * 9 + (u + 2))
                    e.wait_ge(bias_in, 16)
                    e.wait_ge(s_ready, count)
                    e.tensor_tensor_reduce(lgt[:, u % 2, 0:n], ps[:, S_BANK, 0:n], biasT[:, h, 0:n][:, ::-1], -1.0, BIG,
                                           ALU.add, ALU.min, nmax[:, u + 1:u + 2]).then_inc(logits_done, 1)

                def scale(u):
                    h, qt = u // TT, u % TT
                    cols = slice(qt * P + DH * h, qt * P + DH * h + DH)
                    e.wait_ge(exp_done, it * 9 + (u + 2))
                    e.reciprocal(rden[:, u + 1:u + 2], den[:, u + 1:u + 2]).then_inc(rden_done, 1)
                    e.wait_ge(rden_done, it * 9 + (u + 2))
                    e.wait_ge(v_ready, it * 8 + (u + 1))
                    e.tensor_scalar(o_tok[:, cols], ps[:, O_BANK, cols], rden[:, u + 1:u + 2], None, ALU.mult
                                    ).then_inc(ov_done, 1)

                def rg(step, ins):
                    ins.then_inc(rg_step, 1)

                def rg_wait(step):
                    e.wait_ge(rg_step, it * 12 + step)

                next_lo(0); cache_copy(1)
                next_lo(1); cache_copy(3)
                next_lo(2)
                e.wait_ge(tile_done, it * TILES_IT + 4)
                e.tensor_copy(halves(kT[:, :]), two(1)).then_inc(tile_free[1], 1)
                count = e.to_reg(it * 9 + 1)
                e.wait_ge(consts, 7)
                e.wait_ge(s_ready, count)
                e.tensor_tensor_reduce(lgt_s[:, :], ps[:, S_BANK, 0:KS], mask_s[:, :], -1.0, BIG,
                                       ALU.add, ALU.min, nmax[:, 0:1]).then_inc(logits_done, 1)
                e.wait_ge(exp_done, it * 9 + 1)
                e.reciprocal(rden[:, 0:1], den[:, 0:1]).then_inc(rden_done, 1)
                e.wait_ge(rden_done, it * 9 + 1)
                e.tensor_scalar(lgt_s[:, :], lgt_s[:, :], rden[:, 0:1], None, ALU.mult
                                ).then_inc(probs_done, 1)
                next_lo(3)
                e.wait_ge(bias_in, it * 16 + 16)
                logits(0)
                e.wait_ge(mi_ready, it * 9 + 1)
                e.wait_ge(kv_out, it * 64 + 64)
                e.tensor_copy(tok[:, 1, 0:TT, :], ps[:, M_BANK, :].rearrange("p (tt c) -> p tt c", c=P)).then_inc(mi_free, 1)
                logits(1)
                e.wait_ge(mi_ready, it * 9 + 2)
                e.tensor_copy(tok[0:TS, :, TT, :], ps[0:TS, M_BANK, 0:2 * P].rearrange("p (g c) -> p g c", g=2)
                              ).then_inc(mi_free, 1)
                next_lo(4)
                e.wait_ge(tile_done, it * TILES_IT + 6)
                e.wait_ge(it_ready, it + 1)
                e.tensor_copy(xp[:, CW - 1:CW - 1 + HT], ps[:, 2, 0:HT])
                e.tensor_copy(xp[:, CW - 1 + HT:CW - 1 + SEQ], ps[:, 3, 0:SEQ - HT])
                e.tensor_copy(xps[:, :, CW - 1:CW - 1 + DEC_T], bt(ps[:, 3, SEQ - HT:HT])).then_inc(tile_free[1], 1)
                scale(0); logits(2)
                e.wait_ge(tile_free[1], it * 4 + 3)
                for j in range(CW):
                    for g, (dst, src) in enumerate((
                            (xc[:, 0:SEQ], xp[:, j:j + SEQ]),
                            (xc[:, SEQ:EXT].rearrange("p (b k) -> p b k", b=DEC_B)[:, :, 1:1 + DEC_T],
                             xps[:, :, j:j + DEC_T]))):
                        if j == 0:
                            e.tensor_scalar(dst, src, prm_it[:, 0:1], prm_it[:, 4:5], ALU.mult, ALU.add
                                            ).then_inc(conv_step, 1)
                        else:
                            e.wait_ge(conv_step, it * 8 + (2 * j + g - 1))
                            e.scalar_tensor_tensor(dst, src, prm_it[:, j:j + 1], dst, ALU.mult, ALU.add
                                                   ).then_inc(conv_step, 1)
                scale(1); logits(3)
                next_lo(5)
                e.wait_ge(so_hi, it + 1)
                for h in range(2):
                    last = e.tensor_tensor(sample_cols(ocat_lo, it, h), sample_rows(h), sample_cols(ocat_hi, it, h).bitcast(F32),
                                           ALU.subtract)
                last.then_inc(mi_free, 1)
                scale(2); logits(4); scale(3); logits(5)
                next_lo(6)
                scale(4); logits(6)
                e.wait_ge(th_done, it + 1)
                rg(1, e.tensor_scalar(dd[:, :], th[:, :], 1.0, None, ALU.add))
                rg_wait(1)
                rg(2, e.reciprocal(dd[:, :], dd[:, :]))
                scale(5); logits(7)
                rg_wait(2)
                rg(3, e.tensor_scalar(aa[:, :], dd[:, :], 2.0, -1.0, ALU.mult, ALU.add))
                rg_wait(3)
                resets = [b[:, SEQ:EXT].rearrange("p (b k) -> p b k", b=DEC_B)[:, :, 0:1] for b in (aa, ti)]
                rg(4, e.memset(resets[0], 0.0))
                next_lo(7)
                scale(6)
                rg(5, e.scalar_tensor_tensor(ti[:, :], ti[:, :], 1.0, xc[:, :], ALU.add, ALU.mult))
                e.wait_ge(sq_done, it + 1)
                rg(6, e.tensor_tensor(sq[:, :], sq[:, :], dd[:, :], ALU.mult))
                rg_wait(6)
                rg(7, e.tensor_tensor(ti[:, :], ti[:, :], sq[:, :], ALU.mult))
                rg_wait(7)
                scale(7)
                rg(8, e.tensor_copy(resets[1], stT[:, bass.ds(it, 1), 24:32].rearrange("p o b -> p b o")))
                rg_wait(8)
                rg(9, e.tensor_tensor_scan(sq[:, :], aa[:, :], ti[:, :], 0.0, ALU.mult, ALU.add))
                e.wait_ge(tg_done, it + 1)
                rg(10, e.scalar_tensor_tensor(gp[:, :], gp[:, :], 1.0, gb[:, :], ALU.add, ALU.mult))
                rg_wait(10)
                rg(11, e.scalar_tensor_tensor(dd[:, 0:SEQ], sq[:, 0:SEQ], 0.5, gp[:, 0:SEQ], ALU.mult, ALU.mult))
                rg(12, e.scalar_tensor_tensor(bt(dd[:, SEQ:T]),
                                              sq[:, SEQ:EXT].rearrange("p (b k) -> p b k", b=DEC_B)[:, :, 1:1 + DEC_T], 0.5,
                                              bt(gp[:, SEQ:T]), ALU.mult, ALU.mult))
                e.wait_ge(o_hi, it + 1)
                e.tensor_tensor(ocat_lo[:, bass.ds(it, 1), 0:SEQ], ps[:, O_BANK, :],
                                ocat_hi[:, bass.ds(it, 1), 0:SEQ].bitcast(F32), ALU.subtract).then_inc(o_free, 1)
                e.wait_ge(orn_hi, it + 1)
                e.tensor_tensor(ocat_lo[:, bass.ds(it + PAIRS, 1), :], dd[:, 0:T],
                                ocat_hi[:, bass.ds(it + PAIRS, 1), :].bitcast(F32), ALU.subtract).then_inc(rg_done, 1)

            with e.Fori(0, GT_TAIL // 2) as n:
                for s in range(2):
                    lo(n * 2 + (C_TAIL + s + 1), 1 - s)
            e.wait_ge(st_ready, 1)
            e.tensor_copy(st_out[:, :], ps[0:36, M_BANK, :]).then_inc(st_copied, 1)

            e.wait_ge(kv_out, 64 * (PAIRS + 1))
            with e.Fori(0, KD // 2) as n:
                for s in range(2):
                    i = n * 2 + (C_MIX + s)
                    lo(i + 1, 1 - s)
                    e.wait_ge(tile_done, i + 3)
                    for g, dst in ((0, ma[s]), (1, mr[s])):
                        last = e.scalar_tensor_tensor(halves(dst[:, :]), tile_of(gates, n * 2, s + KD * g), 1.0,
                                                      two(2 * s + g), ALU.add, ALU.mult)
                    last.then_inc(mix_free, 1)
                    e.wait_ge(mix_free, n * 2 + (s + 3))
                    e.tensor_tensor(ma[s][:, :], ma[s][:, :], mr[s][:, :], ALU.add).then_inc(mix_sum, 1)
                    e.wait_ge(mix_hi, n * 2 + (s + 1))
                    e.scalar_tensor_tensor(tile_of(xin_lo, n * 2, s), halves(ma[s][:, :]), 0.5,
                                           tile_of(xin_hi, n * 2, s).bitcast(F32), ALU.mult, ALU.subtract
                                           ).then_inc(mix_lo, 1)

            e.wait_ge(tile_done, C_OUT + 2)
            lo(C_OUT + 1, 1)
            e.memset(oacc[0][:, :], 0.0).then_inc(acc_zero, 1)
            e.wait_ge(acc_zero, 1)
            e.wait_ge(st_out_s, 64)

            def out_square(m, s, h):
                e.wait_ge(out_free, m + (KD * h + 3))
                e.wait_ge(osq_used, m + (KD * h + 2))
                acc = oacc[0][:, h * HT:h * HT + HT]
                e.tensor_tensor(acc, acc, osq[s][:, :], ALU.add).then_inc(osq_used, 1)

            def residual(k, j, h):
                o, x = half_of(og, k, h), half_of(x1, k, h)
                e.tensor_tensor(o, o, rb[0][:, h * HT:h * HT + HT], ALU.mult).then_inc(t_done, 1)
                e.wait_ge(t_done, j + 1)
                e.tensor_tensor(x, x, o, ALU.add).then_inc(x1_done, 1)

            def x1_low(k, j, h):
                e.wait_ge(f_hi, j + 1)
                e.scalar_tensor_tensor(half_of(xin_lo, k, h), half_of(x1, k, h), prm[:, bass.ds(k + 40, 1)],
                                       half_of(xin_hi, k, h).bitcast(F32), ALU.mult, ALU.subtract).then_inc(f_lo, 1)

            def inverse(n, out, src):
                e.wait_ge(n_std, n)
                e.reciprocal(out, src).then_inc(n_rstd, 1)
                e.wait_ge(n_rstd, n)

            for m in range(KD):
                if m + 2 < KD:
                    lo(C_OUT + m + 2, m % 2, w=w_out_of[m + 2], count=1 if m + 3 < KD else 1 + KD)
                e.wait_ge(xT_ready, m + 1)
                e.tensor_copy(x1[:, m, 0:SEQ], ps[:, 4 + 2 * (m % 2), :])
                e.tensor_copy(x1[:, m, SEQ:T], ps[:, 5 + 2 * (m % 2), 0:TS]).then_inc(xT_free, 1)
                out_square(m, m % 2, 0)
            out_square(0, 0, 1)
            inverse(1, rb[0][:, 0:HT], std[:, 0:HT])
            for m in range(1, KD):
                if m <= 4:
                    lo(C_FFN + m - 1, (m - 1) % 2, w=w_out_of[m - 1])
                for k in RESIDUALS[m]:
                    residual(k, k, 0)
                out_square(m, m % 2, 1)
                for k in RESIDUALS[m - 1]:
                    x1_low(k, k, 0)
            inverse(2, rb[0][:, HT:T], std[:, HT:T])
            for k in RESIDUALS[KD - 1]:
                x1_low(k, k, 0)
            for k in range(KD + 1):
                if k < KD:
                    residual(k, KD + k, 1)
                if k >= 1:
                    x1_low(k - 1, KD + k - 1, 1)

            rms_b = halves(rb[1][:, :])

            def ffn_lo(n, s, c):
                lo(n * 4 + (C_FFN + 2 * s + 2 + c), c)

            def ffn_gate(n, s):
                e.wait_ge(tile_done, n * 4 + (C_FFN + 2 * s + 3))
                e.wait_ge(lo_done, n * 4 + (C_FFN + 2 * s + 5))
                e.tensor_tensor(halves(fg[:, :]), two(2 * s), rms_b, ALU.mult).then_inc(gu_scaled, 1)

            def ffn_silu(n, s):
                e.wait_ge(fsil, n * 2 + (s + 1))
                e.scalar_tensor_tensor(fg[:, :], ft[:, :], 1.0, fg[:, :], ALU.add, ALU.mult).then_inc(fprod, 1)

            def ffn_up(n, s):
                e.wait_ge(tile_done, n * 4 + (C_FFN + 2 * s + 4))
                e.tensor_tensor(halves(fu[:, :]), two(2 * s + 1), rms_b, ALU.mult).then_inc(gu_free, 1)
                e.wait_ge(gu_free, n * 2 + (s + 3))
                e.wait_ge(fprod, n * 4 + (2 * s + 1))
                e.tensor_tensor(fg[:, :], fg[:, :], fu[:, :], ALU.mult).then_inc(fprod, 1)
                e.wait_ge(hid_h, n * 2 + (s + 1))
                e.scalar_tensor_tensor(tile_of(hid_lo, n * 2, s), halves(fg[:, :]), 0.5,
                                       tile_of(hid_hi, n * 2, s).bitcast(F32), ALU.mult, ALU.subtract
                                       ).then_inc(hid_l, 1)

            def ffn_tile(n, s):
                ffn_lo(n, s, 0)
                ffn_gate(n, s)
                ffn_silu(n, s)
                ffn_lo(n, s, 1)
                ffn_up(n, s)

            inverse(3, rb[1][:, :], std[:, :])
            ffn_gate(0, 0)
            ffn_silu(0, 0)
            ffn_up(0, 0)
            ffn_tile(0, 1)
            with e.Fori(1, KF // 2) as n:
                ffn_tile(n, 0)
                ffn_tile(n, 1)

            e.wait_ge(tile_done, C_DOWN + 2)
            e.memset(yacc[:, :], 0.0).then_inc(acc_zero, 1)
            e.wait_ge(acc_zero, 2)

            def down_lo(n, odd, c):
                q = 3 * odd + c + 2
                lo(n * 6 + (C_DOWN + q), q % 2, DOWN_K[(c + 2) % 3])

            def x1_copy(m):
                e.wait_ge(x1t_ready, m + 1)
                e.tensor_copy(x1tok[:, 0:TT, bass.ds(m * P, P)], ps[:, 4, :].rearrange("p (tt c) -> p tt c", c=P))
                e.tensor_copy(x1tok[0:TS, TT, bass.ds(m * P, P)], ps[0:TS, 5, 0:P]).then_inc(x1t_free, 1)

            def y_square(m, sem_=y_free, count=None):
                e.wait_ge(sem_, m + 3 if count is None else count)
                e.wait_ge(ysq_used, m + 1)
                e.tensor_tensor(yacc[:, :], yacc[:, :], ysq[:, :], ALU.add).then_inc(ysq_used, 1)

            def y_tile(n, odd, copy=True):
                m = n * 2 + odd
                down_lo(n, odd, 0)
                if copy:
                    x1_copy(m - 1)
                down_lo(n, odd, 1)
                down_lo(n, odd, 2)
                y_square(m)

            y_tile(0, 0, copy=False)
            with e.Fori(0, (KD - 2) // 2) as n:
                y_tile(n, 1)
                y_tile(n + 1, 0)
            lo(C_DOWN + 3 * KD - 1, (C_DOWN + 3 * KD - 1) % 2, DOWN_K[2])
            x1_copy(KD - 2)
            x1_copy(KD - 1)
            y_square(KD - 1, y_sq_last, 1)
            e.wait_ge(ycol_step, 1)
            e.reciprocal(ycol[:, 8:8 + TT], ycol[:, 0:TT])
            e.reciprocal(ycol[0:TS, 8 + TT:9 + TT], ycol[0:TS, TT:TT + 1]).then_inc(ycol_step, 1)
            e.wait_ge(ycol_step, 2)
            e.wait_ge(x1t_free, KD + 2)
            e.wait_ge(yt_free, KD + 1)
            for tt in range(TT + 1):
                rows = slice(0, P if tt < TT else TS)
                e.scalar_tensor_tensor(ytok[rows, tt, :], ytok[rows, tt, :], ycol[rows, 8 + tt:9 + tt], x1tok[rows, tt, :],
                                       ALU.mult, ALU.add).then_inc(z_done, 1)


_INS = ["x_prompt", "x_sample", "cache_k", "cache_v", "page_table", "state_conv", "state_h",
        "norm_mix_pre", "norm_mix_post", "w_in", "rel_bias", "conv_w", "conv_b", "rg_w_r", "rg_b_r",
        "rg_w_i", "rg_b_i", "rg_lambda", "w_proj_attn", "w_proj_rnn", "w_out", "norm_ffn_pre",
        "norm_ffn_post", "w_gate_up", "w_down"]
_OUTS = [(1, SEQ, D), (DEC_B, DEC_T, D), (1, 1, SEQ, HEADS, DH), (1, 1, SEQ, HEADS, DH),
         (1, DEC_B, DEC_T, HEADS, DH), (1, DEC_B, DEC_T, HEADS, DH), (1, 1, CW - 1, DR), (1, 1, DR),
         (1, DEC_B, CW - 1, DR), (1, DEC_B, DR)]


def kernel(**inputs):
    import numpy as _np
    import concourse.bacc as _bacc
    from concourse import mybir as _mybir
    from concourse.bass_utils import run_bass_kernel_spmd as _run

    nc = _bacc.Bacc("TRN2", target_bir_lowering=False, num_devices=1)
    arrays, args = {}, []
    for name in _INS + ["bucket_of"]:
        a = bucket_table() if name == "bucket_of" else _np.ascontiguousarray(inputs[name])
        arrays[f"in_{name}_dram"] = a
        args.append(nc.dram_tensor(f"in_{name}_dram", a.shape, _mybir.dt.from_np(a.dtype), kind="ExternalInput").ap())
    for i, shape in enumerate(_OUTS):
        args.append(nc.dram_tensor(f"out_{i}_dram", shape, _mybir.dt.float32, kind="ExternalOutput").ap())
    program(nc, *args)
    r = _run(nc, [arrays], core_ids=[0])
    return tuple(r.results[0][f"out_{i}_dram"] for i in range(len(_OUTS)))
```
